# Optimizing a Trainium2 kernel written in Bass

```python
import math
import jax, jax.numpy as jnp
from jax import lax
import numpy as np

D_MODEL = 1024
BATCH = 1
SEQ = 256
DEPTH = 2

N_EVEN = (DEPTH + 1) // 2
N_ODD = DEPTH // 2

D_A = D_MODEL // 2
D_B = D_MODEL // 2
CONV_A = 31
CONV_B = 3
D_IN_EVEN = 2 * D_A + 3 * D_B

D_RNN = D_MODEL
RNN_BLOCK = 256
RNN_HEADS = D_RNN // RNN_BLOCK
CONV_C = 4
LRU_C = 8.0

N_EXPERTS = 16
N_EXPERT_GROUPS = 4
EXPERTS_PER_GROUP = N_EXPERTS // N_EXPERT_GROUPS
TOP_K = 2
D_EXPERT = D_MODEL
MOE_BLOCK = 128

LN_EPS = 1e-5
ALPHA = (2.0 * DEPTH) ** 0.25
BETA = (8.0 * DEPTH) ** -0.25


def layer_norm(x, g, b):
    xf = x.astype(jnp.float32)
    mu = jnp.mean(xf, axis=-1, keepdims=True)
    var = jnp.mean(jnp.square(xf - mu), axis=-1, keepdims=True)
    y = (xf - mu) * lax.rsqrt(var + LN_EPS)
    return (y * g.astype(jnp.float32) + b.astype(jnp.float32)).astype(x.dtype)

def causal_depthwise_conv(x, w):
    k, c = w.shape
    return lax.conv_general_dilated(
        x, w[:, None, :].astype(x.dtype), window_strides=(1,), padding=[(k - 1, 0)],
        dimension_numbers=("NWC", "WIO", "NWC"), feature_group_count=c)

def conv_mixer(x, w_in, a_dw, a_dw_b, a_ln_g, a_ln_b, b_dw, w_out):
    u = jnp.einsum("bsd,de->bse", x, w_in)
    a_val, a_gate, b_b, b_c, b_x = jnp.split(
        u, [D_A, 2 * D_A, 2 * D_A + D_B, 2 * D_A + 2 * D_B], axis=-1)
    a = a_val * jax.nn.sigmoid(a_gate)
    a = causal_depthwise_conv(a, a_dw) + a_dw_b
    a = jax.nn.silu(layer_norm(a, a_ln_g, a_ln_b))
    bb = b_b * causal_depthwise_conv(b_c * b_x, b_dw)
    return jnp.einsum("bse,ed->bsd", jnp.concatenate([a, bb], axis=-1), w_out)

def _linear_recurrence_combine(c1, c2):
    a1, b1 = c1
    a2, b2 = c2
    return a1 * a2, a2 * b1 + b2

def rglru_mixer(x, w_in, c_dw, c_dw_b, w_gate_a, b_gate_a, w_gate_x, b_gate_x, lam, w_out):
    bsz, seq, _ = x.shape
    u = jnp.einsum("bsd,de->bse", x, w_in)
    y_branch, xr = jnp.split(u, 2, axis=-1)
    xr = causal_depthwise_conv(xr, c_dw) + c_dw_b
    xh = xr.reshape(bsz, seq, RNN_HEADS, RNN_BLOCK)
    r = jax.nn.sigmoid(jnp.einsum("bshi,hij->bshj", xh, w_gate_a) + b_gate_a)
    i = jax.nn.sigmoid(jnp.einsum("bshi,hij->bshj", xh, w_gate_x) + b_gate_x)
    r = r.reshape(bsz, seq, D_RNN).astype(jnp.float32)
    i = i.reshape(bsz, seq, D_RNN)
    log_a = -LRU_C * r * jax.nn.softplus(-lam.astype(jnp.float32))
    a = jnp.exp(log_a)
    mult = jnp.sqrt(-jnp.expm1(2.0 * log_a))
    b = mult * (i * xr).astype(jnp.float32)
    _, h = lax.associative_scan(_linear_recurrence_combine, (a, b), axis=1)
    out = jax.nn.gelu(y_branch) * h.astype(x.dtype)
    return jnp.einsum("bse,ed->bsd", out, w_out)

def route(xf, w_router, b_router):
    t = xf.shape[0]
    logits = (xf @ w_router + b_router).astype(jnp.float32)
    probs = jax.nn.softmax(logits, axis=-1)
    pg = probs.reshape(t, N_EXPERT_GROUPS, EXPERTS_PER_GROUP)
    group_score = lax.top_k(pg, TOP_K)[0].sum(-1)
    g_sel = jnp.argmax(group_score, axis=-1)
    p_in = jnp.take_along_axis(pg, g_sel[:, None, None], axis=1)[:, 0]
    top_p, top_i = lax.top_k(p_in, TOP_K)
    expert_idx = g_sel[:, None] * EXPERTS_PER_GROUP + top_i
    gates = top_p / jnp.sum(top_p, axis=-1, keepdims=True)
    return expert_idx, gates

def moe(x, w_router, b_router, w1, w3, w2):
    bsz, seq, d = x.shape
    t = bsz * seq
    xf = x.reshape(t, d)
    e_idx, gates = route(xf, w_router, b_router)
    n_assign = t * TOP_K
    e_flat = e_idx.reshape(n_assign)
    tok_flat = jnp.repeat(jnp.arange(t, dtype=jnp.int32), TOP_K)
    g_flat = gates.reshape(n_assign)
    order = jnp.argsort(e_flat)
    e_s, tok_s, g_s = e_flat[order], tok_flat[order], g_flat[order]
    counts = jnp.bincount(e_flat, length=N_EXPERTS)
    padded = (counts + MOE_BLOCK - 1) // MOE_BLOCK * MOE_BLOCK
    start = jnp.cumsum(counts) - counts
    pend = jnp.cumsum(padded)
    pstart = pend - padded
    dest = pstart[e_s] + jnp.arange(n_assign, dtype=jnp.int32) - start[e_s]
    n_blocks = -(-n_assign // MOE_BLOCK) + N_EXPERTS
    n_pad = n_blocks * MOE_BLOCK
    x_pad = jnp.zeros((n_pad, d), x.dtype).at[dest].set(xf[tok_s])
    block_expert = jnp.minimum(
        jnp.searchsorted(pend, jnp.arange(n_blocks, dtype=pend.dtype) * MOE_BLOCK, side="right"),
        N_EXPERTS - 1)

    def expert_block(args):
        xb, e = args
        hb = jax.nn.silu(xb @ w1[e]) * (xb @ w3[e])
        return hb @ w2[e]

    y_pad = lax.map(expert_block, (x_pad.reshape(n_blocks, MOE_BLOCK, d), block_expert))
    y = y_pad.reshape(n_pad, d)[dest] * g_s[:, None].astype(x.dtype)
    out = jnp.zeros((t, d), x.dtype).at[tok_s].add(y)
    return out.reshape(bsz, seq, d)

def first_inputs(seed: int = 0) -> dict:
    key = jax.random.key(seed)
    ks = jax.random.split(key, 26)
    nrm = lambda k, shape, s: jax.random.normal(k, shape, jnp.float32) * s
    a0 = jax.random.uniform(ks[19], (N_ODD, D_RNN), jnp.float32, 0.9, 0.999)
    s0 = a0 ** (1.0 / LRU_C)
    lam = jnp.log(s0) - jnp.log1p(-s0)
    return {
        "x": nrm(ks[0], (BATCH, SEQ, D_MODEL), 1.0),
        "ln1_g": 1.0 + nrm(ks[1], (DEPTH, D_MODEL), 0.02),
        "ln1_b": nrm(ks[2], (DEPTH, D_MODEL), 0.02),
        "ln2_g": 1.0 + nrm(ks[3], (DEPTH, D_MODEL), 0.02),
        "ln2_b": nrm(ks[4], (DEPTH, D_MODEL), 0.02),
        "even_w_in": nrm(ks[5], (N_EVEN, D_MODEL, D_IN_EVEN), D_MODEL ** -0.5),
        "even_a_dw": nrm(ks[6], (N_EVEN, CONV_A, D_A), CONV_A ** -0.5),
        "even_a_dw_b": nrm(ks[7], (N_EVEN, D_A), 0.02),
        "even_a_ln_g": 1.0 + nrm(ks[8], (N_EVEN, D_A), 0.02),
        "even_a_ln_b": nrm(ks[9], (N_EVEN, D_A), 0.02),
        "even_b_dw": nrm(ks[10], (N_EVEN, CONV_B, D_B), CONV_B ** -0.5),
        "even_w_out": nrm(ks[11], (N_EVEN, D_A + D_B, D_MODEL), BETA * (D_A + D_B) ** -0.5),
        "odd_w_in": nrm(ks[12], (N_ODD, D_MODEL, 2 * D_RNN), D_MODEL ** -0.5),
        "odd_c_dw": nrm(ks[13], (N_ODD, CONV_C, D_RNN), CONV_C ** -0.5),
        "odd_c_dw_b": nrm(ks[14], (N_ODD, D_RNN), 0.02),
        "odd_w_gate_a": nrm(ks[15], (N_ODD, RNN_HEADS, RNN_BLOCK, RNN_BLOCK), RNN_BLOCK ** -0.5),
        "odd_b_gate_a": nrm(ks[16], (N_ODD, RNN_HEADS, RNN_BLOCK), 0.02),
        "odd_w_gate_x": nrm(ks[17], (N_ODD, RNN_HEADS, RNN_BLOCK, RNN_BLOCK), RNN_BLOCK ** -0.5),
        "odd_b_gate_x": nrm(ks[18], (N_ODD, RNN_HEADS, RNN_BLOCK), 0.02),
        "odd_lam": lam,
        "odd_w_out": nrm(ks[20], (N_ODD, D_RNN, D_MODEL), BETA * D_RNN ** -0.5),
        "w_router": nrm(ks[21], (D_MODEL, N_EXPERTS), D_MODEL ** -0.5),
        "b_router": nrm(ks[22], (N_EXPERTS,), 0.01),
        "moe_w1": nrm(ks[23], (DEPTH, N_EXPERTS, D_MODEL, D_EXPERT), D_MODEL ** -0.5),
        "moe_w3": nrm(ks[24], (DEPTH, N_EXPERTS, D_MODEL, D_EXPERT), D_MODEL ** -0.5),
        "moe_w2": nrm(ks[25], (DEPTH, N_EXPERTS, D_EXPERT, D_MODEL), BETA * D_EXPERT ** -0.5),
    }

def first_block(x, ln1_g, ln1_b, ln2_g, ln2_b, even_w_in, even_a_dw, even_a_dw_b, even_a_ln_g,
              even_a_ln_b, even_b_dw, even_w_out, odd_w_in, odd_c_dw, odd_c_dw_b, odd_w_gate_a,
              odd_b_gate_a, odd_w_gate_x, odd_b_gate_x, odd_lam, odd_w_out, w_router, b_router,
              moe_w1, moe_w3, moe_w2):
    for layer in range(DEPTH):
        j = layer // 2
        if layer % 2 == 0:
            m = conv_mixer(x, even_w_in[j], even_a_dw[j], even_a_dw_b[j], even_a_ln_g[j],
                           even_a_ln_b[j], even_b_dw[j], even_w_out[j])
        else:
            m = rglru_mixer(x, odd_w_in[j], odd_c_dw[j], odd_c_dw_b[j], odd_w_gate_a[j],
                            odd_b_gate_a[j], odd_w_gate_x[j], odd_b_gate_x[j], odd_lam[j],
                            odd_w_out[j])
        x = layer_norm(ALPHA * x + m, ln1_g[layer], ln1_b[layer])
        f = moe(x, w_router, b_router, moe_w1[layer], moe_w3[layer], moe_w2[layer])
        x = layer_norm(ALPHA * x + f, ln2_g[layer], ln2_b[layer])
    return x


HEAD_DIM = 64
A_HEADS = 4
IDX_HEADS = 8
IDX_DIM = 64
DSA_TOPK_MAX = 256
DSA_IDX_SCALE = (IDX_HEADS ** -0.5) * (IDX_DIM ** -0.5)
B_HEADS = 4
MOBA_BLOCK = 256
MOBA_TOPK = 3
MOBA_Q_CHUNK = 64
C_HEADS = 8
Q_BLOCK = 128
D_FF = 2816
ROPE_THETA = 10000.0
RMS_EPS = 1e-6

A_WIDTH = A_HEADS * HEAD_DIM
B_WIDTH = B_HEADS * HEAD_DIM
C_WIDTH = C_HEADS * HEAD_DIM
MIX_WIDTH = A_WIDTH + B_WIDTH + C_WIDTH
IN_SIZES = (A_WIDTH, HEAD_DIM, HEAD_DIM, IDX_HEADS * IDX_DIM, IDX_DIM, IDX_HEADS,
            B_WIDTH, B_WIDTH, B_WIDTH,
            C_WIDTH, C_WIDTH, C_WIDTH, C_HEADS, C_WIDTH)
IN_WIDTH = sum(IN_SIZES)


def rms_norm(x, g):
    xf = x.astype(jnp.float32)
    y = xf * lax.rsqrt(jnp.mean(xf * xf, axis=-1, keepdims=True) + RMS_EPS)
    return (y * g.astype(jnp.float32)).astype(x.dtype)

def rope_tables(seq, dim):
    inv = 1.0 / (ROPE_THETA ** (jnp.arange(0, dim, 2, dtype=jnp.float32) / dim))
    ang = jnp.arange(seq, dtype=jnp.float32)[:, None] * inv[None, :]
    return jnp.cos(ang), jnp.sin(ang)

def apply_rope(x, cos, sin):
    x1, x2 = jnp.split(x.astype(jnp.float32), 2, axis=-1)
    c = cos[None, :, None, :]
    s = sin[None, :, None, :]
    return jnp.concatenate([x1 * c - x2 * s, x2 * c + x1 * s], axis=-1).astype(x.dtype)

def swiglu(x, w_gate, w_up, w_down):
    return (jax.nn.silu(x @ w_gate) * (x @ w_up)) @ w_down

def dsa_attention(q, k, v, qi, ki, wi):
    B, S, H, D = q.shape
    topk = min(DSA_TOPK_MAX, S // 4)
    scale = D ** -0.5
    key_pos = jnp.arange(S)
    ki_f = ki.astype(jnp.float32)

    def block(i):
        q0 = i * Q_BLOCK
        qb = lax.dynamic_slice_in_dim(q, q0, Q_BLOCK, 1)
        qib = lax.dynamic_slice_in_dim(qi, q0, Q_BLOCK, 1).astype(jnp.float32)
        wib = lax.dynamic_slice_in_dim(wi, q0, Q_BLOCK, 1).astype(jnp.float32)
        qpos = q0 + jnp.arange(Q_BLOCK)
        causal = key_pos[None, :] <= qpos[:, None]
        idx_logits = jnp.einsum('bqhe,bse->bqhs', qib, ki_f)
        score = jnp.einsum('bqh,bqhs->bqs', wib * DSA_IDX_SCALE, jax.nn.relu(idx_logits))
        score = jnp.where(causal[None], score, -jnp.inf)
        _, sel = lax.top_k(score, topk)
        valid = sel <= qpos[None, :, None]
        kg = jax.vmap(lambda kk, ii: kk[ii])(k, sel)
        vg = jax.vmap(lambda vv, ii: vv[ii])(v, sel)
        s = jnp.einsum('bqhd,bqkd->bhqk', qb, kg).astype(jnp.float32) * scale
        s = jnp.where(valid[:, None], s, -jnp.inf)
        p = jax.nn.softmax(s, axis=-1).astype(v.dtype)
        return jnp.einsum('bhqk,bqkd->bqhd', p, vg)

    out = lax.map(block, jnp.arange(S // Q_BLOCK))
    return out.transpose(1, 0, 2, 3, 4).reshape(B, S, H * D)

def moba_attention(q, k, v):
    B, S, H, D = q.shape
    scale = D ** -0.5
    nblk = -(-S // MOBA_BLOCK)
    pad = nblk * MOBA_BLOCK - S
    kp = jnp.pad(k, ((0, 0), (0, pad), (0, 0), (0, 0)))
    vp = jnp.pad(v, ((0, 0), (0, pad), (0, 0), (0, 0)))
    kbh = kp.reshape(B, nblk, MOBA_BLOCK, H, D).transpose(0, 3, 1, 2, 4)
    vbh = vp.reshape(B, nblk, MOBA_BLOCK, H, D).transpose(0, 3, 1, 2, 4)
    kmean = jnp.mean(kbh.astype(jnp.float32), axis=3)
    n_sel = min(MOBA_TOPK, nblk - 1)
    blk_ids = jnp.arange(nblk)
    in_blk = jnp.arange(MOBA_BLOCK)

    def chunk(i):
        q0 = i * MOBA_Q_CHUNK
        own = q0 // MOBA_BLOCK
        qb = lax.dynamic_slice_in_dim(q, q0, MOBA_Q_CHUNK, 1)
        qpos = q0 + jnp.arange(MOBA_Q_CHUNK)
        k_own = lax.dynamic_index_in_dim(kbh, own, 2, keepdims=False)
        v_own = lax.dynamic_index_in_dim(vbh, own, 2, keepdims=False)
        own_pos = own * MOBA_BLOCK + in_blk
        s_own = jnp.einsum('bqhd,bhkd->bhqk', qb, k_own).astype(jnp.float32) * scale
        s_own = jnp.where((own_pos[None, :] <= qpos[:, None])[None, None], s_own, -jnp.inf)
        if n_sel == 0:
            p = jax.nn.softmax(s_own, axis=-1).astype(v.dtype)
            return jnp.einsum('bhqk,bhkd->bqhd', p, v_own)
        gate = jnp.einsum('bqhd,bhnd->bhqn', qb.astype(jnp.float32), kmean)
        gate = jnp.where((blk_ids < own)[None, None, None], gate, -jnp.inf)
        _, sel = lax.top_k(gate, n_sel)
        valid = sel < own
        gather = jax.vmap(jax.vmap(lambda kk, ii: kk[ii]))
        kg = gather(kbh, sel)
        vg = gather(vbh, sel)
        s_sel = jnp.einsum('bqhd,bhqnkd->bhqnk', qb, kg).astype(jnp.float32) * scale
        s_sel = jnp.where(valid[..., None], s_sel, -jnp.inf)
        s_sel = s_sel.reshape(B, H, MOBA_Q_CHUNK, n_sel * MOBA_BLOCK)
        p = jax.nn.softmax(jnp.concatenate([s_sel, s_own], axis=-1), axis=-1).astype(v.dtype)
        p_sel = p[..., :n_sel * MOBA_BLOCK].reshape(B, H, MOBA_Q_CHUNK, n_sel, MOBA_BLOCK)
        p_own = p[..., n_sel * MOBA_BLOCK:]
        return (jnp.einsum('bhqnk,bhqnkd->bqhd', p_sel, vg)
                + jnp.einsum('bhqk,bhkd->bqhd', p_own, v_own))

    out = lax.map(chunk, jnp.arange(S // MOBA_Q_CHUNK))
    return out.transpose(1, 0, 2, 3, 4).reshape(B, S, H * D)

def forgetting_attention(q, k, v, log_f):
    B, S, H, D = q.shape
    scale = D ** -0.5
    c = jnp.cumsum(log_f, axis=1).transpose(0, 2, 1)
    key_pos = jnp.arange(S)

    def block(i):
        q0 = i * Q_BLOCK
        qb = lax.dynamic_slice_in_dim(q, q0, Q_BLOCK, 1)
        cq = lax.dynamic_slice_in_dim(c, q0, Q_BLOCK, 2)
        qpos = q0 + jnp.arange(Q_BLOCK)
        s = jnp.einsum('bqhd,bkhd->bhqk', qb, k).astype(jnp.float32) * scale
        s = s + cq[..., None] - c[:, :, None, :]
        s = jnp.where((key_pos[None, :] <= qpos[:, None])[None, None], s, -jnp.inf)
        p = jax.nn.softmax(s, axis=-1).astype(v.dtype)
        return jnp.einsum('bhqk,bkhd->bqhd', p, v)

    out = lax.map(block, jnp.arange(S // Q_BLOCK))
    return out.transpose(1, 0, 2, 3, 4).reshape(B, S, H * D)

def hybrid_mixer(u, w_in, forget_bias, a_q_norm, a_k_norm, b_q_norm, b_k_norm,
                 c_q_norm, c_k_norm, w_out, cos, sin):
    B, S, _ = u.shape
    proj = u @ w_in
    splits = np.cumsum(np.array(IN_SIZES))[:-1].tolist()
    (aq, ak, av, iq, ik, iw, bq, bk, bv, cq, ck, cv, cf, cg) = jnp.split(proj, splits, axis=-1)

    aq = apply_rope(rms_norm(aq.reshape(B, S, A_HEADS, HEAD_DIM), a_q_norm), cos, sin)
    ak = apply_rope(rms_norm(ak.reshape(B, S, 1, HEAD_DIM), a_k_norm), cos, sin)[:, :, 0]
    iq = apply_rope(iq.reshape(B, S, IDX_HEADS, IDX_DIM), cos, sin)
    ik = apply_rope(ik.reshape(B, S, 1, IDX_DIM), cos, sin)[:, :, 0]
    o_a = dsa_attention(aq, ak, av, iq, ik, iw)

    bq = apply_rope(rms_norm(bq.reshape(B, S, B_HEADS, HEAD_DIM), b_q_norm), cos, sin)
    bk = apply_rope(rms_norm(bk.reshape(B, S, B_HEADS, HEAD_DIM), b_k_norm), cos, sin)
    o_b = moba_attention(bq, bk, bv.reshape(B, S, B_HEADS, HEAD_DIM))

    cq = rms_norm(cq.reshape(B, S, C_HEADS, HEAD_DIM), c_q_norm)
    ck = rms_norm(ck.reshape(B, S, C_HEADS, HEAD_DIM), c_k_norm)
    log_f = jax.nn.log_sigmoid(cf.astype(jnp.float32) + forget_bias.astype(jnp.float32))
    o_c = forgetting_attention(cq, ck, cv.reshape(B, S, C_HEADS, HEAD_DIM), log_f)
    o_c = o_c * jax.nn.sigmoid(cg)

    return jnp.concatenate([o_a, o_b, o_c], axis=-1) @ w_out

def second_inputs(seed: int = 0) -> dict:
    key = jax.random.key(seed)
    ks = jax.random.split(key, 24)

    def w(k, shape, fan_in):
        return jax.random.normal(k, shape, jnp.float32) * (fan_in ** -0.5)

    def gain(k, shape):
        return 1.0 + 0.05 * jax.random.normal(k, shape, jnp.float32)

    return {
        "x": jax.random.normal(ks[0], (BATCH, SEQ, D_MODEL), jnp.float32),
        "ffn1_norm": gain(ks[1], (DEPTH, D_MODEL)),
        "ffn1_w_gate": w(ks[2], (DEPTH, D_MODEL, D_FF), D_MODEL),
        "ffn1_w_up": w(ks[3], (DEPTH, D_MODEL, D_FF), D_MODEL),
        "ffn1_w_down": w(ks[4], (DEPTH, D_FF, D_MODEL), D_FF),
        "mix_norm": gain(ks[5], (DEPTH, D_MODEL)),
        "w_in": w(ks[6], (DEPTH, D_MODEL, IN_WIDTH), D_MODEL),
        "forget_bias": jax.random.uniform(ks[7], (DEPTH, C_HEADS), jnp.float32, 1.0, 4.0),
        "a_q_norm": gain(ks[8], (DEPTH, HEAD_DIM)),
        "a_k_norm": gain(ks[9], (DEPTH, HEAD_DIM)),
        "b_q_norm": gain(ks[10], (DEPTH, HEAD_DIM)),
        "b_k_norm": gain(ks[11], (DEPTH, HEAD_DIM)),
        "c_q_norm": gain(ks[12], (DEPTH, HEAD_DIM)),
        "c_k_norm": gain(ks[13], (DEPTH, HEAD_DIM)),
        "w_out": w(ks[14], (DEPTH, MIX_WIDTH, D_MODEL), MIX_WIDTH),
        "ffn2_norm": gain(ks[15], (DEPTH, D_MODEL)),
        "ffn2_w_gate": w(ks[16], (DEPTH, D_MODEL, D_FF), D_MODEL),
        "ffn2_w_up": w(ks[17], (DEPTH, D_MODEL, D_FF), D_MODEL),
        "ffn2_w_down": w(ks[18], (DEPTH, D_FF, D_MODEL), D_FF),
    }

def second_block(x, ffn1_norm, ffn1_w_gate, ffn1_w_up, ffn1_w_down, mix_norm, w_in, forget_bias,
              a_q_norm, a_k_norm, b_q_norm, b_k_norm, c_q_norm, c_k_norm, w_out,
              ffn2_norm, ffn2_w_gate, ffn2_w_up, ffn2_w_down):
    S = x.shape[1]
    cos, sin = rope_tables(S, HEAD_DIM)
    h = x
    for l in range(DEPTH):
        h = h + 0.5 * swiglu(rms_norm(h, ffn1_norm[l]), ffn1_w_gate[l], ffn1_w_up[l], ffn1_w_down[l])
        h = h + hybrid_mixer(rms_norm(h, mix_norm[l]), w_in[l], forget_bias[l],
                             a_q_norm[l], a_k_norm[l], b_q_norm[l], b_k_norm[l],
                             c_q_norm[l], c_k_norm[l], w_out[l], cos, sin)
        h = h + 0.5 * swiglu(rms_norm(h, ffn2_norm[l]), ffn2_w_gate[l], ffn2_w_up[l], ffn2_w_down[l])
    return h


def setup_inputs(seed=0):
    out = dict(first_inputs(seed))
    for name, value in second_inputs(seed + 1).items():
        if name != "x":
            out[name + "_2"] = value
    return out


def reference(
    x, ln1_g, ln1_b, ln2_g, ln2_b, even_w_in, even_a_dw, even_a_dw_b, even_a_ln_g, even_a_ln_b,
    even_b_dw, even_w_out, odd_w_in, odd_c_dw, odd_c_dw_b, odd_w_gate_a, odd_b_gate_a,
    odd_w_gate_x, odd_b_gate_x, odd_lam, odd_w_out, w_router, b_router, moe_w1, moe_w3, moe_w2,
    ffn1_norm_2, ffn1_w_gate_2, ffn1_w_up_2, ffn1_w_down_2, mix_norm_2, w_in_2, forget_bias_2,
    a_q_norm_2, a_k_norm_2, b_q_norm_2, b_k_norm_2, c_q_norm_2, c_k_norm_2, w_out_2,
    ffn2_norm_2, ffn2_w_gate_2, ffn2_w_up_2, ffn2_w_down_2,
):
    x = first_block(
        x, ln1_g, ln1_b, ln2_g, ln2_b, even_w_in, even_a_dw, even_a_dw_b, even_a_ln_g,
        even_a_ln_b, even_b_dw, even_w_out, odd_w_in, odd_c_dw, odd_c_dw_b, odd_w_gate_a,
        odd_b_gate_a, odd_w_gate_x, odd_b_gate_x, odd_lam, odd_w_out, w_router, b_router,
        moe_w1, moe_w3, moe_w2,
    )
    return second_block(
        x, ffn1_norm_2, ffn1_w_gate_2, ffn1_w_up_2, ffn1_w_down_2, mix_norm_2, w_in_2,
        forget_bias_2, a_q_norm_2, a_k_norm_2, b_q_norm_2, b_k_norm_2, c_q_norm_2, c_k_norm_2,
        w_out_2, ffn2_norm_2, ffn2_w_gate_2, ffn2_w_up_2, ffn2_w_down_2,
    )


_drawn_inputs = setup_inputs


def setup_inputs(seed=0):
    import zlib

    import numpy as np

    out = dict(_drawn_inputs(seed))
    spreads = {}
    factors = {'even_a_ln_g': 2.682,
     'even_a_ln_b': 2.754,
     'odd_b_gate_a': 7.209,
     'odd_b_gate_x': 6.414,
     'a_q_norm_2': 6.952,
     'a_k_norm_2': 7.623,
     'b_q_norm_2': 7.714,
     'b_k_norm_2': 7.604,
     'c_q_norm_2': 6.119,
     'c_k_norm_2': 6.311}
    for name, (base, spread) in spreads.items():
        noise = np.random.default_rng([zlib.crc32(name.encode()), seed]).standard_normal(out[name].shape)
        drawn = base * np.exp(spread * noise) if base else spread * noise
        out[name] = __import__('jax').numpy.asarray(drawn.astype(out[name].dtype))
    for name, factor in factors.items():
        out[name] = (out[name] * factor).astype(out[name].dtype)
    return out
```

```python
from contextlib import ExitStack

import concourse.bass as bass
from concourse import mybir

ALU = mybir.AluOpType
ACT = mybir.ActivationFunctionType
AX = mybir.AxisListType.X
F32 = mybir.dt.float32
F32R = mybir.dt.float32r
I32 = mybir.dt.int32

P = 128
SEQ = 256
TB = SEQ // P
D = 1024
KC = D // P
SLOT = 2048
RAW_SLOTS = 6
SPLIT_SLOTS = 3
AHEAD = 3

DEPTH = 2
ALPHA = (2.0 * DEPTH) ** 0.25
LN_EPS = 1e-5
RMS_EPS = 1e-6

D_A = 512
CONV_A = 31
CONV_B = 3
EVEN_IN = 2560
CONV_C = 4
LRU_C = 8.0
RNN_HEADS = 4

NE = 16
NG = 4
EPG = NE // NG
CAP = 64
ROUNDS = SEQ // CAP
TURN_BANK = (1, 3)
MOE_CHUNKS = 12

D_FF = 2816
FF_COLS = 256
FF_GROUPS = D_FF // FF_COLS
FF_CHUNKS = 3 * FF_GROUPS

X_LAYERS = 5
HD = 64
IN_WIDTH = 3792
IN_COLS = 474
IN_GROUPS = IN_WIDTH // IN_COLS
AQ, AK, AV, IQ, IK, IW, BQ, BK, BV, CQ, CK, CV, CF, CG = (
    0, 256, 320, 384, 896, 960, 968, 1224, 1480, 1736, 2248, 2760, 3272, 3280)
NORM_REGIONS = ((AQ, 5), (BQ, 8), (CQ, 16))
NORM_HEADS = 29
DSA_TOPK = 64
DSA_IDX_SCALE = (8 ** -0.5) * (64 ** -0.5)
QK_SCALE = HD ** -0.5
BIG = 1e30
REPLACED = -3e38
C_HEADS = 8

C_EVEN_IN = 0
C_EVEN_OUT = C_EVEN_IN + 2 * (EVEN_IN // 512)
C_MOE0 = C_EVEN_OUT + KC
C_ODD_IN = C_MOE0 + NE * MOE_CHUNKS
C_GATES = C_ODD_IN + 2 * (2 * D // 512)
C_ODD_OUT = C_GATES + 2
C_MOE1 = C_ODD_OUT + KC
C_LAYERS = C_MOE1 + NE * MOE_CHUNKS
C_FFN1 = 0
C_MIX_IN = C_FFN1 + FF_CHUNKS
C_MIX_OUT = C_MIX_IN + 2 * IN_GROUPS
C_FFN2 = C_MIX_OUT + KC
LAYER_CHUNKS = C_FFN2 + FF_CHUNKS

VEC_SETS = (
    (("even_a_dw", 124),),
    (("even_a_dw_b", 4), ("even_a_ln_g", 4), ("even_a_ln_b", 4), ("even_b_dw", 12),
     ("odd_c_dw", 32), ("odd_c_dw_b", 8), ("odd_b_gate_a", 8), ("odd_b_gate_x", 8), ("odd_lam", 8)),
    (("ffn1_norm_2", 16), ("mix_norm_2", 16), ("ffn2_norm_2", 16)),
)
VEC_AT = {}
_at = 0
for _set in VEC_SETS:
    for _name, _rows in _set:
        VEC_AT[_name] = _at
        _at += _rows
VEC_COLS = _at


class N:

    def __init__(self, base, *terms):
        self.base, self.terms = base, terms

    def __add__(self, n):
        return N(self.base + n, *self.terms)

    def __sub__(self, n):
        return self + (-n)

    def times(self, m):
        return N(self.base * m, *[(r, k * m) for r, k in self.terms])

    def plus(self, reg, k):
        if isinstance(reg, int):
            return self + reg * k
        return N(self.base, *self.terms, (reg, k))

    @property
    def v(self):
        out = self.base
        for r, k in self.terms:
            out = r * k + out
        return out


def rope_tables():
    import numpy as np

    inv = (1.0 / (10000.0 ** (np.arange(0, HD, 2, dtype=np.float32) / np.float32(HD)))).astype(np.float32)
    ang = np.arange(SEQ, dtype=np.float32)[:, None] * inv[None, :]
    cos, sin = np.cos(ang).astype(np.float32), np.sin(ang).astype(np.float32)
    return np.concatenate([cos, cos], 1), np.concatenate([-sin, sin], 1)


def build_program(nc, A, out):
    ctx = ExitStack()
    with ctx:
        base = (nc.sbuf_base + 63) // 64 * 64
        place = [base]

        def at(name, shape, dt=F32):
            cols = 1
            for s in shape[1:]:
                cols *= s
            t = nc.alloc_sbuf_tensor_at(name, shape, dt, offset=place[0])
            place[0] += (cols * 4 + 31) // 32 * 32
            assert place[0] <= nc.sbuf_usable_end, name
            return t

        def sem(name):
            return ctx.enter_context(nc.semaphore(name))

        raw = [at(f"raw{i}", [P, SLOT]) for i in range(RAW_SLOTS)]
        w_hi = [at(f"w_hi{i}", [P, SLOT], F32R) for i in range(SPLIT_SLOTS)]
        w_lo = [at(f"w_lo{i}", [P, SLOT], F32R) for i in range(SPLIT_SLOTS)]
        x = at("x", [P, TB, D])
        xT_hi = at("xT_hi", [P, KC, SEQ], F32R)
        xT_lo = at("xT_lo", [P, KC, SEQ], F32R)
        ident = at("ident", [P, P])
        tri = at("tri", [P, 2 * P])
        tri_strict = at("tri_strict", [P, P])
        slot_ids = at("slot_ids", [P, ROUNDS, P])
        earlier = at("earlier", [P, 4, 4])
        causal = at("causal", [P, TB, SEQ])
        ropeC = at("ropeC", [P, TB, HD])
        ropeS = at("ropeS", [P, TB, HD])
        vecs = at("vecs", [P, VEC_COLS])
        br = at("br", [P, NE])
        wr = at("wr", [P, KC, NE])
        wr_hi = at("wr_hi", [P, KC, NE], F32R)
        wr_lo = at("wr_lo", [P, KC, NE], F32R)
        zeros = at("zeros", [P, P], F32R)
        lneps = at("lneps", [P, 1])
        rmeps = at("rmeps", [P, 1])
        onec = at("onec", [P, 1])
        stats = at("stats", [P, TB, 2, 6])
        mv = at("mv", [P, TB, 2])
        std = at("std", [P, TB])
        rstd = at("rstd", [P, TB])
        nmr = at("nmr", [P, TB])
        sp8 = at("sp8", [P, 8])
        spt = at("spt", [P, 4, 8])
        head_gain = at("head_gain", [P, 6, HD])
        fb = at("fb", [P, C_HEADS])
        count_i = at("count_i", [P, 1], I32)
        region = place[0]

        lng = at("lng", [P, D])
        lnb = at("lnb", [P, D])
        region1 = place[0]

        vrows = [at(f"vrows{i}", [P, P]) for i in range(len(VEC_SETS))]

        place[0] = region1
        u_even = at("u_even", [P, TB, EVEN_IN])
        aT = at("aT", [P, 4, CONV_A - 1 + SEQ])
        bxT = at("bxT", [P, 4, CONV_B - 1 + SEQ])
        bbT = at("bbT", [P, 4, SEQ])
        ca = at("ca", [P, 4, SEQ])
        cb = at("cb", [P, 4, SEQ])
        an = at("an", [P, TB, D_A])
        a2 = at("a2", [P, 4, SEQ])

        place[0] = region1
        u_odd = at("u_odd", [P, TB, 2 * D])
        place[0] = region1
        lru_a = at("lru_a", [P, KC, SEQ])
        lru_t = at("lru_t", [P, KC, SEQ])
        xrT = at("xrT", [P, KC, CONV_C - 1 + SEQ])
        yT = at("yT", [P, KC, SEQ])
        xc = at("xc", [P, KC, SEQ])
        lru_r = at("lru_r", [P, KC, SEQ])
        lru_i = at("lru_i", [P, KC, SEQ])

        place[0] = region1
        xe = at("xe", [P, KC, 2 * CAP], F32R)
        pick = at("pick", [P, TB, P])
        pickT = at("pickT", [P, SEQ], F32R)
        gslot = at("gslot", [P, 1])
        gb = at("gb", [CAP, 2, 512])
        ub = at("ub", [CAP, 2, 512])
        heT = at("heT", [P, KC, 2 * CAP], F32R)
        Y_hi = at("Y_hi", [P, D], F32R)
        Y_lo = at("Y_lo", [P, D], F32R)
        prob = at("prob", [P, TB, NE])
        rmax = at("rmax", [P, TB])
        rsum = at("rsum", [P, TB])
        cmp = at("cmp", [P, TB * NG, 4, 4])
        cmp2 = at("cmp2", [P, TB * NG, 4, 4])
        rank = at("rank", [P, TB, NE])
        top2 = at("top2", [P, TB, NE])
        gscore = at("gscore", [P, TB, NG])
        grank = at("grank", [P, TB, NG])
        gcmp = at("gcmp", [P, TB, NG, NG])
        gcmp2 = at("gcmp2", [P, TB, NG, NG])
        chosen = at("chosen", [P, TB, NE])
        pos = at("pos", [P, TB, NE])
        gate = at("gate", [P, TB, NE])
        count_max = at("count_max", [P, 1])
        ov_raw = at("ov_raw", [P, D])
        ov_hi = at("ov_hi", [P, D], F32R)
        ov_lo = at("ov_lo", [P, D], F32R)

        place[0] = region
        xn = at("xn", [P, TB, D])
        sg = at("sg", [P, 2, 512])
        hb = at("hb", [P, 512])
        hT_hi = at("hT_hi", [P, 2, 2, SEQ], F32R)
        hT_lo = at("hT_lo", [P, 2, 2, SEQ], F32R)
        place[0] = region
        proj = at("proj", [P, TB, IN_WIDTH])
        QKT = at("QKT", [P, 20, SEQ])
        after_qkt = place[0]
        QK = at("QK", [P, TB, 2560])
        hsum = at("hsum", [P, TB, NORM_HEADS])
        hrs = at("hrs", [P, TB, NORM_HEADS])
        lf = at("lf", [P, TB, C_HEADS])
        lft = at("lft", [P, TB, C_HEADS])
        iws = at("iws", [P, TB, 8])
        top8 = at("top8", [P, TB, 8, 8])
        amax = at("amax", [P, 8, 4])
        asum = at("asum", [P, 8, 4])
        nlf = at("nlf", [P, TB, C_HEADS])
        after_mix = place[0]
        place[0] = after_qkt
        attn = at("attn", [P, TB, D])
        Sb = at("Sb", [P, 2, 4, SEQ])
        PT = at("PT", [P, 4, SEQ])
        place[0] = after_qkt
        relu = at("relu", [P, 8, SEQ])
        score = at("score", [P, TB, SEQ])
        work = at("work", [P, TB, SEQ])
        place[0] = after_mix
        dsa_bias = at("dsa_bias", [P, TB, SEQ])
        sq = nc.alloc_sbuf_tensor_at("sq", [P, TB, NORM_HEADS * HD], F32, offset=after_qkt - 20480)
        rt_d = nc.alloc_sbuf_tensor_at("rt_d", [P, TB, 9 * HD], F32, offset=after_qkt - 20480)
        rt_p = nc.alloc_sbuf_tensor_at("rt_p", [P, TB, 9 * HD], F32, offset=after_qkt - 20480 + 8192)

        acc = ctx.enter_context(nc.psum_tensor("acc", [P, 4, 512], F32))
        W = ctx.enter_context(nc.psum_tensor("W", [P, 4, 512], F32))

        landed = [sem(f"landed{i}") for i in range(RAW_SLOTS)]
        hi_ready = sem("hi_ready")
        lo_ready = sem("lo_ready")
        used = sem("used")
        small_in = sem("small_in")
        consts = sem("consts")
        vec_ps = sem("vec_ps")
        vecs_ok = sem("vecs_ok")
        wr_ok = sem("wr_ok")
        xt_ps, xt_hi_s, xt_lo_s = sem("xt_ps"), sem("xt_hi_s"), sem("xt_lo_s")
        tm_act, tm_dve = sem("tm_act"), sem("tm_dve")
        ln_in = sem("ln_in")
        ln_mv, ln_std, ln_rs = sem("ln_mv"), sem("ln_std"), sem("ln_rs")
        ln_x1a, ln_x0, ln_x1 = sem("ln_x1a"), sem("ln_x0"), sem("ln_x1")
        x_ready = sem("x_ready")
        ev = {n: sem("ev_" + n) for n in ("pad", "sig", "a", "bx", "tp", "tr", "conv", "back", "mv", "std", "an", "an_ps", "silu", "done")}
        od = {n: sem("od_" + n) for n in ("pad", "tp", "tr", "xc", "hi", "lo", "gates", "ri", "nla", "exp", "m2", "sqrt", "h", "out_hi", "done", "sp", "sp2")}
        rt = {n: sem("rt_" + n) for n in ("logits", "max", "exp", "chosen", "ranks", "counts", "ready")}
        me = {n: sem("me_" + n) for n in ("pick", "ga", "xh", "xe", "pt", "pte", "gb", "g", "sg", "ub", "h", "tr", "hh", "hT", "yh", "y", "sc")}
        rm = {n: sem("rm_" + n) for n in ("ssa", "ssd", "std", "rs", "xa", "xd")}
        ff = {n: sem("ff_" + n) for n in ("sg", "h", "hT")}
        mx = {n: sem("mx_" + n) for n in ("in", "sq", "ss", "std", "ng", "qkp", "qkd", "dup", "qkt", "qkta", "qktd", "is", "relu",
                                          "bias", "z", "e", "ln", "nlf", "s", "sb", "p", "t", "te", "o", "at", "x", "cg", "ib")}
        ov = [{n: sem(f"ov{i}_" + n) for n in ("landed", "hi", "lo", "free", "tensor", "scalar", "vector")} for i in range(DEPTH)]
        stored = sem("stored")

        block = ctx.enter_context(nc.Block())

        def slot_of(c):
            return c.base % RAW_SLOTS

        def split_slot(c):
            return c.base % SPLIT_SLOTS

        def landed_count(c):
            return N(16 * (c.base // RAW_SLOTS + 1), *[(r, 16 * (k // RAW_SLOTS)) for r, k in c.terms])

        OV_STEPS = {"tensor": ("gathered", "turned", "hidden_turned", "added"),
                    "scalar": ("tokens_hi", "choice", "lower_halves", "gated", "hidden_hi", "out_hi"),
                    "vector": ("pick", "tokens_lo", "gate_sum", "hidden", "hidden_lo", "out_lo")}

        def ov_done(o, step, k):
            engine = next(n for n, steps in OV_STEPS.items() if step in steps)
            steps = OV_STEPS[engine]
            return o[engine], (k.times(len(steps)) + (steps.index(step) + 1)).v

        def crowded(eng, layer, later=0):
            eng.wait_ge(rt["ready"], layer + 1)
            return eng.If(eng.value_load(count_i[0:1, 0:1], min_val=0, max_val=SEQ) > later * SEQ + CAP)

        def vec(name, i):
            return vecs[:, VEC_AT[name] + i:VEC_AT[name] + i + 1]

        def rotate(eng, src_at, dst_at, heads, scratch):
            w = heads * HD
            src = proj[:, :, src_at:src_at + w].rearrange("p b (h d) -> p b h d", d=HD)
            dst = QK[:, :, dst_at:dst_at + w].rearrange("p b (h d) -> p b h d", d=HD)
            tmp = scratch[:, :, 0:w].rearrange("p b (h d) -> p b h d", d=HD)
            for b in range(TB):
                eng.tensor_tensor(dst[:, b], src[:, b], ropeC[:, b:b + 1, :].to_broadcast([P, heads, HD]), ALU.mult)
                for lo, hi in ((0, 32), (32, 0)):
                    sin = ropeS[:, b:b + 1, lo:lo + 32].to_broadcast([P, heads, 32])
                    eng.tensor_tensor(tmp[:, b, :, lo:lo + 32], src[:, b, :, hi:hi + 32], sin, ALU.mult)
            eng.drain()
            flat = QK[:, :, dst_at:dst_at + w]
            eng.tensor_tensor(flat, flat, scratch[:, :, 0:w], ALU.add)

        @block.sync
        def _(sp):
            def load(c, src, shape):
                if c.terms or c.base >= RAW_SLOTS:
                    sp.wait_ge(lo_ready, (c - (RAW_SLOTS - 1)).v)
                k, n = shape
                dst = raw[slot_of(c)][:, 0:k * n].rearrange("p (k n) -> p k n", k=k)
                sp.dma_start(dst, src).then_inc(landed[slot_of(c)], 16)

            def rows(w, r0, k, c0, n):
                return w[r0:r0 + k * P, c0:c0 + n].rearrange("(k p) n -> p k n", p=P)

            def projection(c0, w, groups, n, first=0):
                for j in range(first, groups):
                    for half in range(2):
                        load(c0 + (2 * j + half), rows(w, 512 * half, 4, n * j, n), (4, n))

            def out_projection(c0, w):
                for k in range(KC):
                    load(c0 + k, rows(w, k * P, 1, 0, D), (1, D))

            def moe(layer, c0):
                def weights(e, ahead=0):
                    return [A[name][layer, ahead:][bass.ds(e, 1)].rearrange("a k n -> (a k) n") for name in ("moe_w1", "moe_w3", "moe_w2")]

                def half_columns(c, w, n):
                    for half in range(2):
                        load(c + half, rows(w, 512 * half, 4, 512 * (1 - n), 512), (4, 512))

                def down(c, w2, half):
                    for k in range(2):
                        load(c + k, rows(w2, 512 * (1 - half) + 256 * k, 2, 0, D), (2, D))

                def expert(e, c, last):
                    w1, w3, w2 = weights(e)
                    half_columns(c, w1, 1)
                    half_columns(c + 2, w3, 1)
                    down(c + 4, w2, 0)
                    if last:
                        down(c + 6, w2, 1)
                    else:
                        half_columns(c + 6, weights(e, 1)[0], 0)
                        down(c + 8, w2, 1)
                        half_columns(c + 10, weights(e, 1)[1], 0)

                half_columns(N(c0), weights(0)[0], 0)
                half_columns(N(c0 + 2), weights(0)[1], 0)
                with sp.Fori(0, NE - 1) as e:
                    expert(e, N(c0 + 4).plus(e, MOE_CHUNKS), False)
                expert(NE - 1, N(c0 + 4 + MOE_CHUNKS * (NE - 1)), True)

            def more_rounds(layer, crowd):
                o = ov[layer]
                with crowd:
                    with sp.Fori(0, ROUNDS - 1) as r:
                        with sp.Fori(0, NE) as e:
                            for i, name in enumerate(("moe_w1", "moe_w3", "moe_w2")):
                                w = A[name][layer, bass.ds(e, 1)].rearrange("a k n -> (a k) n")
                                for kc in range(KC):
                                    sp.wait_ge(o["free"], N(KC * i + kc + 1, (r, 24 * NE), (e, 24)).v)
                                    sp.dma_start(ov_raw[:], w[kc * P:(kc + 1) * P, :]).then_inc(o["landed"], 16)

            def ffn(c0, l, which):
                wg = A[f"ffn{which}_w_gate_2"][bass.ds(l, 1)].rearrange("a k n -> (a k) n")
                wu = A[f"ffn{which}_w_up_2"][bass.ds(l, 1)].rearrange("a k n -> (a k) n")
                wd = A[f"ffn{which}_w_down_2"][bass.ds(l, 1)].rearrange("a k n -> (a k) n")

                def up(w, c, j):
                    src = w[:, bass.ds(j * FF_COLS, FF_COLS)].rearrange("(k p) n -> p k n", p=P)
                    load(c, src, (KC, FF_COLS))

                def down(c, j):
                    src = wd[bass.ds(j * FF_COLS, FF_COLS), :].rearrange("(k p) n -> p k n", p=P)
                    load(c, src, (2, D))

                up(wg, c0, 0)
                up(wu, c0 + 1, 0)
                for j in range(2):
                    c = c0 + (2 + 3 * j)
                    up(wg, c, j + 1)
                    up(wu, c + 1, j + 1)
                    down(c + 2, j)
                    if j == 0 and which == 1:
                        more_rounds(1, crowded(sp, 1, l))
                with sp.Fori(1, (FF_GROUPS - 1) // 2) as i:
                    for t in range(2):
                        c = (c0 + (2 + 3 * t)).plus(i, 6)
                        up(wg, c, i * 2 + (t + 1))
                        up(wu, c + 1, i * 2 + (t + 1))
                        down(c + 2, i * 2 + t)
                down(c0 + (FF_CHUNKS - 1), FF_GROUPS - 1)

            projection(N(C_EVEN_IN), A["even_w_in"][0], EVEN_IN // 512, 512)
            out_projection(N(C_EVEN_OUT), A["even_w_out"][0])
            moe(0, C_MOE0)
            projection(N(C_ODD_IN), A["odd_w_in"][0], 3, 512)
            more_rounds(0, crowded(sp, 0))
            projection(N(C_ODD_IN), A["odd_w_in"][0], 2 * D // 512, 512, 3)
            for i, name in enumerate(("odd_w_gate_a", "odd_w_gate_x")):
                src = A[name].rearrange("a h (c p) j -> p (a h c) j", p=P)
                load(N(C_GATES + i), src, (8, 256))
            out_projection(N(C_ODD_OUT), A["odd_w_out"][0])
            moe(1, C_MOE1)
            with sp.Fori(0, DEPTH) as l:
                c0 = N(C_LAYERS).plus(l, LAYER_CHUNKS)
                ffn(c0 + C_FFN1, l, 1)
                w_in = A["w_in_2"][bass.ds(l, 1)].rearrange("a k n -> (a k) n")
                w_out = A["w_out_2"][bass.ds(l, 1)].rearrange("a k n -> (a k) n")
                projection(c0 + C_MIX_IN, w_in, IN_GROUPS, IN_COLS)
                out_projection(c0 + C_MIX_OUT, w_out)
                ffn(c0 + C_FFN2, l, 2)
            sp.wait_ge(x_ready, X_LAYERS + 3 * DEPTH)
            sp.dma_start(out.rearrange("a (b p) d -> p (a b) d", p=P), x[:]).then_inc(stored, 16)
            sp.wait_ge(stored, 16)

        @block.gpsimd
        def _(pool):
            g = nc.gpsimd
            pool.dma_start(x[:], A["x"].rearrange("a (b p) d -> p (a b) d", p=P)).then_inc(small_in, 16)
            for i, names in enumerate(VEC_SETS):
                r = 0
                for name, n in names:
                    a = A[name]
                    dims = "abcd"[:len(a.shape)]
                    flat = a.rearrange(f"{' '.join(dims)} -> ({' '.join(dims)})")
                    src = flat.rearrange("(r c) -> r c", c=P)
                    pool.dma_start(vrows[i][r:r + n, :], src).then_inc(small_in, 16)
                    r += n
            pool.dma_start(wr[:], A["w_router"].rearrange("(k p) e -> p k e", p=P)).then_inc(small_in, 16)
            pool.dma_start(br[:], A["b_router"].partition_broadcast(P)).then_inc(small_in, 16)
            pool.dma_start(ropeC[:], A["rope_cos"].rearrange("(b p) d -> p b d", p=P)).then_inc(small_in, 16)
            pool.dma_start(ropeS[:], A["rope_sin"].rearrange("(b p) d -> p b d", p=P)).then_inc(small_in, 16)

            def load_ln(i):
                which, layer = 1 + i % 2, i // 2
                pool.dma_start(lng[:], A[f"ln{which}_g"][layer].partition_broadcast(P)).then_inc(ln_in, 16)
                pool.dma_start(lnb[:], A[f"ln{which}_b"][layer].partition_broadcast(P)).then_inc(ln_in, 16)

            load_ln(0)
            g.memset(ident[:], 0.0)
            g.memset(tri[:], 1.0)
            g.memset(tri_strict[:], 1.0)
            g.memset(earlier[:], 1.0)
            g.memset(causal[:], 0.0)
            g.iota(slot_ids[:].rearrange("p r (h s) -> p r h s", h=2), [[CAP, ROUNDS], [0, 2], [1, CAP]], base=0,
                   channel_multiplier=0, allow_small_or_imprecise_dtypes=True)
            g.drain()
            g.affine_select(ident[:], ident[:], [[-1, P]], ALU.not_equal, 1.0, base=0, channel_multiplier=1)
            g.affine_select(tri[:, 0:P], tri[:, 0:P], [[1, P]], ALU.is_ge, 0.0, base=0, channel_multiplier=-1)
            g.affine_select(tri_strict[:], tri_strict[:], [[1, P]], ALU.is_gt, 0.0, base=0, channel_multiplier=-1)
            g.affine_select(earlier[:], earlier[:], [[1, 4], [-1, 4]], ALU.is_gt, 0.0, base=0, channel_multiplier=0)
            for b in range(TB):
                g.affine_select(causal[:, b, :], causal[:, b, :], [[-1, SEQ]], ALU.is_ge, -BIG, base=b * P,
                                channel_multiplier=1)
            g.drain().then_inc(consts, 1)

            def layer_norm(i):
                pool.wait_ge(ln_x1a, i + 1)
                pool.wait_ge(ln_in, 32 * (i + 1))
                g.tensor_tensor(x[:, 1, :], x[:, 1, :], lng[:], ALU.mult)
                g.drain()
                g.tensor_tensor(x[:, 1, :], x[:, 1, :], lnb[:], ALU.add)
                g.drain().then_inc(ln_x1, 1)
                if i + 1 < 2 * DEPTH:
                    pool.wait_ge(ln_x0, i + 1)
                    load_ln(i + 1)

            pool.wait_ge(tm_act, EVEN_IN // 512)
            pool.wait_ge(tm_dve, EVEN_IN // 512)
            g.tensor_tensor(u_even[:, :, 1536:2048], u_even[:, :, 1536:2048], u_even[:, :, 2048:2560],
                            ALU.mult).then_inc(ev["bx"], 1)
            layer_norm(0)
            layer_norm(1)
            layer_norm(2)
            layer_norm(3)

            with pool.Fori(0, DEPTH) as l:
                pool.wait_ge(x_ready, (N(X_LAYERS - 1, (l, 3))).v)
                for i, name in enumerate(("a_q_norm_2", "a_k_norm_2", "b_q_norm_2", "b_k_norm_2", "c_q_norm_2", "c_k_norm_2")):
                    src = A[name][bass.ds(l, 1)].rearrange("a d -> (a d)").partition_broadcast(P)
                    pool.dma_start(head_gain[:, i, :], src).then_inc(mx["in"], 16)
                src = A["forget_bias_2"][bass.ds(l, 1)].rearrange("a d -> (a d)").partition_broadcast(P)
                pool.dma_start(fb[:], src).then_inc(mx["in"], 16)
                pool.wait_ge(mx["ss"], (N(1, (l, 1))).v)
                rotate(g, IQ, 384, 9, rt_p)
                g.drain().then_inc(mx["qkp"], 1)

        @block.scalar
        def _(act):
            s = nc.scalar

            def split(c, cols=SLOT):
                act.wait_ge(landed[slot_of(c)], landed_count(c).v)
                if c.terms or c.base >= SPLIT_SLOTS:
                    act.wait_ge(used, (c - (SPLIT_SLOTS - 1)).v)
                s.activation(w_hi[split_slot(c)][:, 0:cols], raw[slot_of(c)][:, 0:cols], ACT.Copy).then_inc(hi_ready, 1)

            def transposed(call, gain=None):
                for q in range(4):
                    act.wait_ge(xt_ps, (call.times(4) + (q + 1)).v)
                    if gain is None:
                        last = s.activation(xT_hi[:, 2 * q:2 * q + 2, :].rearrange("p a t -> p (a t)"), W[:, q, :], ACT.Copy)
                    else:
                        for kk in range(2):
                            last = s.activation(xT_hi[:, 2 * q + kk, :], W[:, q, kk * SEQ:(kk + 1) * SEQ], ACT.Copy,
                                                scale=gain(2 * q + kk))
                    last.then_inc(xt_hi_s, 1)

            def projection(c0, dst, groups, n):
                for j in range(groups):
                    split(c0 + (2 * j + AHEAD), n_after(c0 + (2 * j + AHEAD)))
                    act.wait_ge(used, (c0 + (2 * j + 2)).v)
                    s.activation(dst[:, 0, n * j:n * (j + 1)], W[:, (2 * j) % 4, 0:n], ACT.Copy).then_inc(tm_act, 1)
                    split(c0 + (2 * j + 1 + AHEAD), n_after(c0 + (2 * j + 1 + AHEAD)))

            def n_after(c):
                i = c.base
                if not c.terms:
                    for a in (C_EVEN_OUT, C_ODD_OUT):
                        if a <= i < a + KC:
                            return D
                return SLOT

            def layer_norm(i):
                act.wait_ge(ln_mv, i + 1)
                s.activation(std[:], mv[:, :, 1], ACT.Sqrt, bias=lneps[:]).then_inc(ln_std, 1)
                act.wait_ge(ln_rs, i + 1)
                s.activation(x[:, 1, :], x[:, 1, :], ACT.Identity, bias=nmr[:, 1:2], scale=rstd[:, 1:2]).then_inc(ln_x1a, 1)

            for i, names in enumerate(VEC_SETS):
                n = sum(r for _, r in names)
                c0 = VEC_AT[names[0][0]]
                act.wait_ge(vec_ps, 1)
                last = s.activation(vecs[:, c0:c0 + n], W[:, i, 0:n], ACT.Copy)
            last.then_inc(vecs_ok, 1)
            for c in range(AHEAD):
                split(N(c))
            transposed(N(0))
            projection(N(C_EVEN_IN), u_even, EVEN_IN // 512, 512)

            act.wait_ge(tm_dve, EVEN_IN // 512)
            act.drain()
            s.activation(u_even[:, :, 512:1024], u_even[:, :, 512:1024], ACT.Sigmoid).then_inc(ev["sig"], 1)
            act.wait_ge(ev["pad"], 1)
            for i in range(6):
                act.wait_ge(ev["tp"], i + 1)
                for kk in range(2):
                    c = 2 * i + kk
                    src = W[:, i % 4, kk * SEQ:(kk + 1) * SEQ]
                    dst = (aT[:, c % 4, CONV_A - 1:], bxT[:, c % 4, CONV_B - 1:], bbT[:, c % 4, :])[c // 4]
                    last = s.activation(dst, src, ACT.Copy)
                last.then_inc(ev["tr"], 1)
            act.wait_ge(ev["mv"], 1)
            s.activation(std[:], mv[:, :, 1], ACT.Sqrt, bias=lneps[:]).then_inc(ev["std"], 1)
            for i in range(2):
                act.wait_ge(ev["an_ps"], i + 1)
                for kk in range(2):
                    c = 2 * i + kk
                    last = s.activation(a2[:, c, :], W[:, 2 + i, kk * SEQ:(kk + 1) * SEQ], ACT.Silu,
                                        bias=vec("even_a_ln_b", c), scale=vec("even_a_ln_g", c))
            act.drain()
            s.activation(xT_hi[:, 0:4, :], a2[:], ACT.Copy).then_inc(ev["silu"], 1)

            def out_projection(c0):
                for k in range(KC):
                    split(c0 + (k + AHEAD), n_after(c0 + (k + AHEAD)) if k + AHEAD < KC else SLOT)

            def tail(c0):
                for k in range(KC):
                    split(c0 + (k + AHEAD), D if k + AHEAD < KC else SLOT)

            tail(N(C_EVEN_OUT))
            layer_norm(0)

            def experts(layer, c0):
                i = layer
                transposed(N(1 + 2 * layer))
                act.wait_ge(rt["max"], i + 1)
                s.activation(prob[:], prob[:], ACT.Exp).then_inc(rt["exp"], 1)
                def tokens(e):
                    act.wait_ge(me["ga"], (N(NE * layer).plus(e, 1) + 1).v)
                    s.activation(xe[:, :, 0:CAP], W[:, 3, :].rearrange("p (k t) -> p k t", t=CAP), ACT.Copy).then_inc(me["xh"], 1)

                def bottom(dst, bank, n, used_count, name):
                    act.wait_ge(used, used_count.v)
                    s.activation(dst[:, n, :], W[CAP:P, bank, :], ACT.Copy).then_inc(me[name], 1)

                def expert(e, c, last):
                    one = N(NE * layer).plus(e, 1)
                    two = one.times(2)

                    def silu(n):
                        act.wait_ge(me["g"], (two + (n + 1)).v)
                        s.activation(gb[:, n, :], gb[:, n, :], ACT.Silu).then_inc(me["sg"], 1)

                    def hidden_hi(n):
                        act.wait_ge(me["tr"], (two + (n + 1)).v)
                        s.activation(heT[:, 4 * n:4 * n + 4, 0:CAP],
                                     W[:, TURN_BANK[n], 0:256].rearrange("p (k t) -> p k t", t=CAP),
                                     ACT.Copy).then_inc(me["hh"], 1)

                    silu(0)
                    act.wait_ge(me["pt"], (one + 1).v)
                    s.activation(pickT[:], W[:, 1, 0:SEQ], ACT.Copy)
                    s.activation(gslot[:], W[:, 1, SEQ:SEQ + 1], ACT.Copy).then_inc(me["pte"], 1)
                    split(c + 3)
                    split(c + 4)
                    bottom(gb, 2, 1, c + 2, "gb")
                    split(c + 5)
                    hidden_hi(0)
                    silu(1)
                    split(c + 6)
                    bottom(ub, 0, 1, c + 4, "ub")
                    if not last:
                        tokens(e + 1)
                    split(c + 7)
                    split(c + 8)
                    hidden_hi(1)
                    split(c + 9)
                    if not last:
                        split(c + 10)
                        bottom(gb, 0, 0, c + 8, "gb")
                        split(c + 11)
                    act.wait_ge(me["pte"], (one + 1).v)
                    act.wait_ge(used, (c + (8 if last else 10)).v)
                    for n in range(2):
                        s.activation(Y_hi[:, 512 * n:512 * (n + 1)], W[:, 1 + n, :], ACT.Copy, scale=gslot[:]).then_inc(me["yh"], 1)
                    split(c + (10 if last else 12))
                    if not last:
                        split(c + 13)
                        split(c + 14)
                        bottom(ub, 3, 0, c + 12, "ub")

                tokens(0)
                split(N(c0 + 3))
                split(N(c0 + 4))
                bottom(gb, 0, 0, N(c0 + 2), "gb")
                split(N(c0 + 5))
                split(N(c0 + 6))
                bottom(ub, 3, 0, N(c0 + 4), "ub")
                with act.Fori(0, NE - 1) as e:
                    expert(e, N(c0 + 4).plus(e, MOE_CHUNKS), False)
                expert(NE - 1, N(c0 + 4 + MOE_CHUNKS * (NE - 1)), True)
                with crowded(act, layer):
                    more_rounds(layer)

            def more_rounds(layer):
                o = ov[layer]
                with act.Fori(0, ROUNDS - 1) as r:
                    with act.Fori(0, NE) as e:
                        k = N(0, (r, NE), (e, 1))

                        def split_rows(i):
                            c = k.times(24) + i
                            act.wait_ge(o["landed"], (c + 1).times(16).v)
                            s.activation(ov_hi[:], ov_raw[:], ACT.Copy).then_inc(o["hi"], 1)

                        act.wait_ge(*ov_done(o, "gathered", k))
                        s.activation(xe[:, :, 0:CAP], W[:, 3, :].rearrange("p (k t) -> p k t", t=CAP), ACT.Copy).then_inc(o["scalar"], 1)
                        act.wait_ge(*ov_done(o, "turned", k))
                        s.activation(pickT[:], W[:, 0, 0:SEQ], ACT.Copy)
                        s.activation(gslot[:], W[:, 0, SEQ:SEQ + 1], ACT.Copy).then_inc(o["scalar"], 1)
                        for i in range(2 * KC):
                            split_rows(i)
                        act.wait_ge(o["free"], (k.times(24) + (2 * KC + 1)).v)
                        s.activation(gb[:], W[CAP:P, 0:2, :], ACT.Copy)
                        s.activation(ub[:], W[CAP:P, 2:4, :], ACT.Copy).then_inc(o["scalar"], 1)
                        act.wait_ge(*ov_done(o, "gate_sum", k))
                        s.activation(gb[:], gb[:], ACT.Silu).then_inc(o["scalar"], 1)
                        act.wait_ge(*ov_done(o, "hidden_turned", k))
                        s.activation(heT[:, :, 0:CAP], W[:, 0, :].rearrange("p (k t) -> p k t", t=CAP), ACT.Copy).then_inc(o["scalar"], 1)
                        for i in range(2 * KC, 3 * KC):
                            split_rows(i)
                        act.wait_ge(o["free"], (k.times(24) + (3 * KC + 1)).v)
                        s.activation(Y_hi[:], W[:, 1:3, :].rearrange("p a n -> p (a n)"), ACT.Copy, scale=gslot[:]).then_inc(o["scalar"], 1)

            experts(0, C_MOE0)
            layer_norm(1)

            transposed(N(2))
            projection(N(C_ODD_IN), u_odd, 2 * D // 512, 512)
            act.wait_ge(od["pad"], 1)
            for i in range(8):
                act.wait_ge(od["tp"], i + 1)
                if i < 4:
                    last = s.activation(xrT[:, 2 * i:2 * i + 2, CONV_C - 1:], W[:, i % 4, :].rearrange("p (a t) -> p a t", a=2), ACT.Copy)
                else:
                    last = s.activation(yT[:, 2 * i - 8:2 * i - 6, :], W[:, i % 4, :].rearrange("p (a t) -> p a t", a=2), ACT.Gelu_apprx_tanh)
                last.then_inc(od["tr"], 1)
            act.wait_ge(od["sp"], 1)
            s.activation(spt[:, 1, :], spt[:, 0, :], ACT.Exp, scale=-1.0)
            act.drain()
            s.activation(spt[:, 2, :], spt[:, 1, :], ACT.Ln, bias=onec[:]).then_inc(od["sp2"], 1)
            act.wait_ge(od["xc"], 1)
            s.activation(xT_hi[:], xc[:], ACT.Copy).then_inc(od["hi"], 1)
            for i in range(8):
                act.wait_ge(od["gates"], i + 1)
                s.activation(lru_r[:, i, :], W[:, i % 4, 0:SEQ], ACT.Sigmoid, bias=vec("odd_b_gate_a", i))
                s.activation(lru_i[:, i, :], W[:, i % 4, SEQ:2 * SEQ], ACT.Sigmoid, bias=vec("odd_b_gate_x", i)).then_inc(od["ri"], 1)
            split(N(C_GATES + AHEAD), D)
            split(N(C_GATES + AHEAD + 1), D)
            act.wait_ge(od["nla"], 1)
            s.activation(lru_a[:], lru_r[:], ACT.Exp, scale=-1.0)
            s.activation(lru_t[:], lru_r[:], ACT.Tanh).then_inc(od["exp"], 1)
            act.wait_ge(od["m2"], 1)
            s.activation(lru_t[:], lru_t[:], ACT.Sqrt).then_inc(od["sqrt"], 1)
            act.wait_ge(od["h"], 1)
            s.activation(xT_hi[:], xc[:], ACT.Copy).then_inc(od["out_hi"], 1)
            tail(N(C_ODD_OUT))
            layer_norm(2)

            experts(1, C_MOE1)
            layer_norm(3)

            def rms(call):
                act.wait_ge(x_ready, (call + X_LAYERS).v)
                s.activation(xn[:, 0, :], x[:, 0, :], ACT.Square, accum_out=std[:, 0:1])
                act.drain().then_inc(rm["ssa"], 1)
                act.wait_ge(rm["ssd"], (call + 1).v)
                s.activation(std[:], std[:], ACT.Sqrt, bias=rmeps[:], scale=1.0 / D).then_inc(rm["std"], 1)
                act.wait_ge(rm["rs"], (call + 1).v)
                s.activation(xn[:, 0, :], x[:, 0, :], ACT.Copy, scale=rstd[:, 0:1]).then_inc(rm["xa"], 1)

            def gain_of(name, l):
                a = VEC_AT[name]
                return lambda k: vecs[:, bass.ds(l * KC + (a + k), 1)]

            def ffn(c0, last):
                def silu(parity, consumed):
                    act.wait_ge(used, consumed.v)
                    s.activation(sg[:, parity, :], W[:, 2 * parity, :], ACT.Silu).then_inc(ff["sg"], 1)

                split(c0 + 3)
                silu(0, c0 + 1)
                split(c0 + 4)
                with act.Fori(0, (FF_GROUPS - 3) // 2) as i:
                    for t in range(2):
                        c = (c0 + (2 + 3 * t)).plus(i, 6)
                        split(c + 3)
                        silu(1 - t, c + 1)
                        split(c + 4)
                        split(c + 5)
                for t in range(2):
                    for k in range(3):
                        i = 2 + 3 * (FF_GROUPS - 3 + t) + k
                        if i + AHEAD < FF_CHUNKS or not last:
                            split(c0 + (i + AHEAD))
                        if k == 0:
                            silu(1 - t, c0 + (i + 1))
                if not last:
                    split(c0 + (FF_CHUNKS - 1 + AHEAD))

            def mixer(l, c0):
                lay = N(0, (l, 1))
                c = c0 + C_MIX_IN
                for j in range(IN_GROUPS):
                    split(c + (2 * j + 3), 4 * IN_COLS if 2 * j + 3 < 16 else D)
                    act.wait_ge(used, (c + (2 * j + 2)).v)
                    s.activation(proj[:, 0, IN_COLS * j:IN_COLS * (j + 1)], W[:, (2 * j) % 4, 0:IN_COLS],
                                 ACT.Copy).then_inc(tm_act, 1)
                    split(c + (2 * j + 4), 4 * IN_COLS if 2 * j + 4 < 16 else D)
                act.drain()
                act.wait_ge(tm_dve, N(9 + IN_GROUPS, (l, IN_GROUPS)).v)
                o = 0
                for at0, n in NORM_REGIONS:
                    last = s.activation(sq[:, :, o:o + n * HD], proj[:, :, at0:at0 + n * HD], ACT.Square)
                    o += n * HD
                last.then_inc(mx["sq"], 1)
                s.activation(proj[:, :, CG:IN_WIDTH], proj[:, :, CG:IN_WIDTH], ACT.Sigmoid).then_inc(mx["cg"], 1)
                act.wait_ge(mx["ss"], (lay + 1).v)
                s.activation(hrs[:], hsum[:], ACT.Sqrt, bias=rmeps[:], scale=1.0 / HD).then_inc(mx["std"], 1)
                act.wait_ge(mx["z"], (lay + 1).v)
                s.activation(lft[:], lft[:], ACT.Exp, scale=-1.0)
                act.drain()
                s.activation(lft[:], lft[:], ACT.Ln, bias=onec[:]).then_inc(mx["ln"], 1)
                act.wait_ge(mx["qkd"], (lay + 1).v)
                s.activation(QK[:, :, 320:384], QK[:, :, 256:320], ACT.Copy)
                act.wait_ge(mx["qkp"], (lay + 1).v)
                s.activation(QK[:, :, 960:1024], QK[:, :, 896:960], ACT.Copy).then_inc(mx["dup"], 1)
                for i in range(0, 10, 2):
                    act.wait_ge(mx["qkt"], (lay.times(10) + (i + 1)).v)
                    s.activation(QKT[:, 2 * i:2 * i + 2, :], W[:, i % 4, :].rearrange("p (a t) -> p a t", a=2),
                                 ACT.Copy).then_inc(mx["qkta"], 1)
                for b in range(TB):
                    act.wait_ge(mx["is"], (lay.times(2) + (b + 1)).v)
                    if b == 1:
                        act.wait_ge(mx["ib"], (lay + 1).v)
                    n = P * (b + 1)
                    src = (acc, W)[b][:, 0:2 * (b + 1), :].rearrange("p a (h k) -> p (a h) k", k=n)
                    s.activation(relu[:, :, 0:n], src, ACT.Relu).then_inc(mx["relu"], 1)
                for u in range(8):
                    b, n = u // 4, P * (u // 4 + 1)
                    act.wait_ge(mx["sb"], (lay.times(8) + (u + 1)).v)
                    for h in range(4):
                        s.activation(Sb[:, u % 2, h, 0:n], Sb[:, u % 2, h, 0:n], ACT.Exp, bias=amax[:, u, h:h + 1],
                                     accum_out=asum[:, u, h:h + 1])
                    act.drain().then_inc(mx["p"], 1)
                    act.wait_ge(mx["t"], (lay.times(8) + (u + 1)).v)
                    s.activation(PT[:, :, 0:n], acc[:, 0:b + 1, :].rearrange("p a (h k) -> p (a h) k", k=n),
                                 ACT.Copy).then_inc(mx["te"], 1)
                transposed(N(6, (l, 4)))
                for k in range(KC):
                    split(c0 + (C_MIX_OUT + k + AHEAD), D if k + AHEAD < KC else SLOT)

            with act.Fori(0, DEPTH) as l:
                c0 = N(C_LAYERS).plus(l, LAYER_CHUNKS)
                rms(N(0, (l, 3)))
                transposed(N(4, (l, 4)), gain_of("ffn1_norm_2", l))
                ffn(c0 + C_FFN1, False)
                rms(N(1, (l, 3)))
                transposed(N(5, (l, 4)), gain_of("mix_norm_2", l))
                mixer(l, c0)
                rms(N(2, (l, 3)))
                transposed(N(7, (l, 4)), gain_of("ffn2_norm_2", l))
                ffn(c0 + C_FFN2, True)
                with act.If(l < DEPTH - 1):
                    for k in range(AHEAD):
                        split(c0 + (LAYER_CHUNKS + k))

        @block.vector
        def _(dve):
            v = nc.vector

            def rest(c, cols=SLOT):
                dve.wait_ge(hi_ready, (c + 1).v)
                v.tensor_tensor(w_lo[split_slot(c)][:, 0:cols], raw[slot_of(c)][:, 0:cols],
                                w_hi[split_slot(c)][:, 0:cols].bitcast(F32), ALU.subtract).then_inc(lo_ready, 1)

            def n_after(c):
                for a in (C_EVEN_OUT, C_ODD_OUT):
                    if a <= c.base < a + KC:
                        return D
                return SLOT

            def transposed(call, gain=None):
                for q in range(4):
                    dve.wait_ge(xt_hi_s, (call.times(4) + (q + 1)).v)
                    hi = xT_hi[:, 2 * q:2 * q + 2, :].rearrange("p a t -> p (a t)").bitcast(F32)
                    lo = xT_lo[:, 2 * q:2 * q + 2, :].rearrange("p a t -> p (a t)")
                    if gain is None:
                        last = v.tensor_tensor(lo, W[:, q, :], hi, ALU.subtract)
                    else:
                        for kk in range(2):
                            cols = slice(kk * SEQ, (kk + 1) * SEQ)
                            last = v.scalar_tensor_tensor(lo[:, cols], W[:, q, cols], gain(2 * q + kk), hi[:, cols],
                                                          ALU.mult, ALU.subtract)
                    last.then_inc(xt_lo_s, 1)

            def projection(c0, dst, groups, n):
                for j in range(groups):
                    rest(c0 + (2 * j + AHEAD), n_after(c0 + (2 * j + AHEAD)))
                    dve.wait_ge(used, (c0 + (2 * j + 2)).v)
                    v.tensor_copy(dst[:, 1, n * j:n * (j + 1)], W[:, (2 * j + 1) % 4, 0:n]).then_inc(tm_dve, 1)
                    rest(c0 + (2 * j + 1 + AHEAD), n_after(c0 + (2 * j + 1 + AHEAD)))

            def tail(c0):
                for k in range(KC):
                    rest(c0 + (k + AHEAD), D if k + AHEAD < KC else SLOT)

            def layer_norm(i, ready, count):
                dve.wait_ge(ready, count)
                for b in range(TB):
                    v.scalar_tensor_tensor(x[:, b, :], x[:, b, :], ALPHA, acc[:, 2 * b:2 * b + 2, :].rearrange("p a n -> p (a n)"),
                                           ALU.mult, ALU.add)
                v.drain()
                for b in range(TB):
                    for n in range(2):
                        v.bn_stats(stats[:, b, n, :], x[:, b, 512 * n:512 * (n + 1)])
                v.drain()
                for b in range(TB):
                    v.bn_aggr(mv[:, b, :], stats[:, b, :, :].rearrange("p a s -> p (a s)"))
                v.drain().then_inc(ln_mv, 1)
                dve.wait_ge(ln_std, i + 1)
                v.reciprocal(rstd[:], std[:])
                v.drain()
                v.scalar_tensor_tensor(nmr[:], mv[:, :, 0], -1.0, rstd[:], ALU.mult, ALU.mult)
                v.drain().then_inc(ln_rs, 1)
                v.tensor_scalar(x[:, 0, :], x[:, 0, :], mv[:, 0, 0:1], rstd[:, 0:1], ALU.subtract, ALU.mult)
                v.drain()
                dve.wait_ge(ln_in, 32 * (i + 1))
                v.tensor_tensor(x[:, 0, :], x[:, 0, :], lng[:], ALU.mult)
                v.drain()
                v.tensor_tensor(x[:, 0, :], x[:, 0, :], lnb[:], ALU.add)
                v.drain().then_inc(ln_x0, 1)
                dve.wait_ge(ln_x1, i + 1)
                dve.sem_inc(x_ready, 1)

            v.memset(zeros[:].bitcast(F32), 0.0)
            v.memset(lneps[:], LN_EPS)
            v.memset(rmeps[:], RMS_EPS)
            v.memset(onec[:], 1.0)
            v.memset(aT[:, :, 0:CONV_A - 1], 0.0)
            v.memset(bxT[:, :, 0:CONV_B - 1], 0.0)
            v.drain().then_inc(ff["h"], 1)
            dve.wait_ge(small_in, SMALL_LOADS * 16)
            dve.sem_inc(ev["pad"], 1)
            dve.sem_inc(x_ready, 1)
            v.tensor_copy(wr_hi[:], wr[:])
            v.drain()
            v.tensor_tensor(wr_lo[:], wr[:], wr_hi[:].bitcast(F32), ALU.subtract).then_inc(wr_ok, 1)
            for c in range(AHEAD):
                rest(N(c))
            transposed(N(0))
            projection(N(C_EVEN_IN), u_even, EVEN_IN // 512, 512)

            dve.wait_ge(ev["sig"], 1)
            v.tensor_tensor(u_even[:, :, 0:512], u_even[:, :, 0:512], u_even[:, :, 512:1024], ALU.mult).then_inc(ev["a"], 1)
            dve.wait_ge(ev["tr"], 2)
            for k in range(CONV_A):
                for c in range(4):
                    tap = vec("even_a_dw", 4 * k + c)
                    src = aT[:, c, k:k + SEQ]
                    if k == 0:
                        v.tensor_scalar(ca[:, c, :], src, tap, vec("even_a_dw_b", c), ALU.mult, ALU.add)
                    else:
                        last = v.scalar_tensor_tensor(ca[:, c, :], src, tap, ca[:, c, :], ALU.mult, ALU.add)
                if k < CONV_A - 1:
                    v.drain()
            last.then_inc(ev["conv"], 1)
            dve.wait_ge(ev["tr"], 6)
            for k in range(CONV_B):
                for c in range(4):
                    tap = vec("even_b_dw", 4 * k + c)
                    src = bxT[:, c, k:k + SEQ]
                    if k == 0:
                        v.tensor_scalar(cb[:, c, :], src, tap, None, ALU.mult)
                    else:
                        v.scalar_tensor_tensor(cb[:, c, :], src, tap, cb[:, c, :], ALU.mult, ALU.add)
                v.drain()
            v.tensor_tensor(cb[:], cb[:], bbT[:], ALU.mult)
            v.drain()
            v.tensor_copy(xT_hi[:, 4:8, :], cb[:])
            v.drain()
            v.tensor_tensor(xT_lo[:, 4:8, :], cb[:], xT_hi[:, 4:8, :].bitcast(F32), ALU.subtract)
            dve.wait_ge(ev["back"], 1)
            for b in range(TB):
                v.bn_stats(stats[:, b, 0, :], W[:, b, :])
            v.drain()
            for b in range(TB):
                v.bn_aggr(mv[:, b, :], stats[:, b, 0, :])
            v.drain().then_inc(ev["mv"], 1)
            dve.wait_ge(ev["std"], 1)
            v.reciprocal(rstd[:], std[:])
            v.drain()
            for b in range(TB):
                last = v.tensor_scalar(an[:, b, :], W[:, b, :], mv[:, b, 0:1], rstd[:, b:b + 1], ALU.subtract, ALU.mult)
            last.then_inc(ev["an"], 1)
            dve.wait_ge(ev["silu"], 1)
            v.tensor_tensor(xT_lo[:, 0:4, :], a2[:], xT_hi[:, 0:4, :].bitcast(F32), ALU.subtract).then_inc(ev["done"], 1)
            tail(N(C_EVEN_OUT))
            layer_norm(0, used, C_EVEN_OUT + KC)

            def top_ranks(values, greater, equal, out, n, groups):
                shape = [P, groups, n, n]
                other, own = values.unsqueeze(2).to_broadcast(shape), values.unsqueeze(3).to_broadcast(shape)
                v.tensor_tensor(greater, other, own, ALU.is_gt)
                v.tensor_tensor(equal, other, own, ALU.is_equal)
                v.drain()
                v.tensor_tensor(equal, equal, earlier[:].unsqueeze(1).to_broadcast(shape), ALU.mult)
                v.drain()
                v.tensor_tensor(greater, greater, equal, ALU.add)
                v.drain()
                v.tensor_reduce(out, greater, AX, ALU.add)
                v.drain()

            def experts(layer, c0):
                i = layer
                transposed(N(1 + 2 * layer))
                dve.wait_ge(rt["logits"], i + 1)
                wide = [P, TB, NE]
                v.tensor_tensor(prob[:], W[:, 0, 0:TB * NE].rearrange("p (b e) -> p b e", b=TB),
                                br[:].unsqueeze(1).to_broadcast(wide), ALU.add)
                v.drain()
                v.tensor_reduce(rmax[:], prob[:], AX, ALU.max)
                v.drain()
                v.tensor_tensor(prob[:], prob[:], rmax[:].unsqueeze(2).to_broadcast(wide), ALU.subtract)
                v.drain().then_inc(rt["max"], 1)
                dve.wait_ge(rt["exp"], i + 1)
                v.tensor_reduce(rsum[:], prob[:], AX, ALU.add)
                v.drain()
                v.reciprocal(rsum[:], rsum[:])
                v.drain()
                v.tensor_tensor(prob[:], prob[:], rsum[:].unsqueeze(2).to_broadcast(wide), ALU.mult)
                v.drain()
                grouped = prob[:].rearrange("p b (g c) -> p (b g) c", c=EPG)
                top_ranks(grouped, cmp[:], cmp2[:], rank[:].rearrange("p b (g c) -> p (b g) c", c=EPG), EPG, TB * NG)
                v.tensor_scalar(top2[:], rank[:], 1.5, None, ALU.is_lt)
                v.drain()
                v.tensor_tensor(chosen[:], prob[:], top2[:], ALU.mult)
                v.drain()
                v.tensor_reduce(gscore[:].rearrange("p b g -> p (b g)"), chosen[:].rearrange("p b (g c) -> p (b g) c", c=EPG), AX, ALU.add)
                v.drain()
                top_ranks(gscore[:], gcmp[:], gcmp2[:], grank[:], NG, TB)
                v.tensor_scalar(grank[:], grank[:], 0.5, None, ALU.is_lt)
                v.drain()
                v.tensor_tensor(top2[:].rearrange("p b (g c) -> p (b g) c", c=EPG), top2[:].rearrange("p b (g c) -> p (b g) c", c=EPG),
                                grank[:].rearrange("p b g -> p (b g)").unsqueeze(2).to_broadcast([P, TB * NG, EPG]), ALU.mult)
                v.drain().then_inc(rt["chosen"], 1)
                v.tensor_tensor(chosen[:], prob[:], top2[:], ALU.mult)
                v.drain()
                v.tensor_reduce(rsum[:], chosen[:], AX, ALU.add)
                v.drain()
                v.reciprocal(rsum[:], rsum[:])
                v.drain()
                v.tensor_tensor(gate[:], chosen[:], rsum[:].unsqueeze(2).to_broadcast(wide), ALU.mult)
                dve.wait_ge(rt["ranks"], i + 1)
                v.scalar_tensor_tensor(pos[:, :, 0:NE], W[:, 1, 0:TB * NE].rearrange("p (b e) -> p b e", b=TB), 1.0, top2[:],
                                       ALU.add, ALU.mult)
                v.tensor_reduce(count_max[:], W[:, 1, TB * NE:(TB + 1) * NE], AX, ALU.max)
                v.drain()
                v.tensor_scalar(pos[:, :, 0:NE], pos[:, :, 0:NE], -1.0, None, ALU.add)
                v.tensor_copy(count_i[:], count_max[:])
                v.drain().then_inc(rt["ready"], 1)

                def pick_tokens(e):
                    for b in range(TB):
                        last = v.tensor_scalar(pick[:, b, :], slot_ids[:, 0, :], pos[:, b, e], None, ALU.is_equal)
                    last.then_inc(me["pick"], 1)

                def gate_first(count):
                    dve.wait_ge(me["gb"], count.v)
                    v.tensor_tensor(gb[:, 0, :], W[0:CAP, 0, :], gb[:, 0, :], ALU.add).then_inc(me["g"], 1)

                def expert(e, c, last):
                    one = N(NE * layer).plus(e, 1)
                    two = one.times(2)

                    def add_bottom(buf, bank, n, name):
                        dve.wait_ge(me[name], (two + (n + 1)).v)
                        return v.tensor_tensor(buf[:, n, :], W[0:CAP, bank, :], buf[:, n, :], ALU.add)

                    def hidden(bank, n):
                        add_bottom(ub, bank, n, "ub")
                        v.drain()
                        dve.wait_ge(me["sg"], (two + (n + 1)).v)
                        v.tensor_tensor(ub[:, n, :], ub[:, n, :], gb[:, n, :], ALU.mult).then_inc(me["h"], 1)

                    def hidden_lo(n):
                        dve.wait_ge(me["hh"], (two + (n + 1)).v)
                        v.tensor_tensor(heT[:, 4 * n:4 * n + 4, CAP:2 * CAP],
                                        W[:, TURN_BANK[n], 0:256].rearrange("p (k t) -> p k t", t=CAP),
                                        heT[:, 4 * n:4 * n + 4, 0:CAP].bitcast(F32), ALU.subtract).then_inc(me["hT"], 1)

                    hidden(3, 0)
                    rest(c + 3)
                    if not last:
                        dve.wait_ge(me["pt"], (one + 1).v)
                        pick_tokens(bass.ds(e + 1, 1))
                    rest(c + 4)
                    add_bottom(gb, 2, 1, "gb").then_inc(me["g"], 1)
                    rest(c + 5)
                    hidden_lo(0)
                    rest(c + 6)
                    hidden(0, 1)
                    if not last:
                        tokens_lo(e + 1)
                    rest(c + 7)
                    rest(c + 8)
                    hidden_lo(1)
                    rest(c + 9)
                    if not last:
                        rest(c + 10)
                        gate_first(two + 3)
                        rest(c + 11)
                    for n in range(2):
                        dve.wait_ge(me["yh"], (two + (n + 1)).v)
                        cols = slice(512 * n, 512 * (n + 1))
                        v.scalar_tensor_tensor(Y_lo[:, cols], W[:, 1 + n, :], gslot[:, 0:1], Y_hi[:, cols].bitcast(F32),
                                               ALU.mult, ALU.subtract).then_inc(me["y"], 1)
                    rest(c + (10 if last else 12))
                    if not last:
                        rest(c + 13)
                        rest(c + 14)

                def tokens_lo(e):
                    dve.wait_ge(me["xh"], (N(NE * layer).plus(e, 1) + 1).v)
                    v.tensor_tensor(xe[:, :, CAP:2 * CAP], W[:, 3, :].rearrange("p (k t) -> p k t", t=CAP),
                                    xe[:, :, 0:CAP].bitcast(F32), ALU.subtract).then_inc(me["xe"], 1)

                pick_tokens(slice(0, 1))
                tokens_lo(0)
                rest(N(c0 + 3))
                rest(N(c0 + 4))
                gate_first(N(2 * NE * layer + 1))
                rest(N(c0 + 5))
                rest(N(c0 + 6))
                with dve.Fori(0, NE - 1) as e:
                    expert(e, N(c0 + 4).plus(e, MOE_CHUNKS), False)
                expert(NE - 1, N(c0 + 4 + MOE_CHUNKS * (NE - 1)), True)
                with crowded(dve, layer):
                    more_rounds(layer)

            def more_rounds(layer):
                o = ov[layer]
                dve.wait_ge(me["ga"], NE * (layer + 1))
                with dve.Fori(0, ROUNDS - 1) as r:
                    with dve.Fori(0, NE) as e:
                        k = N(0, (r, NE), (e, 1))

                        def rest_rows(i):
                            dve.wait_ge(o["hi"], (k.times(24) + (i + 1)).v)
                            v.tensor_tensor(ov_lo[:], ov_raw[:], ov_hi[:].bitcast(F32), ALU.subtract).then_inc(o["lo"], 1)

                        v.drain()
                        for b in range(TB):
                            last = v.tensor_scalar(pick[:, b, :], slot_ids[:, bass.ds(r + 1, 1), :].rearrange("p a s -> p (a s)"),
                                                   pos[:, b, bass.ds(e, 1)], None, ALU.is_equal)
                        last.then_inc(o["vector"], 1)
                        dve.wait_ge(*ov_done(o, "tokens_hi", k))
                        v.tensor_tensor(xe[:, :, CAP:2 * CAP], W[:, 3, :].rearrange("p (k t) -> p k t", t=CAP),
                                        xe[:, :, 0:CAP].bitcast(F32), ALU.subtract).then_inc(o["vector"], 1)
                        for i in range(2 * KC):
                            rest_rows(i)
                        dve.wait_ge(*ov_done(o, "lower_halves", k))
                        v.tensor_tensor(gb[:], W[0:CAP, 0:2, :], gb[:], ALU.add).then_inc(o["vector"], 1)
                        v.tensor_tensor(ub[:], W[0:CAP, 2:4, :], ub[:], ALU.add)
                        v.drain()
                        dve.wait_ge(*ov_done(o, "gated", k))
                        v.tensor_tensor(ub[:], ub[:], gb[:], ALU.mult).then_inc(o["vector"], 1)
                        dve.wait_ge(*ov_done(o, "hidden_hi", k))
                        v.tensor_tensor(heT[:, :, CAP:2 * CAP], W[:, 0, :].rearrange("p (k t) -> p k t", t=CAP),
                                        heT[:, :, 0:CAP].bitcast(F32), ALU.subtract).then_inc(o["vector"], 1)
                        for i in range(2 * KC, 3 * KC):
                            rest_rows(i)
                        dve.wait_ge(*ov_done(o, "out_hi", k))
                        v.scalar_tensor_tensor(Y_lo[:], W[:, 1:3, :].rearrange("p a n -> p (a n)"), gslot[:, 0:1],
                                               Y_hi[:].bitcast(F32), ALU.mult, ALU.subtract).then_inc(o["vector"], 1)
                        dve.wait_ge(*ov_done(o, "added", k))

            experts(0, C_MOE0)
            layer_norm(1, me["sc"], NE)

            v.memset(xrT[:, :, 0:CONV_C - 1], 0.0).then_inc(od["pad"], 1)
            v.scalar_tensor_tensor(spt[:, 0, :], vecs[:, VEC_AT["odd_lam"]:VEC_AT["odd_lam"] + 8], -1.0,
                                   vecs[:, VEC_AT["odd_lam"]:VEC_AT["odd_lam"] + 8], ALU.mult, ALU.max).then_inc(od["sp"], 1)
            transposed(N(2))
            projection(N(C_ODD_IN), u_odd, 2 * D // 512, 512)
            dve.wait_ge(od["tr"], 4)
            for k in range(CONV_C):
                for c in range(KC):
                    tap = vec("odd_c_dw", 8 * k + c)
                    src = xrT[:, c, k:k + SEQ]
                    if k == 0:
                        v.tensor_scalar(xc[:, c, :], src, tap, vec("odd_c_dw_b", c), ALU.mult, ALU.add)
                    else:
                        v.scalar_tensor_tensor(xc[:, c, :], src, tap, xc[:, c, :], ALU.mult, ALU.add)
                v.drain()
            dve.sem_inc(od["xc"], 1)
            dve.wait_ge(od["sp2"], 1)
            lam = vecs[:, VEC_AT["odd_lam"]:VEC_AT["odd_lam"] + 8]
            v.tensor_scalar(spt[:, 0, :], spt[:, 1, :], 1.0, None, ALU.add)
            v.drain()
            v.scalar_tensor_tensor(spt[:, 3, :], spt[:, 0, :], -1.0, spt[:, 1, :], ALU.add, ALU.subtract)
            v.drain()
            v.reciprocal(spt[:, 1, :], spt[:, 0, :])
            v.drain()
            v.tensor_tensor(spt[:, 3, :], spt[:, 3, :], spt[:, 1, :], ALU.mult)
            v.drain()
            v.tensor_scalar(spt[:, 0, :], lam, -1.0, 0.0, ALU.mult, ALU.max)
            v.drain()
            v.tensor_tensor(spt[:, 2, :], spt[:, 2, :], spt[:, 3, :], ALU.subtract)
            v.drain()
            v.tensor_tensor(spt[:, 2, :], spt[:, 2, :], spt[:, 0, :], ALU.add)
            v.drain()
            v.tensor_scalar(sp8[:], spt[:, 2, :], LRU_C, None, ALU.mult)
            dve.wait_ge(od["hi"], 1)
            v.tensor_tensor(xT_lo[:], xc[:], xT_hi[:].bitcast(F32), ALU.subtract).then_inc(od["lo"], 1)
            v.drain()
            dve.wait_ge(od["ri"], 8)
            v.tensor_tensor(lru_r[:], lru_r[:], sp8[:].unsqueeze(2).to_broadcast([P, KC, SEQ]), ALU.mult).then_inc(od["nla"], 1)
            v.tensor_tensor(lru_i[:], lru_i[:], xc[:], ALU.mult)
            rest(N(C_GATES + AHEAD), D)
            rest(N(C_GATES + AHEAD + 1), D)
            v.drain()
            dve.wait_ge(od["exp"], 1)
            v.tensor_tensor(xc[:], lru_a[:], lru_a[:], ALU.mult)
            v.drain()
            v.scalar_tensor_tensor(lru_t[:].rearrange("p a t -> p (a t)"), xc[:].rearrange("p a t -> p (a t)"), 1.0,
                                   lru_t[:].rearrange("p a t -> p (a t)"), ALU.add, ALU.mult).then_inc(od["m2"], 1)
            dve.wait_ge(od["sqrt"], 1)
            v.tensor_tensor(lru_t[:], lru_t[:], lru_i[:], ALU.mult)
            v.drain()
            for c in range(KC):
                v.tensor_tensor_scan(lru_r[:, c, :], lru_a[:, c, :], lru_t[:, c, :], 0.0, ALU.mult, ALU.add)
            v.drain()
            dve.wait_ge(od["tr"], 8)
            v.tensor_tensor(xc[:], lru_r[:], yT[:], ALU.mult).then_inc(od["h"], 1)
            dve.wait_ge(od["out_hi"], 1)
            v.tensor_tensor(xT_lo[:], xc[:], xT_hi[:].bitcast(F32), ALU.subtract).then_inc(od["done"], 1)
            tail(N(C_ODD_OUT))
            layer_norm(2, used, C_ODD_OUT + KC)

            experts(1, C_MOE1)
            layer_norm(3, me["sc"], 2 * NE)

            def rms(call):
                dve.wait_ge(x_ready, (call + X_LAYERS).v)
                v.tensor_tensor_reduce(xn[:, 1, :], x[:, 1, :], x[:, 1, :], 1.0, 0.0, ALU.mult, ALU.add, std[:, 1:2])
                v.drain().then_inc(rm["ssd"], 1)
                dve.wait_ge(rm["std"], (call + 1).v)
                v.reciprocal(rstd[:], std[:])
                v.drain().then_inc(rm["rs"], 1)
                v.tensor_scalar(xn[:, 1, :], x[:, 1, :], rstd[:, 1:2], None, ALU.mult).then_inc(rm["xd"], 1)

            def add_to_x(count, scale):
                dve.wait_ge(used, count.v)
                for b in range(TB):
                    v.scalar_tensor_tensor(x[:, b, :], acc[:, 2 * b:2 * b + 2, :].rearrange("p a n -> p (a n)"), scale,
                                           x[:, b, :], ALU.mult, ALU.add)
                v.drain().then_inc(x_ready, 1)

            def gain_of(name, l):
                a = VEC_AT[name]
                return lambda k: vecs[:, bass.ds(l * KC + (a + k), 1)]

            def ffn(c0, sg0, last):
                def hidden(parity, consumed, n):
                    dve.wait_ge(used, consumed.v)
                    dve.wait_ge(ff["sg"], n.v)
                    v.tensor_tensor(hb[:], W[:, 2 * parity + 1, :], sg[:, parity, :], ALU.mult)
                    v.drain().then_inc(ff["h"], 1)
                    hi, lo = (t[:, parity].rearrange("p a t -> p (a t)") for t in (hT_hi, hT_lo))
                    v.tensor_copy(hi, hb[:])
                    v.drain()
                    v.tensor_tensor(lo, hb[:], hi.bitcast(F32), ALU.subtract)
                    v.drain().then_inc(ff["hT"], 1)

                rest(c0 + 3)
                rest(c0 + 4)
                hidden(0, c0 + 2, sg0 + 1)
                with dve.Fori(0, (FF_GROUPS - 3) // 2) as i:
                    for t in range(2):
                        c = (c0 + (2 + 3 * t)).plus(i, 6)
                        rest(c + 3)
                        rest(c + 4)
                        hidden(1 - t, c + 2, (sg0 + (t + 2)).plus(i, 2))
                        rest(c + 5)
                for t in range(2):
                    for k in range(3):
                        i = 2 + 3 * (FF_GROUPS - 3 + t) + k
                        if i + AHEAD < FF_CHUNKS or not last:
                            rest(c0 + (i + AHEAD))
                        if k == 1:
                            hidden(1 - t, c0 + (i + 1), sg0 + (FF_GROUPS - 1 + t))
                if not last:
                    rest(c0 + (FF_CHUNKS - 1 + AHEAD))
                add_to_x(c0 + FF_CHUNKS, 0.5)

            def mixer(l, c0):
                lay = N(0, (l, 1))
                c = c0 + C_MIX_IN
                for j in range(IN_GROUPS):
                    rest(c + (2 * j + 3), 4 * IN_COLS if 2 * j + 3 < 16 else D)
                    dve.wait_ge(used, (c + (2 * j + 2)).v)
                    v.tensor_copy(proj[:, 1, IN_COLS * j:IN_COLS * (j + 1)], W[:, (2 * j + 1) % 4, 0:IN_COLS]).then_inc(tm_dve, 1)
                    rest(c + (2 * j + 4), 4 * IN_COLS if 2 * j + 4 < 16 else D)
                v.drain()
                dve.wait_ge(mx["in"], (lay + 1).times(112).v)
                dve.wait_ge(tm_act, N(9 + IN_GROUPS, (l, IN_GROUPS)).v)
                v.tensor_tensor(lf[:], proj[:, :, CF:CG], fb[:].unsqueeze(1).to_broadcast([P, TB, C_HEADS]), ALU.add)
                for b in range(TB):
                    v.tensor_scalar(iws[:, b, :].rearrange("p (r a) -> p r a", r=2),
                                    proj[:, b, IW:BQ].rearrange("p (a r) -> p r a", r=2), DSA_IDX_SCALE, None, ALU.mult)
                for i in (0, 2, 4):
                    v.tensor_scalar(head_gain[:, i, :], head_gain[:, i, :], QK_SCALE, None, ALU.mult)
                v.drain()
                v.scalar_tensor_tensor(lft[:], lf[:], -1.0, lf[:], ALU.mult, ALU.max).then_inc(mx["z"], 1)
                dve.wait_ge(mx["sq"], (lay + 1).v)
                v.tensor_reduce(hsum[:].rearrange("p b h -> p (b h)"), sq[:].rearrange("p b (h d) -> p (b h) d", d=HD), AX,
                                ALU.add).then_inc(mx["ss"], 1)
                dve.wait_ge(mx["std"], (lay + 1).v)
                v.reciprocal(hrs[:], hrs[:])
                v.drain()
                o = 0
                for at0, n in NORM_REGIONS:
                    for b in range(TB):
                        heads = proj[:, b, at0:at0 + n * HD].rearrange("p (h d) -> p h d", d=HD)
                        v.tensor_tensor(heads, heads, hrs[:, b, o:o + n].unsqueeze(2).to_broadcast([P, n, HD]), ALU.mult)
                    o += n
                v.drain()
                for i, (at0, n, to) in enumerate(((AQ, 4, None), (AK, 1, None), (BQ, 4, None), (BK, 4, None),
                                                  (CQ, 8, 1536), (CK, 8, 2048))):
                    for b in range(TB):
                        heads = proj[:, b, at0:at0 + n * HD].rearrange("p (h d) -> p h d", d=HD)
                        dst = heads if to is None else QK[:, b, to:to + n * HD].rearrange("p (h d) -> p h d", d=HD)
                        v.tensor_tensor(dst, heads, head_gain[:, i:i + 1, :].to_broadcast([P, n, HD]), ALU.mult)
                v.drain()
                rotate(v, AQ, 0, 5, rt_d)
                v.drain()
                rotate(v, BQ, 1024, 8, rt_d)
                v.drain().then_inc(mx["qkd"], 1)
                dve.wait_ge(mx["ln"], (lay + 1).v)
                v.tensor_scalar(lf[:], lf[:], -1.0, 0.0, ALU.mult, ALU.max)
                v.drain()
                v.tensor_tensor(nlf[:], lf[:], lft[:], ALU.add).then_inc(mx["nlf"], 1)
                for i in range(1, 10, 2):
                    dve.wait_ge(mx["qkt"], (lay.times(10) + (i + 1)).v)
                    v.tensor_copy(QKT[:, 2 * i:2 * i + 2, :], W[:, i % 4, :].rearrange("p (a t) -> p a t", a=2)).then_inc(mx["qktd"], 1)
                for b in range(TB):
                    n = P * (b + 1)
                    dve.wait_ge(mx["relu"], (lay.times(2) + (b + 1)).v)
                    v.tensor_tensor(relu[:, :, 0:n], relu[:, :, 0:n], iws[:, b, :].unsqueeze(2).to_broadcast([P, 8, n]), ALU.mult)
                    v.drain()
                    v.tensor_reduce(score[:, b, 0:n], relu[:, :, 0:n].rearrange("p h k -> p k h"), AX, ALU.add)
                    if b == 0:
                        v.drain().then_inc(mx["ib"], 1)
                    else:
                        v.drain()
                    v.tensor_tensor(score[:, b, 0:n], score[:, b, 0:n], causal[:, b, 0:n], ALU.add)
                    v.drain()
                    left = score
                    for r in range(DSA_TOPK // 8):
                        v.max(top8[:, b, r, :], left[:, b, 0:n])
                        v.drain()
                        v.match_replace(work[:, b, 0:n], top8[:, b, r, :], left[:, b, 0:n], REPLACED)
                        v.drain()
                        left = work
                    v.tensor_tensor(dsa_bias[:, b, 0:n], work[:, b, 0:n], score[:, b, 0:n], ALU.is_equal)
                    v.drain()
                    v.scalar_tensor_tensor(dsa_bias[:, b, 0:n], dsa_bias[:, b, 0:n], -BIG, causal[:, b, 0:n], ALU.mult, ALU.min)
                    v.drain()

                def finish(u):
                    b, grp = u // 4, u % 4
                    dve.wait_ge(mx["o"], (lay.times(8) + (u + 1)).v)
                    v.reciprocal(asum[:, u, :], asum[:, u, :])
                    v.drain()
                    for r in range(2):
                        dst = attn[:, b, 256 * grp:256 * (grp + 1)].rearrange("p (a r d) -> p r a d", r=2, d=HD)[:, r]
                        last = v.tensor_tensor(dst, acc[:, 2 + u % 2, P * r:P * (r + 1)].rearrange("p (a d) -> p a d", d=HD),
                                               asum[:, u, 2 * r:2 * r + 2].unsqueeze(2).to_broadcast([P, 2, HD]), ALU.mult)
                    if grp >= 2:
                        v.drain()
                        flat = attn[:, b, 256 * grp:256 * (grp + 1)]
                        cg = CG + 256 * (grp - 2)
                        last = v.tensor_tensor(flat, flat, proj[:, b, cg:cg + 256], ALU.mult)
                    last.then_inc(mx["at"], 1)

                for u in range(8):
                    b, n = u // 4, P * (u // 4 + 1)
                    dve.wait_ge(mx["s"], (lay.times(8) + (u + 1)).v)
                    if u >= 2:
                        dve.wait_ge(mx["t"], (lay.times(8) + (u - 1)).v)
                    bias = (dsa_bias if u % 4 == 0 else causal)[:, b:b + 1, 0:n].to_broadcast([P, 2, n])
                    k = 2 * (u % 2)
                    for r in range(2):
                        v.tensor_tensor(Sb[:, u % 2, 2 * r:2 * r + 2, 0:n], W[:, k + r, 0:2 * n].rearrange("p (h k) -> p h k", k=n),
                                        bias, ALU.add)
                    v.drain()
                    v.tensor_reduce(amax[:, u, :], Sb[:, u % 2, :, 0:n], AX, ALU.max, negate=True)
                    v.drain().then_inc(mx["sb"], 1)
                    if u:
                        finish(u - 1)
                finish(7)
                transposed(N(6, (l, 4)))
                for k in range(KC):
                    rest(c0 + (C_MIX_OUT + k + AHEAD), D if k + AHEAD < KC else SLOT)
                add_to_x(c0 + (C_MIX_OUT + KC), 1.0)

            with dve.Fori(0, DEPTH) as l:
                c0 = N(C_LAYERS).plus(l, LAYER_CHUNKS)
                rms(N(0, (l, 3)))
                transposed(N(4, (l, 4)), gain_of("ffn1_norm_2", l))
                ffn(c0 + C_FFN1, N(0, (l, 2 * FF_GROUPS)), False)
                rms(N(1, (l, 3)))
                transposed(N(5, (l, 4)), gain_of("mix_norm_2", l))
                mixer(l, c0)
                rms(N(2, (l, 3)))
                transposed(N(7, (l, 4)), gain_of("ffn2_norm_2", l))
                ffn(c0 + C_FFN2, N(FF_GROUPS, (l, 2 * FF_GROUPS)), True)
                with dve.If(l < DEPTH - 1):
                    for k in range(AHEAD):
                        rest(c0 + (LAYER_CHUNKS + k))

        @block.tensor
        def _(pe):
            t = nc.tensor

            def transposes(call, src, waits):
                for sm, n in waits:
                    pe.wait_ge(sm, n)
                for q in range(4):
                    for kk in range(2):
                        for b in range(TB):
                            k = 2 * q + kk
                            last = t.transpose(W[:, q, kk * SEQ + b * P:kk * SEQ + (b + 1) * P], src[:, b, k * P:(k + 1) * P], ident[:])
                    last.then_inc(xt_ps, 1)

            def wait_xT(call):
                pe.wait_ge(xt_lo_s, (call + 1).times(4).v)

            def exact(out, a_hi, a_lo, b_hi, b_lo, first, last):
                t.matmul(out, a_hi, b_hi, start=first, stop=False)
                t.matmul(out, a_hi, b_lo, start=False, stop=False)
                return t.matmul(out, a_lo, b_hi, start=False, stop=last)

            def projection(c0, groups, n, before):
                for j in range(groups):
                    for half in range(2):
                        c = c0 + (2 * j + half)
                        pe.wait_ge(lo_ready, (c + 1).v)
                        if half == 0 and j >= 2:
                            pe.wait_ge(tm_act, (before + (j - 1)).v)
                            pe.wait_ge(tm_dve, (before + (j - 1)).v)
                        hi, lo = w_hi[split_slot(c)], w_lo[split_slot(c)]
                        for k in range(4):
                            kc = 4 * half + k
                            for b in range(TB):
                                tok = slice(b * P, (b + 1) * P)
                                last = exact(W[:, (2 * j + b) % 4, 0:n], xT_hi[:, kc, tok], xT_lo[:, kc, tok],
                                             hi[:, k * n:(k + 1) * n], lo[:, k * n:(k + 1) * n], kc == 0, kc == KC - 1)
                        last.then_inc(used, 1)

            def into_acc(c, kn, a_hi, a_lo, first, final):
                pe.wait_ge(lo_ready, (c + 1).v)
                hi, lo = w_hi[split_slot(c)], w_lo[split_slot(c)]
                for k in range(kn):
                    for b in range(TB):
                        tok = slice(b * P, (b + 1) * P)
                        st, sp_ = first and k == 0, final and k == kn - 1
                        for n in range(2):
                            cols = slice(k * D + 512 * n, k * D + 512 * (n + 1))
                            t.matmul(acc[:, 2 * b + n, :], a_hi(k)[:, tok], hi[:, cols], start=st, stop=False)
                            t.matmul(acc[:, 2 * b + n, :], a_hi(k)[:, tok], lo[:, cols], start=False, stop=False)
                        for n in range(2):
                            cols = slice(k * D + 512 * n, k * D + 512 * (n + 1))
                            last = t.matmul(acc[:, 2 * b + n, :], a_lo(k)[:, tok], hi[:, cols], start=False, stop=sp_)
                last.then_inc(used, 1)

            def out_projection(c0):
                for kc in range(KC):
                    into_acc(c0 + kc, 1, lambda k: xT_hi[:, kc, :], lambda k: xT_lo[:, kc, :], kc == 0, kc == KC - 1)

            pe.wait_ge(consts, 1)
            pe.wait_ge(small_in, SMALL_LOADS * 16)
            for i, names in enumerate(VEC_SETS):
                n = sum(r for _, r in names)
                last = t.transpose(W[:, i, 0:n], vrows[i][0:n, :], ident[0:n, 0:n])
            last.then_inc(vec_ps, 1)
            pe.wait_ge(vecs_ok, 1)
            transposes(N(0), x, ((x_ready, 1),))
            wait_xT(N(0))
            projection(N(C_EVEN_IN), EVEN_IN // 512, 512, N(0))

            pe.wait_ge(tm_act, EVEN_IN // 512)
            pe.wait_ge(tm_dve, EVEN_IN // 512)
            for i in range(6):
                if i == 0:
                    pe.wait_ge(ev["a"], 1)
                if i == 2:
                    pe.wait_ge(ev["bx"], 1)
                if i >= 4:
                    pe.wait_ge(ev["tr"], i - 3)
                for kk in range(2):
                    c = 2 * i + kk
                    col = (0, 1536, 1024)[c // 4] + (c % 4) * P
                    for b in range(TB):
                        last = t.transpose(W[:, i % 4, kk * SEQ + b * P:kk * SEQ + (b + 1) * P], u_even[:, b, col:col + P], ident[:])
                last.then_inc(ev["tp"], 1)
            pe.wait_ge(ev["conv"], 1)
            pe.wait_ge(ev["tr"], 6)
            for b in range(TB):
                for c in range(4):
                    last = t.transpose(W[:, b, c * P:(c + 1) * P], ca[:, c, b * P:(b + 1) * P], ident[:])
            last.then_inc(ev["back"], 1)
            pe.wait_ge(ev["an"], 1)
            for i in range(2):
                for kk in range(2):
                    c = 2 * i + kk
                    for b in range(TB):
                        last = t.transpose(W[:, 2 + i, kk * SEQ + b * P:kk * SEQ + (b + 1) * P], an[:, b, c * P:(c + 1) * P], ident[:])
                last.then_inc(ev["an_ps"], 1)
            pe.wait_ge(ev["done"], 1)
            out_projection(N(C_EVEN_OUT))

            def gather(done):
                for kc in range(KC):
                    for b in range(TB):
                        last = t.matmul(W[:, 3, kc * CAP:(kc + 1) * CAP], x[:, b, kc * P:(kc + 1) * P],
                                        pick[:, b, 0:CAP], start=(b == 0), stop=(b == TB - 1))
                last.then_inc(done, 1)

            def scatter(done, ready):
                for n in range(2):
                    pe.wait_ge(*ready[n])
                    for b in range(TB):
                        for Y in (Y_hi, Y_lo):
                            last = t.matmul(acc[:, 2 * b + n, :], pickT[:, b * P:(b + 1) * P], Y[:, 512 * n:512 * (n + 1)],
                                            start=False, stop=False, skip_group_check=True)
                last.then_inc(done, 1)

            def experts(layer, c0):
                i = layer
                transposes(N(1 + 2 * layer), x, ((x_ready, 2 + 2 * layer),))
                wait_xT(N(1 + 2 * layer))
                pe.wait_ge(wr_ok, 1)
                for b in range(TB):
                    tok = slice(b * P, (b + 1) * P)
                    for k in range(KC):
                        last = exact(W[:, 0, b * NE:(b + 1) * NE], xT_hi[:, k, tok], xT_lo[:, k, tok],
                                     wr_hi[:, k, :], wr_lo[:, k, :], k == 0, k == KC - 1)
                last.then_inc(rt["logits"], 1)
                for n in range(4):
                    t.matmul(acc[:, n, :], zeros[:], xT_hi[:, 0:2, :].rearrange("p a t -> p (a t)"), start=True, stop=False, skip_group_check=True)
                pe.wait_ge(rt["chosen"], i + 1)
                ones = tri[:, P:2 * P]
                t.matmul(W[:, 1, 0:NE], tri_strict[:], top2[:, 0, :], start=True, stop=True)
                t.matmul(W[:, 1, NE:2 * NE], ones, top2[:, 0, :], start=True, stop=False)
                t.matmul(W[:, 1, NE:2 * NE], tri_strict[:], top2[:, 1, :], start=False, stop=True)
                t.matmul(W[:, 1, 2 * NE:3 * NE], ones, top2[:, 0, :], start=True, stop=False)
                t.matmul(W[:, 1, 2 * NE:3 * NE], ones, top2[:, 1, :], start=False, stop=True).then_inc(rt["ranks"], 1)

                pe.wait_ge(me["pick"], NE * layer + 1)
                gather(me["ga"])
                def chunk(c, bank, first):
                    pe.wait_ge(lo_ready, (c + 1).v)
                    for k in range(4):
                        kc = k + (0 if first else 4)
                        cols = slice(512 * k, 512 * (k + 1))
                        t.matmul(W[:, bank, :], xe[:, kc, :], w_hi[split_slot(c)][:, cols], start=(kc == 0), stop=False)
                        last = t.matmul(W[:, bank, :], xe[:, kc, :], w_lo[split_slot(c)][:, cols], start=False, stop=(kc == KC - 1))
                    last.then_inc(used, 1)

                def expert(e, c, last):
                    one = N(NE * layer).plus(e, 1)
                    two = one.times(2)

                    def turn_hidden(n):
                        pe.wait_ge(me["h"], (two + (n + 1)).v)
                        for k in range(4):
                            turn = t.matmul if k == 0 else t.transpose
                            last = turn(W[:, TURN_BANK[n], k * CAP:(k + 1) * CAP], ub[:, n, k * P:(k + 1) * P],
                                        ident[0:CAP, 0:CAP], **({"start": True, "stop": True} if k == 0 else {}))
                        last.then_inc(me["tr"], 1)

                    def down(c, i):
                        pe.wait_ge(lo_ready, (c + 1).v)
                        for k in range(2):
                            kc = 2 * i + k
                            for w in (w_hi, w_lo):
                                for n in range(2):
                                    cols = slice(k * D + 512 * n, k * D + 512 * (n + 1))
                                    last = t.matmul(W[:, 1 + n, :], heT[:, kc, :], w[split_slot(c)][:, cols],
                                                    start=(kc == 0 and w is w_hi),
                                                    stop=(kc == KC - 1 and w is w_lo))
                        last.then_inc(used, 1)

                    for b in range(TB):
                        t.transpose(W[:, 1, b * P:(b + 1) * P], pick[:, b, :], ident[:])
                    gates = gate[:, :, bass.ds(e, 1)]
                    for b in range(TB):
                        turned = t.matmul(W[:, 1, SEQ:SEQ + 1], pick[:, b, :], gates[:, b], start=(b == 0), stop=(b == TB - 1))
                    turned.then_inc(me["pt"], 1)
                    chunk(c, 2, True)
                    chunk(c + 1, 2, False)
                    pe.wait_ge(me["g"], (two + 1).v)
                    chunk(c + 2, 0, True)
                    pe.wait_ge(me["pte"], (one + 1).v)
                    turn_hidden(0)
                    chunk(c + 3, 0, False)
                    if not last:
                        pe.wait_ge(me["pick"], (one + 2).v)
                        gather(me["ga"])
                    pe.wait_ge(me["hT"], (two + 1).v)
                    pe.wait_ge(me["g"], (two + 2).v)
                    down(c + 4, 0)
                    down(c + 5, 1)
                    if not last:
                        pe.wait_ge(me["xe"], (one + 2).v)
                    turn_hidden(1)
                    if not last:
                        chunk(c + 6, 0, True)
                        chunk(c + 7, 0, False)
                    pe.wait_ge(me["hT"], (two + 2).v)
                    d = c + (6 if last else 8)
                    down(d, 2)
                    down(d + 1, 3)
                    if not last:
                        chunk(c + 10, 3, True)
                        chunk(c + 11, 3, False)
                    scatter(me["sc"], [(me["y"], (two + (n + 1)).v) for n in range(2)])

                pe.wait_ge(me["xe"], NE * layer + 1)
                chunk(N(c0), 0, True)
                chunk(N(c0 + 1), 0, False)
                chunk(N(c0 + 2), 3, True)
                chunk(N(c0 + 3), 3, False)
                with pe.Fori(0, NE - 1) as e:
                    expert(e, N(c0 + 4).plus(e, MOE_CHUNKS), False)
                expert(NE - 1, N(c0 + 4 + MOE_CHUNKS * (NE - 1)), True)
                with crowded(pe, layer):
                    more_rounds(layer)

            def more_rounds(layer):
                o = ov[layer]
                pe.sem_inc(o["free"], 1)
                with pe.Fori(0, ROUNDS - 1) as r:
                    with pe.Fori(0, NE) as e:
                        k = N(0, (r, NE), (e, 1))
                        pe.wait_ge(*ov_done(o, "pick", k))
                        gather(o["tensor"])
                        for b in range(TB):
                            t.transpose(W[:, 0, b * P:(b + 1) * P], pick[:, b, :], ident[:])
                        for b in range(TB):
                            last = t.matmul(W[:, 0, SEQ:SEQ + 1], pick[:, b, :], gate[:, b, bass.ds(e, 1)],
                                            start=(b == 0), stop=(b == TB - 1))
                        last.then_inc(o["tensor"], 1)
                        pe.wait_ge(*ov_done(o, "tokens_lo", k))
                        pe.wait_ge(*ov_done(o, "choice", k))
                        for i in range(2 * KC):
                            pe.wait_ge(o["lo"], (k.times(24) + (i + 1)).v)
                            kc = i % KC
                            for n in range(2):
                                cols = slice(512 * n, 512 * (n + 1))
                                out = W[:, 2 * (i // KC) + n, :]
                                t.matmul(out, xe[:, kc, :], ov_hi[:, cols], start=(kc == 0), stop=False)
                                last = t.matmul(out, xe[:, kc, :], ov_lo[:, cols], start=False, stop=(kc == KC - 1))
                            last.then_inc(o["free"], 1)
                        pe.wait_ge(*ov_done(o, "hidden", k))
                        for kc in range(KC):
                            turn = t.matmul if kc == 0 else t.transpose
                            last = turn(W[:, 0, kc * CAP:(kc + 1) * CAP], ub[:, kc // 4, (kc % 4) * P:(kc % 4 + 1) * P],
                                        ident[0:CAP, 0:CAP], **({"start": True, "stop": True} if kc == 0 else {}))
                        last.then_inc(o["tensor"], 1)
                        pe.wait_ge(*ov_done(o, "hidden_lo", k))
                        for kc in range(KC):
                            pe.wait_ge(o["lo"], (k.times(24) + (2 * KC + kc + 1)).v)
                            for n in range(2):
                                cols = slice(512 * n, 512 * (n + 1))
                                t.matmul(W[:, 1 + n, :], heT[:, kc, :], ov_hi[:, cols], start=(kc == 0), stop=False)
                                last = t.matmul(W[:, 1 + n, :], heT[:, kc, :], ov_lo[:, cols], start=False, stop=(kc == KC - 1))
                            last.then_inc(o["free"], 1)
                        scatter(o["tensor"], [ov_done(o, "out_lo", k)] * 2)

            experts(0, C_MOE0)

            transposes(N(2), x, ((x_ready, 3),))
            wait_xT(N(2))
            projection(N(C_ODD_IN), 2 * D // 512, 512, N(5))
            pe.wait_ge(tm_act, 9)
            pe.wait_ge(tm_dve, 9)
            for i in range(8):
                if i >= 4:
                    pe.wait_ge(od["tr"], i - 3)
                for kk in range(2):
                    c = (2 * i + kk) % KC
                    col = (D if i < 4 else 0) + c * P
                    for b in range(TB):
                        last = t.transpose(W[:, i % 4, kk * SEQ + b * P:kk * SEQ + (b + 1) * P], u_odd[:, b, col:col + P], ident[:])
                last.then_inc(od["tp"], 1)
            ga, gx = N(C_GATES), N(C_GATES + 1)
            pe.wait_ge(lo_ready, C_GATES + 2)
            pe.wait_ge(od["tr"], 8)
            pe.wait_ge(od["lo"], 1)
            for h in range(RNN_HEADS):
                for jc in range(2):
                    i = 2 * h + jc
                    if i >= 4:
                        pe.wait_ge(od["ri"], i - 3)
                    for part, c in enumerate((ga, gx)):
                        for ic in range(2):
                            cols = slice((2 * h + ic) * 256 + jc * P, (2 * h + ic) * 256 + (jc + 1) * P)
                            last = exact(W[:, i % 4, part * SEQ:(part + 1) * SEQ], w_hi[split_slot(c)][:, cols], w_lo[split_slot(c)][:, cols],
                                         xT_hi[:, 2 * h + ic, :], xT_lo[:, 2 * h + ic, :], ic == 0, ic == 1)
                    last.then_inc(od["gates"], 1)
            pe.drain().then_inc(used, 2)
            pe.wait_ge(od["done"], 1)
            out_projection(N(C_ODD_OUT))

            experts(1, C_MOE1)

            def ffn(c0, h0):
                def up(c, bank):
                    pe.wait_ge(lo_ready, (c + 1).v)
                    hi, lo = w_hi[split_slot(c)], w_lo[split_slot(c)]
                    for f in range(2):
                        for kc in range(KC):
                            cols = slice(kc * FF_COLS + f * P, kc * FF_COLS + (f + 1) * P)
                            last = exact_w(W[:, bank, f * SEQ:(f + 1) * SEQ], hi[:, cols], lo[:, cols], kc)
                    last.then_inc(used, 1)

                def exact_w(out, hi, lo, kc):
                    t.matmul(out, hi, xT_hi[:, kc, :], start=(kc == 0), stop=False)
                    t.matmul(out, hi, xT_lo[:, kc, :], start=False, stop=False)
                    return t.matmul(out, lo, xT_hi[:, kc, :], start=False, stop=(kc == KC - 1))

                def down(c, parity, n, first, final):
                    pe.wait_ge(ff["hT"], n.v)
                    into_acc(c, 2, lambda k: hT_hi[:, parity, k, :], lambda k: hT_lo[:, parity, k, :], first, final)

                up(c0, 0)
                up(c0 + 1, 1)
                first = True
                def group(c, j_par, n, first):
                    pe.wait_ge(ff["h"], n.v)
                    up(c, 2 * (1 - j_par))
                    up(c + 1, 2 * (1 - j_par) + 1)
                    down(c + 2, j_par, n, first, False)
                group(c0 + 2, 0, h0 + 1, True)
                group(c0 + 5, 1, h0 + 2, False)
                with pe.Fori(0, (FF_GROUPS - 3) // 2) as i:
                    for p in range(2):
                        group((c0 + (8 + 3 * p)).plus(i, 6), p, (h0 + (3 + p)).plus(i, 2), False)
                down(c0 + (FF_CHUNKS - 1), 0, h0 + FF_GROUPS, False, True)

            def mixer(l, c0):
                lay = N(0, (l, 1))
                projection(c0 + C_MIX_IN, IN_GROUPS, IN_COLS, N(9, (l, IN_GROUPS)))
                pe.wait_ge(mx["dup"], (lay + 1).v)
                for i in range(10):
                    if i >= 4:
                        pe.wait_ge(mx["qkta" if i % 2 == 0 else "qktd"], (lay.times(5) + ((i - 4) // 2 + 1)).v)
                    for kk in range(2):
                        ch = 2 * i + kk
                        for b in range(TB):
                            last = t.transpose(W[:, i % 4, kk * SEQ + b * P:kk * SEQ + (b + 1) * P], QK[:, b, ch * P:(ch + 1) * P], ident[:])
                    last.then_inc(mx["qkt"], 1)
                pe.wait_ge(mx["qkta"], (lay + 1).times(5).v)
                pe.wait_ge(mx["qktd"], (lay + 1).times(5).v)

                def rows(ch, r, tok):
                    return QKT[r * HD:(r + 1) * HD, ch, tok]

                for b in range(TB):
                    n = P * (b + 1)
                    for h in range(8):
                        i = 4 * (h % 2) + h // 2
                        k, o = (i * n) // 512, (i * n) % 512
                        last = t.matmul((acc, W)[b][:, k, o:o + n], rows(3 + h // 2, h % 2, slice(b * P, (b + 1) * P)),
                                        rows(7, h % 2, slice(0, n)), start=True, stop=True)
                    last.then_inc(mx["is"], 1)
                pe.wait_ge(mx["relu"], (lay + 1).times(2).v)
                pe.wait_ge(mx["nlf"], (lay + 1).v)

                def scores(u):
                    b, grp = u // 4, u % 4
                    if u >= 2:
                        pe.wait_ge(mx["sb"], (lay.times(8) + (u - 1)).v)
                    for h in range(4):
                        n = P * (b + 1)
                        k, o = 2 * (u % 2) + h % 2, (h // 2) * n
                        hh = 4 * (grp - 2) + h
                        q, kk = ((h // 2, 2), (8 + h // 2, 10 + h // 2), (12 + hh // 2, 16 + hh // 2), (12 + hh // 2, 16 + hh // 2))[grp]
                        last = t.matmul(W[:, k, o:o + n], rows(q, h % 2, slice(b * P, (b + 1) * P)), rows(kk, h % 2, slice(0, n)),
                                        start=True, stop=(grp < 2))
                        if grp >= 2:
                            for sb in range(b + 1):
                                w = n - P * sb
                                last = t.matmul(W[:, k, o + P * sb:o + n], nlf[:, sb, hh:hh + 1].to_broadcast([P, P]), tri[:, 0:w],
                                                start=False, stop=(sb == b))
                    last.then_inc(mx["s"], 1)

                scores(0)
                for u in range(8):
                    b, grp = u // 4, u % 4
                    if u < 7:
                        scores(u + 1)
                    pe.wait_ge(mx["p"], (lay.times(8) + (u + 1)).v)
                    n = P * (b + 1)
                    for h in range(4):
                        for kb in range(b + 1):
                            o = h * n + kb * P
                            last = t.transpose(acc[:, o // 512, o % 512:o % 512 + P], Sb[:, u % 2, h, kb * P:(kb + 1) * P], ident[:])
                    last.then_inc(mx["t"], 1)
                    pe.wait_ge(mx["te"], (lay.times(8) + (u + 1)).v)
                    if u >= 2:
                        pe.wait_ge(mx["at"], (lay.times(8) + (u - 1)).v)
                    for i in range(4):
                        h = 2 * (i % 2) + i // 2
                        hh = 4 * (grp - 2) + h
                        col = (AV, BV + HD * h, CV + HD * hh, CV + HD * hh)[grp]
                        for kb in range(b + 1):
                            last = t.matmul(acc[:, 2 + u % 2, i * HD:(i + 1) * HD], PT[:, i, kb * P:(kb + 1) * P], proj[:, kb, col:col + HD],
                                            start=(kb == 0), stop=(kb == b))
                    last.then_inc(mx["o"], 1)
                transposes(N(6, (l, 4)), attn, ((mx["at"], (lay + 1).times(8).v), (mx["cg"], (lay + 1).v)))
                wait_xT(N(6, (l, 4)))
                out_projection(c0 + C_MIX_OUT)

            with pe.Fori(0, DEPTH) as l:
                c0 = N(C_LAYERS).plus(l, LAYER_CHUNKS)

                def norm(call):
                    transposes(N(4 + call, (l, 4)), xn, ((rm["xa"], N(min(call, 2) + 1, (l, 3)).v), (rm["xd"], N(min(call, 2) + 1, (l, 3)).v)))
                    wait_xT(N(4 + call, (l, 4)))

                norm(0)
                ffn(c0 + C_FFN1, N(0, (l, 2 * FF_GROUPS)))
                norm(1)
                mixer(l, c0)
                norm(3)
                ffn(c0 + C_FFN2, N(FF_GROUPS, (l, 2 * FF_GROUPS)))


SMALL_LOADS = 5 + sum(len(names) for names in VEC_SETS)

_OUT = (1, SEQ, D)


def kernel(**inputs):
    import numpy as np
    import concourse.bacc as bacc
    from concourse.bass_utils import run_bass_kernel_spmd

    nc = bacc.Bacc("TRN2", target_bir_lowering=False, num_devices=1)
    cos, sin = rope_tables()
    arrays, A = {}, {}
    for name, a in {**inputs, "rope_cos": cos, "rope_sin": sin}.items():
        a = np.ascontiguousarray(a)
        arrays[f"in_{name}"] = a
        A[name] = nc.dram_tensor(f"in_{name}", a.shape, mybir.dt.from_np(a.dtype), kind="ExternalInput").ap()
    out = nc.dram_tensor("out", _OUT, F32, kind="ExternalOutput").ap()
    build_program(nc, A, out)
    r = run_bass_kernel_spmd(nc, [arrays], core_ids=[0])
    return r.results[0]["out"]
```

```python
from contextlib import ExitStack

import concourse.bass as bass
from concourse import mybir

ALU = mybir.AluOpType
ACT = mybir.ActivationFunctionType
AX = mybir.AxisListType.X
F32 = mybir.dt.float32
F32R = mybir.dt.float32r
I32 = mybir.dt.int32

P = 128
SEQ = 256
TB = SEQ // P
D = 1024
KC = D // P
SLOT = 2048
RAW_SLOTS = 6
SPLIT_SLOTS = 3
AHEAD = 3

DEPTH = 2
ALPHA = (2.0 * DEPTH) ** 0.25
LN_EPS = 1e-5
RMS_EPS = 1e-6

D_A = 512
CONV_A = 31
CONV_B = 3
EVEN_IN = 2560
CONV_C = 4
LRU_C = 8.0
RNN_HEADS = 4
EVEN_ORDER = (4, 5, 6, 7, 0, 1, 2, 3)

NE = 16
NG = 4
EPG = NE // NG
CAP = 64
ROUNDS = SEQ // CAP
TURN_BANK = (1, 3)
MOE_CHUNKS = 12

D_FF = 2816
FF_COLS = 256
FF_GROUPS = D_FF // FF_COLS
FF_CHUNKS = 3 * FF_GROUPS

X_LAYERS = 5
HD = 64
IN_WIDTH = 3792
IN_COLS = 474
IN_GROUPS = IN_WIDTH // IN_COLS
AQ, AK, AV, IQ, IK, IW, BQ, BK, BV, CQ, CK, CV, CF, CG = (
    0, 256, 320, 384, 896, 960, 968, 1224, 1480, 1736, 2248, 2760, 3272, 3280)
NORM_REGIONS = ((AQ, 5), (BQ, 8), (CQ, 16))
NORM_FIRST = (0, 5, 13)
NORM_GROUP = tuple((at + n * HD - 1) // IN_COLS for at, n in NORM_REGIONS)
INDEX_GROUP = (BQ - 1) // IN_COLS
NORM_HEADS = 29
DSA_TOPK = 64
DSA_IDX_SCALE = (8 ** -0.5) * (64 ** -0.5)
QK_SCALE = HD ** -0.5
BIG = 1e30
REPLACED = -3e38
C_HEADS = 8
UNITS = ((0, 1), (0, 2), (0, 3), (1, 1), (1, 2), (1, 3), (0, 0), (1, 0))

C_EVEN_IN = 0
C_EVEN_OUT = C_EVEN_IN + 2 * (EVEN_IN // 512)
C_MOE0 = C_EVEN_OUT + KC
C_ODD_IN = C_MOE0 + NE * MOE_CHUNKS
C_GATES = C_ODD_IN + 2 * (2 * D // 512)
C_ODD_OUT = C_GATES + 2
C_MOE1 = C_ODD_OUT + KC
C_LAYERS = C_MOE1 + NE * MOE_CHUNKS
C_FFN1 = 0
C_MIX_IN = C_FFN1 + FF_CHUNKS
C_MIX_OUT = C_MIX_IN + 2 * IN_GROUPS
C_FFN2 = C_MIX_OUT + KC
LAYER_CHUNKS = C_FFN2 + FF_CHUNKS

VEC_SETS = (
    (("even_a_dw", 124),),
    (("even_a_dw_b", 4), ("even_a_ln_g", 4), ("even_a_ln_b", 4), ("even_b_dw", 12),
     ("odd_c_dw", 32), ("odd_c_dw_b", 8), ("odd_b_gate_a", 8), ("odd_b_gate_x", 8), ("odd_lam", 8)),
    (("ffn1_norm_2", 16), ("mix_norm_2", 16), ("ffn2_norm_2", 16)),
)
VEC_AT = {}
_at = 0
for _set in VEC_SETS:
    for _name, _rows in _set:
        VEC_AT[_name] = _at
        _at += _rows
VEC_COLS = _at


class N:

    def __init__(self, base, *terms):
        self.base, self.terms = base, terms

    def __add__(self, n):
        return N(self.base + n, *self.terms)

    def __sub__(self, n):
        return self + (-n)

    def times(self, m):
        return N(self.base * m, *[(r, k * m) for r, k in self.terms])

    def plus(self, reg, k):
        if isinstance(reg, int):
            return self + reg * k
        return N(self.base, *self.terms, (reg, k))

    @property
    def v(self):
        out = self.base
        for r, k in self.terms:
            out = r * k + out
        return out


def rope_tables():
    import numpy as np

    inv = (1.0 / (10000.0 ** (np.arange(0, HD, 2, dtype=np.float32) / np.float32(HD)))).astype(np.float32)
    ang = np.arange(SEQ, dtype=np.float32)[:, None] * inv[None, :]
    cos, sin = np.cos(ang).astype(np.float32), np.sin(ang).astype(np.float32)
    return np.concatenate([cos, cos], 1), np.concatenate([-sin, sin], 1)


def build_program(nc, A, out):
    ctx = ExitStack()
    with ctx:
        base = (nc.sbuf_base + 63) // 64 * 64
        place = [base]

        def at(name, shape, dt=F32):
            cols = 1
            for s in shape[1:]:
                cols *= s
            t = nc.alloc_sbuf_tensor_at(name, shape, dt, offset=place[0])
            place[0] += (cols * 4 + 31) // 32 * 32
            assert place[0] <= nc.sbuf_usable_end, name
            return t

        def sem(name):
            return ctx.enter_context(nc.semaphore(name))

        raw = [at(f"raw{i}", [P, SLOT]) for i in range(RAW_SLOTS)]
        w_hi = [at(f"w_hi{i}", [P, SLOT], F32R) for i in range(SPLIT_SLOTS)]
        w_lo = [at(f"w_lo{i}", [P, SLOT], F32R) for i in range(SPLIT_SLOTS)]
        x = at("x", [P, TB, D])
        xT_hi = at("xT_hi", [P, KC, SEQ], F32R)
        xT_lo = at("xT_lo", [P, KC, SEQ], F32R)
        ident = at("ident", [P, P])
        tri = at("tri", [P, 2 * P])
        tri_strict = at("tri_strict", [P, P])
        slot_ids = at("slot_ids", [P, ROUNDS, P])
        earlier = at("earlier", [P, 4, 4])
        causal = at("causal", [P, TB, SEQ])
        ropeC = at("ropeC", [P, TB, HD])
        ropeS = at("ropeS", [P, TB, HD])
        vecs = at("vecs", [P, VEC_COLS])
        br = at("br", [P, NE])
        wr = at("wr", [P, KC, NE])
        wr_hi = at("wr_hi", [P, KC, NE], F32R)
        wr_lo = at("wr_lo", [P, KC, NE], F32R)
        zeros = at("zeros", [P, P], F32R)
        lneps = at("lneps", [P, 1])
        rmeps = at("rmeps", [P, 1])
        onec = at("onec", [P, 1])
        stats = at("stats", [P, TB, 2, 6])
        mv = at("mv", [P, TB, 2])
        std = at("std", [P, TB])
        rstd = at("rstd", [P, TB])
        nmr = at("nmr", [P, TB])
        sp8 = at("sp8", [P, 8])
        spt = at("spt", [P, 4, 8])
        head_gain = at("head_gain", [P, 6, HD])
        fb = at("fb", [P, C_HEADS])
        count_i = at("count_i", [P, 1], I32)
        region = place[0]

        lng = at("lng", [P, D])
        lnb = at("lnb", [P, D])
        region1 = place[0]

        place[0] = region1
        u_even = at("u_even", [P, TB, EVEN_IN])
        aT = at("aT", [P, 4, CONV_A - 1 + SEQ])
        bxT = at("bxT", [P, 4, CONV_B - 1 + SEQ])
        bbT = at("bbT", [P, 4, SEQ])
        ca = at("ca", [P, 4, SEQ])
        cb = at("cb", [P, 4, SEQ])
        an = at("an", [P, TB, D_A])
        a2 = at("a2", [P, 4, SEQ])
        taps = at("taps", [P, 4, 2, SEQ])
        vrows = [at(f"vrows{i}", [P, P]) for i in range(len(VEC_SETS))]

        place[0] = region1
        u_odd = at("u_odd", [P, TB, 2 * D])
        place[0] = region1
        lru_a = at("lru_a", [P, KC, SEQ])
        lru_t = at("lru_t", [P, KC, SEQ])
        xrT = at("xrT", [P, KC, CONV_C - 1 + SEQ])
        yT = at("yT", [P, KC, SEQ])
        xc = at("xc", [P, KC, SEQ])
        lru_r = at("lru_r", [P, KC, SEQ])
        lru_i = at("lru_i", [P, KC, SEQ])

        place[0] = region1
        xe = at("xe", [P, KC, 2 * CAP], F32R)
        pick = at("pick", [P, TB, P])
        pickT = at("pickT", [P, SEQ], F32R)
        gslot = at("gslot", [P, 1])
        gb = at("gb", [CAP, 2, 512])
        ub = at("ub", [CAP, 2, 512])
        heT = at("heT", [P, KC, 2 * CAP], F32R)
        Y_hi = at("Y_hi", [P, D], F32R)
        Y_lo = at("Y_lo", [P, D], F32R)
        logitsT = at("logitsT", [NE, SEQ])
        prob = at("prob", [P, TB, NE])
        rmax = at("rmax", [P, TB])
        rsum = at("rsum", [P, TB])
        cmp = at("cmp", [P, TB * NG, 4, 4])
        cmp2 = at("cmp2", [P, TB * NG, 4, 4])
        rank = at("rank", [P, TB, NE])
        top2 = at("top2", [P, TB, NE])
        gscore = at("gscore", [P, TB, NG])
        grank = at("grank", [P, TB, NG])
        gcmp = at("gcmp", [P, TB, NG, NG])
        gcmp2 = at("gcmp2", [P, TB, NG, NG])
        chosen = at("chosen", [P, TB, NE])
        pos = at("pos", [P, TB, NE])
        gate = at("gate", [P, TB, NE])
        count_max = at("count_max", [P, 1])
        ov_raw = at("ov_raw", [P, D])
        ov_hi = at("ov_hi", [P, D], F32R)
        ov_lo = at("ov_lo", [P, D], F32R)

        place[0] = region
        xn = at("xn", [P, TB, D])
        sg = at("sg", [P, 2, 512])
        hb = at("hb", [P, 512])
        hT_hi = at("hT_hi", [P, 2, 2, SEQ], F32R)
        hT_lo = at("hT_lo", [P, 2, 2, SEQ], F32R)
        place[0] = region
        proj = at("proj", [P, TB, IN_WIDTH])
        QKT = at("QKT", [P, 20, SEQ])
        after_qkt = place[0]
        QK = at("QK", [P, TB, 2560])
        hsum = at("hsum", [P, TB, NORM_HEADS])
        hrs = at("hrs", [P, TB, NORM_HEADS])
        lf = at("lf", [P, TB, C_HEADS])
        lft = at("lft", [P, TB, C_HEADS])
        iws = at("iws", [P, TB, 8])
        top8 = at("top8", [P, TB, 8, 8])
        amax = at("amax", [P, 8, 4])
        asum = at("asum", [P, 8, 4])
        nlf = at("nlf", [P, TB, C_HEADS])
        after_mix = place[0]
        place[0] = after_qkt
        attn = at("attn", [P, TB, D])
        Sb = at("Sb", [P, 2, 4, SEQ])
        PT = at("PT", [P, 4, SEQ])
        place[0] = after_qkt
        relu = at("relu", [P, 8, SEQ])
        place[0] = after_mix
        dsa_bias = at("dsa_bias", [P, TB, SEQ])
        score = at("score", [P, TB, SEQ])
        QKT_BYTES = 20 * SEQ * 4
        sq = nc.alloc_sbuf_tensor_at("sq", [P, TB, 16 * HD], F32, offset=after_qkt - QKT_BYTES)
        rt_d = nc.alloc_sbuf_tensor_at("rt_d", [P, TB, 9 * HD], F32, offset=after_qkt - QKT_BYTES + 8192)
        rt_p = nc.alloc_sbuf_tensor_at("rt_p", [P, TB, 9 * HD], F32, offset=after_qkt - QKT_BYTES + 12800)

        acc = ctx.enter_context(nc.psum_tensor("acc", [P, 4, 512], F32))
        W = ctx.enter_context(nc.psum_tensor("W", [P, 4, 512], F32))

        landed = [sem(f"landed{i}") for i in range(RAW_SLOTS)]
        hi_ready = sem("hi_ready")
        lo_ready = sem("lo_ready")
        used = sem("used")
        x_in = sem("x_in")
        small_in = sem("small_in")
        consts = sem("consts")
        vec_ps = sem("vec_ps")
        vecs_ok = sem("vecs_ok")
        wr_ok = sem("wr_ok")
        xt_ps, xt_hi_s, xt_lo_s = sem("xt_ps"), sem("xt_hi_s"), sem("xt_lo_s")
        tm_act, tm_dve = sem("tm_act"), sem("tm_dve")
        ln_in = sem("ln_in")
        ln_mv, ln_std, ln_rs = sem("ln_mv"), sem("ln_std"), sem("ln_rs")
        ln_x1a, ln_x0, ln_x1 = sem("ln_x1a"), sem("ln_x0"), sem("ln_x1")
        x_ready = sem("x_ready")
        ev = {n: sem("ev_" + n) for n in ("pad", "sig", "a", "bx", "tp", "tr", "product", "summed", "conv", "back", "mv", "std", "an", "an_ps", "silu", "done")}
        od = {n: sem("od_" + n) for n in ("pad", "tp", "tr", "xc", "hi", "lo", "gates", "ri", "nla", "exp", "m2", "sqrt", "h", "out_hi", "done", "sp", "sp2")}
        rt = {n: sem("rt_" + n) for n in ("logitsT", "logits_sb", "logits", "max", "exp", "chosen", "ranks", "ready")}
        me = {n: sem("me_" + n) for n in ("pick", "ga", "xh", "xe", "pt", "pte", "gb", "g", "sg", "ub", "h", "tr", "hh", "hT", "yh", "y", "sc")}
        rm = {n: sem("rm_" + n) for n in ("ssa", "ssd", "std", "rs", "xa", "xd")}
        ff = {n: sem("ff_" + n) for n in ("sg", "h", "hT")}
        mx = {n: sem("mx_" + n) for n in ("in", "sq", "ss", "std", "qkp", "qkd", "dup", "qkt", "qkta", "qktd", "is", "relu",
                                          "z", "ln", "nlf", "s", "sb", "p", "t", "te", "o", "at", "cg", "ib")}
        ov = [{n: sem(f"ov{i}_" + n) for n in ("landed", "hi", "lo", "free", "tensor", "scalar", "vector")} for i in range(DEPTH)]
        stored = sem("stored")

        block = ctx.enter_context(nc.Block())

        def slot_of(c):
            return c.base % RAW_SLOTS

        def split_slot(c):
            return c.base % SPLIT_SLOTS

        def landed_count(c):
            return N(16 * (c.base // RAW_SLOTS + 1), *[(r, 16 * (k // RAW_SLOTS)) for r, k in c.terms])

        OV_STEPS = {"tensor": ("gathered", "turned", "hidden_turned", "added"),
                    "scalar": ("tokens_hi", "choice", "lower_halves", "gated", "hidden_hi", "out_hi"),
                    "vector": ("pick", "tokens_lo", "gate_sum", "hidden", "hidden_lo", "out_lo")}

        def ov_done(o, step, k):
            engine = next(n for n, steps in OV_STEPS.items() if step in steps)
            steps = OV_STEPS[engine]
            return o[engine], (k.times(len(steps)) + (steps.index(step) + 1)).v

        def crowded(eng, layer, later=0):
            eng.wait_ge(rt["ready"], layer + 1)
            return eng.If(eng.value_load(count_i[0:1, 0:1], min_val=0, max_val=SEQ) > later * SEQ + CAP)

        def vec(name, i):
            return vecs[:, VEC_AT[name] + i:VEC_AT[name] + i + 1]

        def rotate(eng, src_at, dst_at, heads, scratch):
            w = heads * HD
            src = proj[:, :, src_at:src_at + w].rearrange("p b (h d) -> p b h d", d=HD)
            dst = QK[:, :, dst_at:dst_at + w].rearrange("p b (h d) -> p b h d", d=HD)
            tmp = scratch[:, :, 0:w].rearrange("p b (h d) -> p b h d", d=HD)
            for b in range(TB):
                eng.tensor_tensor(dst[:, b], src[:, b], ropeC[:, b:b + 1, :].to_broadcast([P, heads, HD]), ALU.mult)
                for lo, hi in ((0, 32), (32, 0)):
                    sin = ropeS[:, b:b + 1, lo:lo + 32].to_broadcast([P, heads, 32])
                    eng.tensor_tensor(tmp[:, b, :, lo:lo + 32], src[:, b, :, hi:hi + 32], sin, ALU.mult)
            eng.drain()
            flat = QK[:, :, dst_at:dst_at + w]
            eng.tensor_tensor(flat, flat, scratch[:, :, 0:w], ALU.add)

        @block.sync
        def _(sp):
            def load(c, src, shape):
                if c.terms or c.base >= RAW_SLOTS:
                    sp.wait_ge(lo_ready, (c - (RAW_SLOTS - 1)).v)
                k, n = shape
                dst = raw[slot_of(c)][:, 0:k * n].rearrange("p (k n) -> p k n", k=k)
                sp.dma_start(dst, src).then_inc(landed[slot_of(c)], 16)

            def rows(w, r0, k, c0, n):
                return w[r0:r0 + k * P, c0:c0 + n].rearrange("(k p) n -> p k n", p=P)

            def projection(c0, w, groups, n, first=0):
                for j in range(first, groups):
                    for half in range(2):
                        load(c0 + (2 * j + half), rows(w, 512 * half, 4, n * j, n), (4, n))

            def out_projection(c0, w, order=range(KC)):
                for i, k in enumerate(order):
                    load(c0 + i, rows(w, k * P, 1, 0, D), (1, D))

            def moe(layer, c0):
                def weights(e, ahead=0):
                    return [A[name][layer, ahead:][bass.ds(e, 1)].rearrange("a k n -> (a k) n") for name in ("moe_w1", "moe_w3", "moe_w2")]

                def half_columns(c, w, n):
                    for half in range(2):
                        load(c + half, rows(w, 512 * half, 4, 512 * (1 - n), 512), (4, 512))

                def down(c, w2, half):
                    for k in range(2):
                        load(c + k, rows(w2, 512 * (1 - half) + 256 * k, 2, 0, D), (2, D))

                def expert(e, c, last):
                    w1, w3, w2 = weights(e)
                    half_columns(c, w1, 1)
                    half_columns(c + 2, w3, 1)
                    down(c + 4, w2, 0)
                    if last:
                        down(c + 6, w2, 1)
                    else:
                        half_columns(c + 6, weights(e, 1)[0], 0)
                        down(c + 8, w2, 1)
                        half_columns(c + 10, weights(e, 1)[1], 0)

                half_columns(N(c0), weights(0)[0], 0)
                half_columns(N(c0 + 2), weights(0)[1], 0)
                with sp.Fori(0, NE - 1) as e:
                    expert(e, N(c0 + 4).plus(e, MOE_CHUNKS), False)
                expert(NE - 1, N(c0 + 4 + MOE_CHUNKS * (NE - 1)), True)

            def more_rounds(layer, crowd):
                o = ov[layer]
                with crowd:
                    with sp.Fori(0, ROUNDS - 1) as r:
                        with sp.Fori(0, NE) as e:
                            for i, name in enumerate(("moe_w1", "moe_w3", "moe_w2")):
                                w = A[name][layer, bass.ds(e, 1)].rearrange("a k n -> (a k) n")
                                for kc in range(KC):
                                    sp.wait_ge(o["free"], N(KC * i + kc + 1, (r, 24 * NE), (e, 24)).v)
                                    sp.dma_start(ov_raw[:], w[kc * P:(kc + 1) * P, :]).then_inc(o["landed"], 16)

            def ffn(c0, l, which):
                wg = A[f"ffn{which}_w_gate_2"][bass.ds(l, 1)].rearrange("a k n -> (a k) n")
                wu = A[f"ffn{which}_w_up_2"][bass.ds(l, 1)].rearrange("a k n -> (a k) n")
                wd = A[f"ffn{which}_w_down_2"][bass.ds(l, 1)].rearrange("a k n -> (a k) n")

                def up(w, c, j):
                    src = w[:, bass.ds(j * FF_COLS, FF_COLS)].rearrange("(k p) n -> p k n", p=P)
                    load(c, src, (KC, FF_COLS))

                def down(c, j):
                    src = wd[bass.ds(j * FF_COLS, FF_COLS), :].rearrange("(k p) n -> p k n", p=P)
                    load(c, src, (2, D))

                up(wg, c0, 0)
                up(wu, c0 + 1, 0)
                for j in range(2):
                    c = c0 + (2 + 3 * j)
                    up(wg, c, j + 1)
                    up(wu, c + 1, j + 1)
                    down(c + 2, j)
                    if j == 0 and which == 1:
                        more_rounds(1, crowded(sp, 1, l))
                with sp.Fori(1, (FF_GROUPS - 1) // 2) as i:
                    for t in range(2):
                        c = (c0 + (2 + 3 * t)).plus(i, 6)
                        up(wg, c, i * 2 + (t + 1))
                        up(wu, c + 1, i * 2 + (t + 1))
                        down(c + 2, i * 2 + t)
                down(c0 + (FF_CHUNKS - 1), FF_GROUPS - 1)

            sp.dma_start(x[:], A["x"].rearrange("a (b p) d -> p (a b) d", p=P)).then_inc(x_in, 16)
            projection(N(C_EVEN_IN), A["even_w_in"][0], EVEN_IN // 512, 512)
            out_projection(N(C_EVEN_OUT), A["even_w_out"][0], EVEN_ORDER)
            moe(0, C_MOE0)
            projection(N(C_ODD_IN), A["odd_w_in"][0], 3, 512)
            more_rounds(0, crowded(sp, 0))
            projection(N(C_ODD_IN), A["odd_w_in"][0], 2 * D // 512, 512, 3)
            for i, name in enumerate(("odd_w_gate_a", "odd_w_gate_x")):
                src = A[name].rearrange("a h (c p) j -> p (a h c) j", p=P)
                load(N(C_GATES + i), src, (8, 256))
            out_projection(N(C_ODD_OUT), A["odd_w_out"][0])
            moe(1, C_MOE1)
            with sp.Fori(0, DEPTH) as l:
                c0 = N(C_LAYERS).plus(l, LAYER_CHUNKS)
                ffn(c0 + C_FFN1, l, 1)
                w_in = A["w_in_2"][bass.ds(l, 1)].rearrange("a k n -> (a k) n")
                w_out = A["w_out_2"][bass.ds(l, 1)].rearrange("a k n -> (a k) n")
                projection(c0 + C_MIX_IN, w_in, IN_GROUPS, IN_COLS)
                out_projection(c0 + C_MIX_OUT, w_out)
                ffn(c0 + C_FFN2, l, 2)
            sp.wait_ge(x_ready, X_LAYERS + 3 * DEPTH)
            sp.dma_start(out.rearrange("a (b p) d -> p (a b) d", p=P), x[:]).then_inc(stored, 16)
            sp.wait_ge(stored, 16)

        @block.gpsimd
        def _(pool):
            g = nc.gpsimd
            def load_ln(i):
                which, layer = 1 + i % 2, i // 2
                pool.dma_start(lng[:], A[f"ln{which}_g"][layer].partition_broadcast(P)).then_inc(ln_in, 16)
                pool.dma_start(lnb[:], A[f"ln{which}_b"][layer].partition_broadcast(P)).then_inc(ln_in, 16)

            load_ln(0)
            g.memset(ident[:], 0.0)
            g.memset(tri[:], 1.0)
            g.memset(tri_strict[:], 1.0)
            g.memset(earlier[:], 1.0)
            g.memset(causal[:], 0.0)
            g.iota(slot_ids[:].rearrange("p r (h s) -> p r h s", h=2), [[CAP, ROUNDS], [0, 2], [1, CAP]], base=0,
                   channel_multiplier=0, allow_small_or_imprecise_dtypes=True)
            g.drain()
            g.affine_select(ident[:], ident[:], [[-1, P]], ALU.not_equal, 1.0, base=0, channel_multiplier=1)
            g.affine_select(tri[:, 0:P], tri[:, 0:P], [[1, P]], ALU.is_ge, 0.0, base=0, channel_multiplier=-1)
            g.affine_select(tri_strict[:], tri_strict[:], [[1, P]], ALU.is_gt, 0.0, base=0, channel_multiplier=-1)
            g.affine_select(earlier[:], earlier[:], [[1, 4], [-1, 4]], ALU.is_gt, 0.0, base=0, channel_multiplier=0)
            for b in range(TB):
                g.affine_select(causal[:, b, :], causal[:, b, :], [[-1, SEQ]], ALU.is_ge, -BIG, base=b * P,
                                channel_multiplier=1)
            g.drain().then_inc(consts, 1)

            def layer_norm(i):
                pool.wait_ge(ln_x1a, i + 1)
                pool.wait_ge(ln_in, 32 * (i + 1))
                g.tensor_tensor(x[:, 1, 0:512], x[:, 1, 0:512], lng[:, 0:512], ALU.mult)
                g.drain()
                g.tensor_tensor(x[:, 1, 0:512], x[:, 1, 0:512], lnb[:, 0:512], ALU.add)
                g.drain().then_inc(ln_x1, 1)
                if i + 1 < 2 * DEPTH:
                    pool.wait_ge(x_ready, i + 2)
                    load_ln(i + 1)

            pool.wait_ge(tm_act, EVEN_IN // 512)
            pool.wait_ge(tm_dve, EVEN_IN // 512)
            g.tensor_tensor(u_even[:, :, 1536:2048], u_even[:, :, 1536:2048], u_even[:, :, 2048:2560],
                            ALU.mult).then_inc(ev["bx"], 1)
            layer_norm(0)
            layer_norm(1)
            layer_norm(2)
            layer_norm(3)

            with pool.Fori(0, DEPTH) as l:
                pool.wait_ge(x_ready, (N(X_LAYERS - 1, (l, 3))).v)
                for i, name in enumerate(("a_q_norm_2", "a_k_norm_2", "b_q_norm_2", "b_k_norm_2", "c_q_norm_2", "c_k_norm_2")):
                    src = A[name][bass.ds(l, 1)].rearrange("a d -> (a d)").partition_broadcast(P)
                    pool.dma_start(head_gain[:, i, :], src).then_inc(mx["in"], 16)
                src = A["forget_bias_2"][bass.ds(l, 1)].rearrange("a d -> (a d)").partition_broadcast(P)
                pool.dma_start(fb[:], src).then_inc(mx["in"], 16)
                pool.wait_ge(tm_act, (N(9 + INDEX_GROUP + 1, (l, IN_GROUPS))).v)
                pool.wait_ge(tm_dve, (N(9 + INDEX_GROUP + 1, (l, IN_GROUPS))).v)
                rotate(g, IQ, 384, 9, rt_p)
                g.drain().then_inc(mx["qkp"], 1)

        @block.scalar
        def _(act):
            s = nc.scalar

            def split(c, cols=SLOT):
                act.wait_ge(landed[slot_of(c)], landed_count(c).v)
                if c.terms or c.base >= SPLIT_SLOTS:
                    act.wait_ge(used, (c - (SPLIT_SLOTS - 1)).v)
                s.activation(w_hi[split_slot(c)][:, 0:cols], raw[slot_of(c)][:, 0:cols], ACT.Copy).then_inc(hi_ready, 1)

            def transposed(call, gain=None):
                for q in range(4):
                    act.wait_ge(xt_ps, (call.times(4) + (q + 1)).v)
                    if gain is None:
                        last = s.activation(xT_hi[:, 2 * q:2 * q + 2, :].rearrange("p a t -> p (a t)"), W[:, q, :], ACT.Copy)
                    else:
                        for kk in range(2):
                            last = s.activation(xT_hi[:, 2 * q + kk, :], W[:, q, kk * SEQ:(kk + 1) * SEQ], ACT.Copy,
                                                scale=gain(2 * q + kk))
                    last.then_inc(xt_hi_s, 1)

            def projection(c0, dst, groups, n):
                for j in range(groups):
                    split(c0 + (2 * j + AHEAD), n_after(c0 + (2 * j + AHEAD)))
                    act.wait_ge(used, (c0 + (2 * j + 2)).v)
                    s.activation(dst[:, 0, n * j:n * (j + 1)], W[:, (2 * j) % 4, 0:n], ACT.Copy).then_inc(tm_act, 1)
                    split(c0 + (2 * j + 1 + AHEAD), n_after(c0 + (2 * j + 1 + AHEAD)))

            def n_after(c):
                i = c.base
                if not c.terms:
                    for a in (C_EVEN_OUT, C_ODD_OUT):
                        if a <= i < a + KC:
                            return D
                return SLOT

            def layer_norm(i):
                act.wait_ge(ln_mv, i + 1)
                s.activation(std[:], mv[:, :, 1], ACT.Sqrt, bias=lneps[:]).then_inc(ln_std, 1)
                act.wait_ge(ln_rs, i + 1)
                s.activation(x[:, 1, :], x[:, 1, :], ACT.Identity, bias=nmr[:, 1:2], scale=rstd[:, 1:2]).then_inc(ln_x1a, 1)

            for i, names in enumerate(VEC_SETS):
                r = 0
                for name, n in names:
                    a = A[name]
                    dims = "abcd"[:len(a.shape)]
                    flat = a.rearrange(f"{' '.join(dims)} -> ({' '.join(dims)})")
                    src = flat.rearrange("(r c) -> r c", c=P)
                    act.dma_start(vrows[i][r:r + n, :], src).then_inc(small_in, 16)
                    r += n
            act.dma_start(wr[:], A["w_router"].rearrange("(k p) e -> p k e", p=P)).then_inc(small_in, 16)
            act.dma_start(br[:], A["b_router"].partition_broadcast(P)).then_inc(small_in, 16)
            act.dma_start(ropeC[:], A["rope_cos"].rearrange("(b p) d -> p b d", p=P)).then_inc(small_in, 16)
            act.dma_start(ropeS[:], A["rope_sin"].rearrange("(b p) d -> p b d", p=P)).then_inc(small_in, 16)
            for c in range(AHEAD):
                split(N(c))
            transposed(N(0))
            projection(N(C_EVEN_IN), u_even, EVEN_IN // 512, 512)
            for i, names in enumerate(VEC_SETS):
                n = sum(r for _, r in names)
                c0 = VEC_AT[names[0][0]]
                act.wait_ge(vec_ps, 1)
                last = s.activation(vecs[:, c0:c0 + n], acc[:, 1 + i, 0:n], ACT.Copy)
            last.then_inc(vecs_ok, 1)

            act.wait_ge(tm_dve, EVEN_IN // 512)
            act.drain()
            s.activation(u_even[:, :, 512:1024], u_even[:, :, 512:1024], ACT.Sigmoid).then_inc(ev["sig"], 1)
            act.wait_ge(ev["pad"], 1)
            for i in range(6):
                act.wait_ge(ev["tp"], i + 1)
                for kk in range(2):
                    c = 2 * i + kk
                    src = W[:, i % 4, kk * SEQ:(kk + 1) * SEQ]
                    dst = (aT[:, c % 4, CONV_A - 1:], bxT[:, c % 4, CONV_B - 1:], bbT[:, c % 4, :])[c // 4]
                    last = s.activation(dst, src, ACT.Copy)
                last.then_inc(ev["tr"], 1)
            act.drain()
            for k in range(CONV_A):
                if k >= 4:
                    act.wait_ge(ev["summed"], k - 3)
                for c in (2, 3):
                    last = s.activation(taps[:, k % 4, c - 2, :], aT[:, c, k:k + SEQ], ACT.Copy, scale=vec("even_a_dw", 4 * k + c))
                last.then_inc(ev["product"], 1)
            act.wait_ge(ev["summed"], CONV_A)
            for c in (2, 3):
                last = s.activation(ca[:, c, :], acc[:, 0, (c - 2) * SEQ:(c - 1) * SEQ], ACT.Identity, bias=vec("even_a_dw_b", c))
            last.then_inc(ev["conv"], 1)
            act.wait_ge(ev["mv"], 1)
            s.activation(std[:], mv[:, :, 1], ACT.Sqrt, bias=lneps[:]).then_inc(ev["std"], 1)
            for i in range(2):
                if i == 0:
                    split(N(C_EVEN_OUT + AHEAD), D)
                act.wait_ge(ev["an_ps"], i + 1)
                for kk in range(2):
                    c = 2 * i + kk
                    last = s.activation(a2[:, c, :], W[:, 2 + i, kk * SEQ:(kk + 1) * SEQ], ACT.Silu,
                                        bias=vec("even_a_ln_b", c), scale=vec("even_a_ln_g", c))
            act.drain()
            s.activation(xT_hi[:, 0:4, :], a2[:], ACT.Copy).then_inc(ev["silu"], 1)

            def out_projection(c0):
                for k in range(KC):
                    split(c0 + (k + AHEAD), n_after(c0 + (k + AHEAD)) if k + AHEAD < KC else SLOT)

            def tail(c0, first=0):
                for k in range(first, KC):
                    split(c0 + (k + AHEAD), D if k + AHEAD < KC else SLOT)

            tail(N(C_EVEN_OUT), 1)
            layer_norm(0)

            def experts(layer, c0):
                i = layer
                transposed(N(1 + 2 * layer))
                act.wait_ge(rt["logitsT"], i + 1)
                s.activation(logitsT[:], W[0:NE, 1, 0:SEQ], ACT.Copy).then_inc(rt["logits_sb"], 1)
                act.wait_ge(rt["max"], i + 1)
                s.activation(prob[:], prob[:], ACT.Exp).then_inc(rt["exp"], 1)
                def tokens(e):
                    act.wait_ge(me["ga"], (N(NE * layer).plus(e, 1) + 1).v)
                    s.activation(xe[:, :, 0:CAP], W[:, 3, :].rearrange("p (k t) -> p k t", t=CAP), ACT.Copy).then_inc(me["xh"], 1)

                def bottom(dst, bank, n, used_count, name):
                    act.wait_ge(used, used_count.v)
                    s.activation(dst[:, n, :], W[CAP:P, bank, :], ACT.Copy).then_inc(me[name], 1)

                def expert(e, c, last):
                    one = N(NE * layer).plus(e, 1)
                    two = one.times(2)

                    def silu(n):
                        act.wait_ge(me["g"], (two + (n + 1)).v)
                        s.activation(gb[:, n, :], gb[:, n, :], ACT.Silu).then_inc(me["sg"], 1)

                    def hidden_hi(n):
                        act.wait_ge(me["tr"], (two + (n + 1)).v)
                        s.activation(heT[:, 4 * n:4 * n + 4, 0:CAP],
                                     W[:, TURN_BANK[n], 0:256].rearrange("p (k t) -> p k t", t=CAP),
                                     ACT.Copy).then_inc(me["hh"], 1)

                    silu(0)
                    act.wait_ge(me["pt"], (one + 1).v)
                    s.activation(pickT[:], W[:, 1, 0:SEQ], ACT.Copy)
                    s.activation(gslot[:], W[:, 1, SEQ:SEQ + 1], ACT.Copy).then_inc(me["pte"], 1)
                    split(c + 3)
                    split(c + 4)
                    bottom(gb, 2, 1, c + 2, "gb")
                    split(c + 5)
                    hidden_hi(0)
                    silu(1)
                    split(c + 6)
                    bottom(ub, 0, 1, c + 4, "ub")
                    if not last:
                        tokens(e + 1)
                    split(c + 7)
                    split(c + 8)
                    hidden_hi(1)
                    split(c + 9)
                    if not last:
                        split(c + 10)
                        bottom(gb, 0, 0, c + 8, "gb")
                        split(c + 11)
                    act.wait_ge(me["pte"], (one + 1).v)
                    act.wait_ge(used, (c + (8 if last else 10)).v)
                    for n in range(2):
                        s.activation(Y_hi[:, 512 * n:512 * (n + 1)], W[:, 1 + n, :], ACT.Copy, scale=gslot[:]).then_inc(me["yh"], 1)
                    split(c + (10 if last else 12))
                    if not last:
                        split(c + 13)
                        split(c + 14)
                        bottom(ub, 3, 0, c + 12, "ub")

                tokens(0)
                split(N(c0 + 3))
                split(N(c0 + 4))
                bottom(gb, 0, 0, N(c0 + 2), "gb")
                split(N(c0 + 5))
                split(N(c0 + 6))
                bottom(ub, 3, 0, N(c0 + 4), "ub")
                with act.Fori(0, NE - 1) as e:
                    expert(e, N(c0 + 4).plus(e, MOE_CHUNKS), False)
                expert(NE - 1, N(c0 + 4 + MOE_CHUNKS * (NE - 1)), True)
                with crowded(act, layer):
                    more_rounds(layer)

            def more_rounds(layer):
                o = ov[layer]
                with act.Fori(0, ROUNDS - 1) as r:
                    with act.Fori(0, NE) as e:
                        k = N(0, (r, NE), (e, 1))

                        def split_rows(i):
                            c = k.times(24) + i
                            act.wait_ge(o["landed"], (c + 1).times(16).v)
                            s.activation(ov_hi[:], ov_raw[:], ACT.Copy).then_inc(o["hi"], 1)

                        act.wait_ge(*ov_done(o, "gathered", k))
                        s.activation(xe[:, :, 0:CAP], W[:, 3, :].rearrange("p (k t) -> p k t", t=CAP), ACT.Copy).then_inc(o["scalar"], 1)
                        act.wait_ge(*ov_done(o, "turned", k))
                        s.activation(pickT[:], W[:, 0, 0:SEQ], ACT.Copy)
                        s.activation(gslot[:], W[:, 0, SEQ:SEQ + 1], ACT.Copy).then_inc(o["scalar"], 1)
                        for i in range(2 * KC):
                            split_rows(i)
                        act.wait_ge(o["free"], (k.times(24) + (2 * KC + 1)).v)
                        s.activation(gb[:], W[CAP:P, 0:2, :], ACT.Copy)
                        s.activation(ub[:], W[CAP:P, 2:4, :], ACT.Copy).then_inc(o["scalar"], 1)
                        act.wait_ge(*ov_done(o, "gate_sum", k))
                        s.activation(gb[:], gb[:], ACT.Silu).then_inc(o["scalar"], 1)
                        act.wait_ge(*ov_done(o, "hidden_turned", k))
                        s.activation(heT[:, :, 0:CAP], W[:, 0, :].rearrange("p (k t) -> p k t", t=CAP), ACT.Copy).then_inc(o["scalar"], 1)
                        for i in range(2 * KC, 3 * KC):
                            split_rows(i)
                        act.wait_ge(o["free"], (k.times(24) + (3 * KC + 1)).v)
                        s.activation(Y_hi[:], W[:, 1:3, :].rearrange("p a n -> p (a n)"), ACT.Copy, scale=gslot[:]).then_inc(o["scalar"], 1)

            experts(0, C_MOE0)
            layer_norm(1)

            act.wait_ge(od["sp"], 1)
            s.activation(spt[:, 1, :], spt[:, 0, :], ACT.Exp, scale=-1.0)
            act.drain()
            s.activation(spt[:, 2, :], spt[:, 1, :], ACT.Ln, bias=onec[:]).then_inc(od["sp2"], 1)
            transposed(N(2))
            projection(N(C_ODD_IN), u_odd, 2 * D // 512, 512)
            act.wait_ge(od["pad"], 1)
            for i in range(8):
                act.wait_ge(od["tp"], i + 1)
                if i < 4:
                    last = s.activation(xrT[:, 2 * i:2 * i + 2, CONV_C - 1:], W[:, i % 4, :].rearrange("p (a t) -> p a t", a=2), ACT.Copy)
                else:
                    last = s.activation(yT[:, 2 * i - 8:2 * i - 6, :], W[:, i % 4, :].rearrange("p (a t) -> p a t", a=2), ACT.Gelu_apprx_tanh)
                last.then_inc(od["tr"], 1)
            def mixed_hi(h, done, signal):
                act.wait_ge(od[done], h + 1)
                s.activation(xT_hi[:, 4 * h:4 * h + 4, :], xc[:, 4 * h:4 * h + 4, :], ACT.Copy).then_inc(od[signal], 1)

            def gates(i):
                act.wait_ge(od["gates"], i + 1)
                s.activation(lru_r[:, i, :], W[:, i % 4, 0:SEQ], ACT.Sigmoid, bias=vec("odd_b_gate_a", i))
                s.activation(lru_i[:, i, :], W[:, i % 4, SEQ:2 * SEQ], ACT.Sigmoid, bias=vec("odd_b_gate_x", i)).then_inc(od["ri"], 1)

            def decay(h):
                own = slice(4 * h, 4 * h + 4)
                act.wait_ge(od["nla"], h + 1)
                s.activation(lru_a[:, own], lru_r[:, own], ACT.Exp, scale=-1.0)
                s.activation(lru_t[:, own], lru_r[:, own], ACT.Tanh).then_inc(od["exp"], 1)
                act.wait_ge(od["m2"], h + 1)
                s.activation(lru_t[:, own], lru_t[:, own], ACT.Sqrt).then_inc(od["sqrt"], 1)

            mixed_hi(0, "xc", "hi")
            gates(0)
            gates(1)
            mixed_hi(1, "xc", "hi")
            gates(2)
            gates(3)
            decay(0)
            for i in range(4, 8):
                gates(i)
            split(N(C_GATES + AHEAD), D)
            split(N(C_GATES + AHEAD + 1), D)
            mixed_hi(0, "h", "out_hi")
            decay(1)
            split(N(C_ODD_OUT + AHEAD), D)
            split(N(C_ODD_OUT + 1 + AHEAD), D)
            mixed_hi(1, "h", "out_hi")
            tail(N(C_ODD_OUT), 2)
            layer_norm(2)

            experts(1, C_MOE1)
            layer_norm(3)

            def rms(call):
                act.wait_ge(x_ready, (call + X_LAYERS).v)
                s.activation(xn[:, 0, :], x[:, 0, :], ACT.Square, accum_out=std[:, 0:1])
                act.drain().then_inc(rm["ssa"], 1)
                act.wait_ge(rm["ssd"], (call + 1).v)
                s.activation(std[:], std[:], ACT.Sqrt, bias=rmeps[:], scale=1.0 / D).then_inc(rm["std"], 1)
                act.wait_ge(rm["rs"], (call + 1).v)
                s.activation(xn[:, 0, :], x[:, 0, :], ACT.Copy, scale=rstd[:, 0:1]).then_inc(rm["xa"], 1)

            def gain_of(name, l):
                a = VEC_AT[name]
                return lambda k: vecs[:, bass.ds(l * KC + (a + k), 1)]

            def ffn(c0, last):
                def silu(parity, consumed):
                    act.wait_ge(used, consumed.v)
                    s.activation(sg[:, parity, :], W[:, 2 * parity, :], ACT.Silu).then_inc(ff["sg"], 1)

                split(c0 + 3)
                silu(0, c0 + 1)
                split(c0 + 4)
                with act.Fori(0, (FF_GROUPS - 3) // 2) as i:
                    for t in range(2):
                        c = (c0 + (2 + 3 * t)).plus(i, 6)
                        split(c + 3)
                        silu(1 - t, c + 1)
                        split(c + 4)
                        split(c + 5)
                for t in range(2):
                    for k in range(3):
                        i = 2 + 3 * (FF_GROUPS - 3 + t) + k
                        if i + AHEAD < FF_CHUNKS or not last:
                            split(c0 + (i + AHEAD))
                        if k == 0:
                            silu(1 - t, c0 + (i + 1))
                if not last:
                    split(c0 + (FF_CHUNKS - 1 + AHEAD))

            def mixer(l, c0):
                lay = N(0, (l, 1))
                c = c0 + C_MIX_IN
                for j in range(IN_GROUPS):
                    split(c + (2 * j + 3), 4 * IN_COLS if 2 * j + 3 < 16 else D)
                    act.wait_ge(used, (c + (2 * j + 2)).v)
                    s.activation(proj[:, 0, IN_COLS * j:IN_COLS * (j + 1)], W[:, (2 * j) % 4, 0:IN_COLS],
                                 ACT.Copy).then_inc(tm_act, 1)
                    split(c + (2 * j + 4), 4 * IN_COLS if 2 * j + 4 < 16 else D)
                    for r in range(3):
                        at0, n = NORM_REGIONS[r]
                        heads = slice(NORM_FIRST[r], NORM_FIRST[r] + n)
                        if j == NORM_GROUP[r] + 1:
                            act.wait_ge(mx["ss"], (lay.times(3) + (r + 1)).v)
                            s.activation(hrs[:, :, heads], hsum[:, :, heads], ACT.Sqrt, bias=rmeps[:], scale=1.0 / HD).then_inc(mx["std"], 1)
                        if j == NORM_GROUP[r]:
                            act.drain()
                            act.wait_ge(tm_dve, N(9 + j + 1, (l, IN_GROUPS)).v)
                            s.activation(sq[:, :, 0:n * HD], proj[:, :, at0:at0 + n * HD], ACT.Square).then_inc(mx["sq"], 1)
                act.wait_ge(mx["z"], (lay + 1).v)
                s.activation(lft[:], lft[:], ACT.Exp, scale=-1.0)
                act.drain()
                s.activation(lft[:], lft[:], ACT.Ln, bias=onec[:]).then_inc(mx["ln"], 1)
                act.wait_ge(tm_dve, N(9 + IN_GROUPS, (l, IN_GROUPS)).v)
                s.activation(proj[:, :, CG:IN_WIDTH], proj[:, :, CG:IN_WIDTH], ACT.Sigmoid).then_inc(mx["cg"], 1)
                act.wait_ge(mx["qkd"], (lay.times(2) + 1).v)
                s.activation(QK[:, :, 320:384], QK[:, :, 256:320], ACT.Copy)
                act.wait_ge(mx["qkp"], (lay + 1).v)
                s.activation(QK[:, :, 960:1024], QK[:, :, 896:960], ACT.Copy).then_inc(mx["dup"], 1)
                for i in range(0, 10, 2):
                    act.wait_ge(mx["qkt"], (lay.times(10) + (i + 1)).v)
                    s.activation(QKT[:, 2 * i:2 * i + 2, :], W[:, i % 4, :].rearrange("p (a t) -> p a t", a=2),
                                 ACT.Copy).then_inc(mx["qkta"], 1)
                for b in range(TB):
                    act.wait_ge(mx["is"], (lay.times(2) + (b + 1)).v)
                    if b == 1:
                        act.wait_ge(mx["ib"], (lay + 1).v)
                    n = P * (b + 1)
                    src = (acc, W)[b][:, 0:2 * (b + 1), :].rearrange("p a (h k) -> p (a h) k", k=n)
                    s.activation(relu[:, :, 0:n], src, ACT.Relu).then_inc(mx["relu"], 1)
                for u in range(8):
                    b, grp = UNITS[u]
                    n = P * (b + 1)
                    act.wait_ge(mx["sb"], (lay.times(8) + (u + 1)).v)
                    for h in range(4):
                        s.activation(Sb[:, u % 2, h, 0:n], Sb[:, u % 2, h, 0:n], ACT.Exp, bias=amax[:, u, h:h + 1],
                                     accum_out=asum[:, u, h:h + 1])
                    act.drain().then_inc(mx["p"], 1)
                    act.wait_ge(mx["t"], (lay.times(8) + (u + 1)).v)
                    s.activation(PT[:, :, 0:n], acc[:, 0:b + 1, :].rearrange("p a (h k) -> p (a h) k", k=n),
                                 ACT.Copy).then_inc(mx["te"], 1)
                transposed(N(6, (l, 4)))
                for k in range(KC):
                    split(c0 + (C_MIX_OUT + k + AHEAD), D if k + AHEAD < KC else SLOT)

            with act.Fori(0, DEPTH) as l:
                c0 = N(C_LAYERS).plus(l, LAYER_CHUNKS)
                rms(N(0, (l, 3)))
                transposed(N(4, (l, 4)), gain_of("ffn1_norm_2", l))
                ffn(c0 + C_FFN1, False)
                rms(N(1, (l, 3)))
                transposed(N(5, (l, 4)), gain_of("mix_norm_2", l))
                mixer(l, c0)
                rms(N(2, (l, 3)))
                transposed(N(7, (l, 4)), gain_of("ffn2_norm_2", l))
                ffn(c0 + C_FFN2, True)
                with act.If(l < DEPTH - 1):
                    for k in range(AHEAD):
                        split(c0 + (LAYER_CHUNKS + k))

        @block.vector
        def _(dve):
            v = nc.vector

            def rest(c, cols=SLOT):
                dve.wait_ge(hi_ready, (c + 1).v)
                v.tensor_tensor(w_lo[split_slot(c)][:, 0:cols], raw[slot_of(c)][:, 0:cols],
                                w_hi[split_slot(c)][:, 0:cols].bitcast(F32), ALU.subtract).then_inc(lo_ready, 1)

            def n_after(c):
                for a in (C_EVEN_OUT, C_ODD_OUT):
                    if a <= c.base < a + KC:
                        return D
                return SLOT

            def transposed(call, gain=None):
                for q in range(4):
                    dve.wait_ge(xt_hi_s, (call.times(4) + (q + 1)).v)
                    hi = xT_hi[:, 2 * q:2 * q + 2, :].rearrange("p a t -> p (a t)").bitcast(F32)
                    lo = xT_lo[:, 2 * q:2 * q + 2, :].rearrange("p a t -> p (a t)")
                    if gain is None:
                        last = v.tensor_tensor(lo, W[:, q, :], hi, ALU.subtract)
                    else:
                        for kk in range(2):
                            cols = slice(kk * SEQ, (kk + 1) * SEQ)
                            last = v.scalar_tensor_tensor(lo[:, cols], W[:, q, cols], gain(2 * q + kk), hi[:, cols],
                                                          ALU.mult, ALU.subtract)
                    last.then_inc(xt_lo_s, 1)

            def projection(c0, dst, groups, n):
                for j in range(groups):
                    rest(c0 + (2 * j + AHEAD), n_after(c0 + (2 * j + AHEAD)))
                    dve.wait_ge(used, (c0 + (2 * j + 2)).v)
                    v.tensor_copy(dst[:, 1, n * j:n * (j + 1)], W[:, (2 * j + 1) % 4, 0:n]).then_inc(tm_dve, 1)
                    rest(c0 + (2 * j + 1 + AHEAD), n_after(c0 + (2 * j + 1 + AHEAD)))

            def tail(c0, first=0):
                for k in range(first, KC - 1):
                    rest(c0 + (k + AHEAD), D if k + AHEAD < KC else SLOT)

            def layer_norm(i, ready, count, ahead=None):
                dve.wait_ge(ready, count)
                for b in range(TB):
                    v.scalar_tensor_tensor(x[:, b, :], x[:, b, :], ALPHA, acc[:, 2 * b:2 * b + 2, :].rearrange("p a n -> p (a n)"),
                                           ALU.mult, ALU.add)
                v.drain()
                for b in range(TB):
                    for n in range(2):
                        v.bn_stats(stats[:, b, n, :], x[:, b, 512 * n:512 * (n + 1)])
                v.drain()
                for b in range(TB):
                    v.bn_aggr(mv[:, b, :], stats[:, b, :, :].rearrange("p a s -> p (a s)"))
                v.drain().then_inc(ln_mv, 1)
                dve.wait_ge(ln_std, i + 1)
                v.reciprocal(rstd[:], std[:])
                v.drain()
                v.scalar_tensor_tensor(nmr[:], mv[:, :, 0], -1.0, rstd[:], ALU.mult, ALU.mult)
                v.drain().then_inc(ln_rs, 1)
                v.tensor_scalar(x[:, 0, :], x[:, 0, :], mv[:, 0, 0:1], rstd[:, 0:1], ALU.subtract, ALU.mult)
                v.drain()
                dve.wait_ge(ln_in, 32 * (i + 1))
                v.tensor_tensor(x[:, 0, :], x[:, 0, :], lng[:], ALU.mult)
                v.drain()
                v.tensor_tensor(x[:, 0, :], x[:, 0, :], lnb[:], ALU.add)
                v.drain().then_inc(ln_x0, 1)
                dve.wait_ge(ln_x1a, i + 1)
                v.tensor_tensor(x[:, 1, 512:], x[:, 1, 512:], lng[:, 512:], ALU.mult)
                v.drain()
                v.tensor_tensor(x[:, 1, 512:], x[:, 1, 512:], lnb[:, 512:], ALU.add)
                v.drain()
                dve.wait_ge(ln_x1, i + 1)
                dve.sem_inc(x_ready, 1)
                if ahead is not None:
                    rest(ahead)

            v.memset(zeros[:].bitcast(F32), 0.0)
            v.memset(lneps[:], LN_EPS)
            v.memset(rmeps[:], RMS_EPS)
            v.memset(onec[:], 1.0)
            v.memset(aT[:, :, 0:CONV_A - 1], 0.0)
            v.memset(bxT[:, :, 0:CONV_B - 1], 0.0)
            v.drain().then_inc(ff["h"], 1)
            dve.sem_inc(ev["pad"], 1)
            dve.wait_ge(x_in, 16)
            dve.sem_inc(x_ready, 1)
            for c in range(AHEAD):
                rest(N(c))
            transposed(N(0))
            projection(N(C_EVEN_IN), u_even, EVEN_IN // 512, 512)

            dve.wait_ge(small_in, SMALL_LOADS * 16)
            v.tensor_copy(wr_hi[:], wr[:])
            v.drain()
            v.tensor_tensor(wr_lo[:], wr[:], wr_hi[:].bitcast(F32), ALU.subtract).then_inc(wr_ok, 1)

            dve.wait_ge(vecs_ok, 1)
            dve.wait_ge(ev["sig"], 1)
            v.tensor_tensor(u_even[:, :, 0:512], u_even[:, :, 0:512], u_even[:, :, 512:1024], ALU.mult).then_inc(ev["a"], 1)
            dve.wait_ge(ev["tr"], 1)
            for k in range(CONV_A):
                for c in range(2):
                    tap = vec("even_a_dw", 4 * k + c)
                    src = aT[:, c, k:k + SEQ]
                    if k == 0:
                        v.tensor_scalar(ca[:, c, :], src, tap, vec("even_a_dw_b", c), ALU.mult, ALU.add)
                    else:
                        last = v.scalar_tensor_tensor(ca[:, c, :], src, tap, ca[:, c, :], ALU.mult, ALU.add)
                if k < CONV_A - 1:
                    v.drain()
            last.then_inc(ev["conv"], 1)
            dve.wait_ge(ev["tr"], 6)
            for k in range(CONV_B):
                for c in range(4):
                    tap = vec("even_b_dw", 4 * k + c)
                    src = bxT[:, c, k:k + SEQ]
                    if k == 0:
                        v.tensor_scalar(cb[:, c, :], src, tap, None, ALU.mult)
                    else:
                        v.scalar_tensor_tensor(cb[:, c, :], src, tap, cb[:, c, :], ALU.mult, ALU.add)
                v.drain()
            v.tensor_tensor(cb[:], cb[:], bbT[:], ALU.mult)
            v.drain()
            v.tensor_copy(xT_hi[:, 4:8, :], cb[:])
            v.drain()
            v.tensor_tensor(xT_lo[:, 4:8, :], cb[:], xT_hi[:, 4:8, :].bitcast(F32), ALU.subtract).then_inc(ev["done"], 1)
            dve.wait_ge(ev["back"], 1)
            for b in range(TB):
                v.bn_stats(stats[:, b, 0, :], W[:, b, :])
            v.drain()
            for b in range(TB):
                v.bn_aggr(mv[:, b, :], stats[:, b, 0, :])
            v.drain().then_inc(ev["mv"], 1)
            dve.wait_ge(ev["std"], 1)
            v.reciprocal(rstd[:], std[:])
            v.drain()
            for b in range(TB):
                last = v.tensor_scalar(an[:, b, :], W[:, b, :], mv[:, b, 0:1], rstd[:, b:b + 1], ALU.subtract, ALU.mult)
            last.then_inc(ev["an"], 1)
            rest(N(C_EVEN_OUT + AHEAD), D)
            dve.wait_ge(ev["silu"], 1)
            v.tensor_tensor(xT_lo[:, 0:4, :], a2[:], xT_hi[:, 0:4, :].bitcast(F32), ALU.subtract).then_inc(ev["done"], 1)
            tail(N(C_EVEN_OUT), 1)
            layer_norm(0, used, C_EVEN_OUT + KC, N(C_EVEN_OUT + KC - 1 + AHEAD))

            def top_ranks(values, greater, equal, out, n, groups):
                shape = [P, groups, n, n]
                other, own = values.unsqueeze(2).to_broadcast(shape), values.unsqueeze(3).to_broadcast(shape)
                v.tensor_tensor(greater, other, own, ALU.is_gt)
                v.tensor_tensor(equal, other, own, ALU.is_equal)
                v.drain()
                v.tensor_tensor(equal, equal, earlier[:].unsqueeze(1).to_broadcast(shape), ALU.mult)
                v.drain()
                v.tensor_tensor(greater, greater, equal, ALU.add)
                v.drain()
                v.tensor_reduce(out, greater, AX, ALU.add)
                v.drain()

            def experts(layer, c0):
                i = layer
                transposed(N(1 + 2 * layer))
                dve.wait_ge(rt["logits"], i + 1)
                wide = [P, TB, NE]
                v.tensor_tensor(prob[:], W[:, 0, 0:TB * NE].rearrange("p (b e) -> p b e", b=TB),
                                br[:].unsqueeze(1).to_broadcast(wide), ALU.add)
                v.drain()
                v.tensor_reduce(rmax[:], prob[:], AX, ALU.max)
                v.drain()
                v.tensor_tensor(prob[:], prob[:], rmax[:].unsqueeze(2).to_broadcast(wide), ALU.subtract)
                v.drain().then_inc(rt["max"], 1)
                dve.wait_ge(rt["exp"], i + 1)
                v.tensor_reduce(rsum[:], prob[:], AX, ALU.add)
                v.drain()
                v.reciprocal(rsum[:], rsum[:])
                v.drain()
                v.tensor_tensor(prob[:], prob[:], rsum[:].unsqueeze(2).to_broadcast(wide), ALU.mult)
                v.drain()
                grouped = prob[:].rearrange("p b (g c) -> p (b g) c", c=EPG)
                top_ranks(grouped, cmp[:], cmp2[:], rank[:].rearrange("p b (g c) -> p (b g) c", c=EPG), EPG, TB * NG)
                v.tensor_scalar(top2[:], rank[:], 1.5, None, ALU.is_lt)
                v.drain()
                v.tensor_tensor(chosen[:], prob[:], top2[:], ALU.mult)
                v.drain()
                v.tensor_reduce(gscore[:].rearrange("p b g -> p (b g)"), chosen[:].rearrange("p b (g c) -> p (b g) c", c=EPG), AX, ALU.add)
                v.drain()
                top_ranks(gscore[:], gcmp[:], gcmp2[:], grank[:], NG, TB)
                v.tensor_scalar(grank[:], grank[:], 0.5, None, ALU.is_lt)
                v.drain()
                v.tensor_tensor(top2[:].rearrange("p b (g c) -> p (b g) c", c=EPG), top2[:].rearrange("p b (g c) -> p (b g) c", c=EPG),
                                grank[:].rearrange("p b g -> p (b g)").unsqueeze(2).to_broadcast([P, TB * NG, EPG]), ALU.mult)
                v.drain().then_inc(rt["chosen"], 1)
                v.tensor_tensor(chosen[:], prob[:], top2[:], ALU.mult)
                v.drain()
                v.tensor_reduce(rsum[:], chosen[:], AX, ALU.add)
                v.drain()
                v.reciprocal(rsum[:], rsum[:])
                v.drain()
                v.tensor_tensor(gate[:], chosen[:], rsum[:].unsqueeze(2).to_broadcast(wide), ALU.mult)
                dve.wait_ge(rt["ranks"], i + 1)
                v.scalar_tensor_tensor(pos[:, :, 0:NE], W[:, 1, 0:TB * NE].rearrange("p (b e) -> p b e", b=TB), 1.0, top2[:],
                                       ALU.add, ALU.mult)
                v.tensor_reduce(count_max[:], W[:, 1, TB * NE:(TB + 1) * NE], AX, ALU.max)
                v.drain()
                v.tensor_scalar(pos[:, :, 0:NE], pos[:, :, 0:NE], -1.0, None, ALU.add)
                v.tensor_copy(count_i[:], count_max[:])
                v.drain().then_inc(rt["ready"], 1)

                def pick_tokens(e):
                    for b in range(TB):
                        last = v.tensor_scalar(pick[:, b, :], slot_ids[:, 0, :], pos[:, b, e], None, ALU.is_equal)
                    last.then_inc(me["pick"], 1)

                def gate_first(count):
                    dve.wait_ge(me["gb"], count.v)
                    v.tensor_tensor(gb[:, 0, :], W[0:CAP, 0, :], gb[:, 0, :], ALU.add).then_inc(me["g"], 1)

                def expert(e, c, last):
                    one = N(NE * layer).plus(e, 1)
                    two = one.times(2)

                    def add_bottom(buf, bank, n, name):
                        dve.wait_ge(me[name], (two + (n + 1)).v)
                        return v.tensor_tensor(buf[:, n, :], W[0:CAP, bank, :], buf[:, n, :], ALU.add)

                    def hidden(bank, n):
                        add_bottom(ub, bank, n, "ub")
                        v.drain()
                        dve.wait_ge(me["sg"], (two + (n + 1)).v)
                        v.tensor_tensor(ub[:, n, :], ub[:, n, :], gb[:, n, :], ALU.mult).then_inc(me["h"], 1)

                    def hidden_lo(n):
                        dve.wait_ge(me["hh"], (two + (n + 1)).v)
                        v.tensor_tensor(heT[:, 4 * n:4 * n + 4, CAP:2 * CAP],
                                        W[:, TURN_BANK[n], 0:256].rearrange("p (k t) -> p k t", t=CAP),
                                        heT[:, 4 * n:4 * n + 4, 0:CAP].bitcast(F32), ALU.subtract).then_inc(me["hT"], 1)

                    hidden(3, 0)
                    rest(c + 3)
                    if not last:
                        dve.wait_ge(me["pt"], (one + 1).v)
                        pick_tokens(bass.ds(e + 1, 1))
                    rest(c + 4)
                    add_bottom(gb, 2, 1, "gb").then_inc(me["g"], 1)
                    rest(c + 5)
                    hidden_lo(0)
                    rest(c + 6)
                    hidden(0, 1)
                    if not last:
                        tokens_lo(e + 1)
                    rest(c + 7)
                    rest(c + 8)
                    hidden_lo(1)
                    rest(c + 9)
                    if not last:
                        rest(c + 10)
                        gate_first(two + 3)
                        rest(c + 11)
                    for n in range(2):
                        dve.wait_ge(me["yh"], (two + (n + 1)).v)
                        cols = slice(512 * n, 512 * (n + 1))
                        v.scalar_tensor_tensor(Y_lo[:, cols], W[:, 1 + n, :], gslot[:, 0:1], Y_hi[:, cols].bitcast(F32),
                                               ALU.mult, ALU.subtract).then_inc(me["y"], 1)
                    rest(c + (10 if last else 12))
                    if not last:
                        rest(c + 13)
                        rest(c + 14)

                def tokens_lo(e):
                    dve.wait_ge(me["xh"], (N(NE * layer).plus(e, 1) + 1).v)
                    v.tensor_tensor(xe[:, :, CAP:2 * CAP], W[:, 3, :].rearrange("p (k t) -> p k t", t=CAP),
                                    xe[:, :, 0:CAP].bitcast(F32), ALU.subtract).then_inc(me["xe"], 1)

                pick_tokens(slice(0, 1))
                tokens_lo(0)
                rest(N(c0 + 3))
                rest(N(c0 + 4))
                gate_first(N(2 * NE * layer + 1))
                rest(N(c0 + 5))
                rest(N(c0 + 6))
                with dve.Fori(0, NE - 1) as e:
                    expert(e, N(c0 + 4).plus(e, MOE_CHUNKS), False)
                expert(NE - 1, N(c0 + 4 + MOE_CHUNKS * (NE - 1)), True)
                with crowded(dve, layer):
                    more_rounds(layer)

            def more_rounds(layer):
                o = ov[layer]
                dve.wait_ge(me["ga"], NE * (layer + 1))
                with dve.Fori(0, ROUNDS - 1) as r:
                    with dve.Fori(0, NE) as e:
                        k = N(0, (r, NE), (e, 1))

                        def rest_rows(i):
                            dve.wait_ge(o["hi"], (k.times(24) + (i + 1)).v)
                            v.tensor_tensor(ov_lo[:], ov_raw[:], ov_hi[:].bitcast(F32), ALU.subtract).then_inc(o["lo"], 1)

                        v.drain()
                        for b in range(TB):
                            last = v.tensor_scalar(pick[:, b, :], slot_ids[:, bass.ds(r + 1, 1), :].rearrange("p a s -> p (a s)"),
                                                   pos[:, b, bass.ds(e, 1)], None, ALU.is_equal)
                        last.then_inc(o["vector"], 1)
                        dve.wait_ge(*ov_done(o, "tokens_hi", k))
                        v.tensor_tensor(xe[:, :, CAP:2 * CAP], W[:, 3, :].rearrange("p (k t) -> p k t", t=CAP),
                                        xe[:, :, 0:CAP].bitcast(F32), ALU.subtract).then_inc(o["vector"], 1)
                        for i in range(2 * KC):
                            rest_rows(i)
                        dve.wait_ge(*ov_done(o, "lower_halves", k))
                        v.tensor_tensor(gb[:], W[0:CAP, 0:2, :], gb[:], ALU.add).then_inc(o["vector"], 1)
                        v.tensor_tensor(ub[:], W[0:CAP, 2:4, :], ub[:], ALU.add)
                        v.drain()
                        dve.wait_ge(*ov_done(o, "gated", k))
                        v.tensor_tensor(ub[:], ub[:], gb[:], ALU.mult).then_inc(o["vector"], 1)
                        dve.wait_ge(*ov_done(o, "hidden_hi", k))
                        v.tensor_tensor(heT[:, :, CAP:2 * CAP], W[:, 0, :].rearrange("p (k t) -> p k t", t=CAP),
                                        heT[:, :, 0:CAP].bitcast(F32), ALU.subtract).then_inc(o["vector"], 1)
                        for i in range(2 * KC, 3 * KC):
                            rest_rows(i)
                        dve.wait_ge(*ov_done(o, "out_hi", k))
                        v.scalar_tensor_tensor(Y_lo[:], W[:, 1:3, :].rearrange("p a n -> p (a n)"), gslot[:, 0:1],
                                               Y_hi[:].bitcast(F32), ALU.mult, ALU.subtract).then_inc(o["vector"], 1)
                        dve.wait_ge(*ov_done(o, "added", k))

            experts(0, C_MOE0)
            layer_norm(1, me["sc"], NE)

            v.memset(xrT[:, :, 0:CONV_C - 1], 0.0).then_inc(od["pad"], 1)
            v.scalar_tensor_tensor(spt[:, 0, :], vecs[:, VEC_AT["odd_lam"]:VEC_AT["odd_lam"] + 8], -1.0,
                                   vecs[:, VEC_AT["odd_lam"]:VEC_AT["odd_lam"] + 8], ALU.mult, ALU.max).then_inc(od["sp"], 1)
            dve.wait_ge(od["sp2"], 1)
            lam = vecs[:, VEC_AT["odd_lam"]:VEC_AT["odd_lam"] + 8]
            v.tensor_scalar(spt[:, 0, :], spt[:, 1, :], 1.0, None, ALU.add)
            v.drain()
            v.scalar_tensor_tensor(spt[:, 3, :], spt[:, 0, :], -1.0, spt[:, 1, :], ALU.add, ALU.subtract)
            v.drain()
            v.reciprocal(spt[:, 1, :], spt[:, 0, :])
            v.drain()
            v.tensor_tensor(spt[:, 3, :], spt[:, 3, :], spt[:, 1, :], ALU.mult)
            v.drain()
            v.tensor_scalar(spt[:, 0, :], lam, -1.0, 0.0, ALU.mult, ALU.max)
            v.drain()
            v.tensor_tensor(spt[:, 2, :], spt[:, 2, :], spt[:, 3, :], ALU.subtract)
            v.drain()
            v.tensor_tensor(spt[:, 2, :], spt[:, 2, :], spt[:, 0, :], ALU.add)
            v.drain()
            v.tensor_scalar(sp8[:], spt[:, 2, :], LRU_C, None, ALU.mult)
            v.drain()
            transposed(N(2))
            projection(N(C_ODD_IN), u_odd, 2 * D // 512, 512)

            def convolve(h):
                for k in range(CONV_C):
                    for c in range(4 * h, 4 * h + 4):
                        tap = vec("odd_c_dw", 8 * k + c)
                        src = xrT[:, c, k:k + SEQ]
                        if k == 0:
                            v.tensor_scalar(xc[:, c, :], src, tap, vec("odd_c_dw_b", c), ALU.mult, ALU.add)
                        else:
                            v.scalar_tensor_tensor(xc[:, c, :], src, tap, xc[:, c, :], ALU.mult, ALU.add)
                    v.drain()
                dve.sem_inc(od["xc"], 1)

            def remainder(h, rounded, signal):
                own = slice(4 * h, 4 * h + 4)
                dve.wait_ge(od[rounded], h + 1)
                v.tensor_tensor(xT_lo[:, own], xc[:, own], xT_hi[:, own].bitcast(F32), ALU.subtract).then_inc(od[signal], 1)

            def recurrence(h):
                own = slice(4 * h, 4 * h + 4)
                v.drain()
                dve.wait_ge(od["ri"], 4 * h + 4)
                v.tensor_tensor(lru_r[:, own], lru_r[:, own], sp8[:, own].unsqueeze(2).to_broadcast([P, 4, SEQ]), ALU.mult).then_inc(od["nla"], 1)
                v.tensor_tensor(lru_i[:, own], lru_i[:, own], xc[:, own], ALU.mult)
                v.drain()
                dve.wait_ge(od["exp"], h + 1)
                v.tensor_tensor(xc[:, own], lru_a[:, own], lru_a[:, own], ALU.mult)
                v.drain()
                v.scalar_tensor_tensor(lru_t[:, own].rearrange("p a t -> p (a t)"), xc[:, own].rearrange("p a t -> p (a t)"), 1.0,
                                       lru_t[:, own].rearrange("p a t -> p (a t)"), ALU.add, ALU.mult).then_inc(od["m2"], 1)
                dve.wait_ge(od["sqrt"], h + 1)
                v.tensor_tensor(lru_t[:, own], lru_t[:, own], lru_i[:, own], ALU.mult)
                v.drain()
                for c in range(4 * h, 4 * h + 4):
                    v.tensor_tensor_scan(lru_r[:, c, :], lru_a[:, c, :], lru_t[:, c, :], 0.0, ALU.mult, ALU.add)
                v.drain()
                dve.wait_ge(od["tr"], 8)
                v.tensor_tensor(xc[:, own], lru_r[:, own], yT[:, own], ALU.mult).then_inc(od["h"], 1)

            dve.wait_ge(od["tr"], 4)
            convolve(0)
            remainder(0, "hi", "lo")
            convolve(1)
            remainder(1, "hi", "lo")
            recurrence(0)
            rest(N(C_GATES + AHEAD), D)
            rest(N(C_GATES + AHEAD + 1), D)
            remainder(0, "out_hi", "done")
            recurrence(1)
            rest(N(C_ODD_OUT + AHEAD), D)
            rest(N(C_ODD_OUT + 1 + AHEAD), D)
            remainder(1, "out_hi", "done")
            tail(N(C_ODD_OUT), 2)
            layer_norm(2, used, C_ODD_OUT + KC, N(C_ODD_OUT + KC - 1 + AHEAD))

            experts(1, C_MOE1)
            layer_norm(3, me["sc"], 2 * NE)

            def rms(call):
                dve.wait_ge(x_ready, (call + X_LAYERS).v)
                v.tensor_tensor_reduce(xn[:, 1, :], x[:, 1, :], x[:, 1, :], 1.0, 0.0, ALU.mult, ALU.add, std[:, 1:2])
                v.drain().then_inc(rm["ssd"], 1)
                dve.wait_ge(rm["std"], (call + 1).v)
                v.reciprocal(rstd[:], std[:])
                v.drain().then_inc(rm["rs"], 1)
                v.tensor_scalar(xn[:, 1, :], x[:, 1, :], rstd[:, 1:2], None, ALU.mult).then_inc(rm["xd"], 1)

            def add_to_x(count, scale):
                dve.wait_ge(used, count.v)
                for b in range(TB):
                    v.scalar_tensor_tensor(x[:, b, :], acc[:, 2 * b:2 * b + 2, :].rearrange("p a n -> p (a n)"), scale,
                                           x[:, b, :], ALU.mult, ALU.add)
                v.drain().then_inc(x_ready, 1)

            def gain_of(name, l):
                a = VEC_AT[name]
                return lambda k: vecs[:, bass.ds(l * KC + (a + k), 1)]

            def ffn(c0, sg0, last):
                def hidden(parity, consumed, n):
                    dve.wait_ge(used, consumed.v)
                    dve.wait_ge(ff["sg"], n.v)
                    v.tensor_tensor(hb[:], W[:, 2 * parity + 1, :], sg[:, parity, :], ALU.mult)
                    v.drain().then_inc(ff["h"], 1)
                    hi, lo = (t[:, parity].rearrange("p a t -> p (a t)") for t in (hT_hi, hT_lo))
                    v.tensor_copy(hi, hb[:])
                    v.drain()
                    v.tensor_tensor(lo, hb[:], hi.bitcast(F32), ALU.subtract)
                    v.drain().then_inc(ff["hT"], 1)

                rest(c0 + 3)
                rest(c0 + 4)
                hidden(0, c0 + 2, sg0 + 1)
                with dve.Fori(0, (FF_GROUPS - 3) // 2) as i:
                    for t in range(2):
                        c = (c0 + (2 + 3 * t)).plus(i, 6)
                        rest(c + 3)
                        rest(c + 4)
                        hidden(1 - t, c + 2, (sg0 + (t + 2)).plus(i, 2))
                        rest(c + 5)
                for t in range(2):
                    for k in range(3):
                        i = 2 + 3 * (FF_GROUPS - 3 + t) + k
                        if i + AHEAD < FF_CHUNKS or not last:
                            rest(c0 + (i + AHEAD))
                        if k == 1:
                            hidden(1 - t, c0 + (i + 1), sg0 + (FF_GROUPS - 1 + t))
                add_to_x(c0 + FF_CHUNKS, 0.5)

            def mixer(l, c0):
                lay = N(0, (l, 1))
                c = c0 + C_MIX_IN

                def head_sums(r):
                    n = NORM_REGIONS[r][1]
                    dve.wait_ge(mx["sq"], (lay.times(3) + (r + 1)).v)
                    for b in range(TB):
                        last = v.tensor_reduce(hsum[:, b, NORM_FIRST[r]:NORM_FIRST[r] + n],
                                               sq[:, b, 0:n * HD].rearrange("p (h d) -> p h d", d=HD), AX, ALU.add)
                    last.then_inc(mx["ss"], 1)

                def normalise(r):
                    at0, n = NORM_REGIONS[r]
                    own = slice(NORM_FIRST[r], NORM_FIRST[r] + n)
                    dve.wait_ge(mx["std"], (lay.times(3) + (r + 1)).v)
                    v.reciprocal(hrs[:, :, own], hrs[:, :, own])
                    v.drain()
                    for b in range(TB):
                        heads = proj[:, b, at0:at0 + n * HD].rearrange("p (h d) -> p h d", d=HD)
                        v.tensor_tensor(heads, heads, hrs[:, b, own].unsqueeze(2).to_broadcast([P, n, HD]), ALU.mult)
                    v.drain()
                    for i, (first, heads_of, to) in enumerate((((AQ, 4, None), (AK, 1, None)), ((BQ, 4, None), (BK, 4, None)),
                                                               ((CQ, 8, 1536), (CK, 8, 2048)))[r]):
                        for b in range(TB):
                            heads = proj[:, b, first:first + heads_of * HD].rearrange("p (h d) -> p h d", d=HD)
                            dst = heads if to is None else QK[:, b, to:to + heads_of * HD].rearrange("p (h d) -> p h d", d=HD)
                            v.tensor_tensor(dst, heads, head_gain[:, 2 * r + i:2 * r + i + 1, :].to_broadcast([P, heads_of, HD]), ALU.mult)
                    v.drain()

                for j in range(IN_GROUPS):
                    rest(c + (2 * j + 3), 4 * IN_COLS if 2 * j + 3 < 16 else D)
                    if j == 0:
                        dve.wait_ge(mx["in"], (lay + 1).times(112).v)
                        for i in (0, 2, 4):
                            v.tensor_scalar(head_gain[:, i, :], head_gain[:, i, :], QK_SCALE, None, ALU.mult)
                    for r in range(3):
                        if j == NORM_GROUP[r] + 1:
                            head_sums(r)
                    dve.wait_ge(used, (c + (2 * j + 2)).v)
                    v.tensor_copy(proj[:, 1, IN_COLS * j:IN_COLS * (j + 1)], W[:, (2 * j + 1) % 4, 0:IN_COLS]).then_inc(tm_dve, 1)
                    rest(c + (2 * j + 4), 4 * IN_COLS if 2 * j + 4 < 16 else D)
                    if j == INDEX_GROUP + 1:
                        v.drain()
                        dve.wait_ge(tm_act, N(9 + j, (l, IN_GROUPS)).v)
                        for b in range(TB):
                            v.tensor_scalar(iws[:, b, :].rearrange("p (r a) -> p r a", r=2),
                                            proj[:, b, IW:BQ].rearrange("p (a r) -> p r a", r=2), DSA_IDX_SCALE, None, ALU.mult)
                    if j == IN_GROUPS - 1:
                        v.drain()
                        dve.wait_ge(tm_act, N(9 + j, (l, IN_GROUPS)).v)
                        v.tensor_tensor(lf[:], proj[:, :, CF:CG], fb[:].unsqueeze(1).to_broadcast([P, TB, C_HEADS]), ALU.add)
                        v.drain()
                        v.scalar_tensor_tensor(lft[:], lf[:], -1.0, lf[:], ALU.mult, ALU.max).then_inc(mx["z"], 1)
                    for r in range(3):
                        if j == NORM_GROUP[r] + 1:
                            normalise(r)
                            if r == 0:
                                rotate(v, AQ, 0, 5, rt_d)
                                v.drain()
                            elif r == 1:
                                rotate(v, BQ, 1024, 8, rt_d)
                                v.drain().then_inc(mx["qkd"], 1)
                            else:
                                v.drain().then_inc(mx["qkd"], 1)
                dve.wait_ge(mx["ln"], (lay + 1).v)
                v.tensor_scalar(lf[:], lf[:], -1.0, 0.0, ALU.mult, ALU.max)
                v.drain()
                v.tensor_tensor(nlf[:], lf[:], lft[:], ALU.add).then_inc(mx["nlf"], 1)
                for i in range(1, 10, 2):
                    dve.wait_ge(mx["qkt"], (lay.times(10) + (i + 1)).v)
                    v.tensor_copy(QKT[:, 2 * i:2 * i + 2, :], W[:, i % 4, :].rearrange("p (a t) -> p a t", a=2)).then_inc(mx["qktd"], 1)
                for b in range(TB):
                    n = P * (b + 1)
                    dve.wait_ge(mx["relu"], (lay.times(2) + (b + 1)).v)
                    v.tensor_tensor(relu[:, :, 0:n], relu[:, :, 0:n], iws[:, b, :].unsqueeze(2).to_broadcast([P, 8, n]), ALU.mult)
                    v.drain()
                    v.tensor_reduce(score[:, b, 0:n], relu[:, :, 0:n].rearrange("p h k -> p k h"), AX, ALU.add)
                    if b == 0:
                        v.drain().then_inc(mx["ib"], 1)
                    else:
                        v.drain()
                    v.tensor_tensor(score[:, b, 0:n], score[:, b, 0:n], causal[:, b, 0:n], ALU.add)
                    v.drain()

                def best_keys(b, first, last):
                    n = P * (b + 1)
                    for r in range(first, last):
                        left = dsa_bias if r else score
                        v.max(top8[:, b, r, :], left[:, b, 0:n])
                        v.drain()
                        v.match_replace(dsa_bias[:, b, 0:n], top8[:, b, r, :], left[:, b, 0:n], REPLACED)
                        v.drain()

                def chosen_bias(b):
                    n = P * (b + 1)
                    v.tensor_tensor(dsa_bias[:, b, 0:n], dsa_bias[:, b, 0:n], score[:, b, 0:n], ALU.is_equal)
                    v.drain()
                    v.scalar_tensor_tensor(dsa_bias[:, b, 0:n], dsa_bias[:, b, 0:n], -BIG, causal[:, b, 0:n], ALU.mult, ALU.min)
                    v.drain()

                def finish(u):
                    b, grp = UNITS[u]
                    dve.wait_ge(mx["o"], (lay.times(8) + (u + 1)).v)
                    v.reciprocal(asum[:, u, :], asum[:, u, :])
                    v.drain()
                    for r in range(2):
                        dst = attn[:, b, 256 * grp:256 * (grp + 1)].rearrange("p (a r d) -> p r a d", r=2, d=HD)[:, r]
                        last = v.tensor_tensor(dst, acc[:, 2 + u % 2, P * r:P * (r + 1)].rearrange("p (a d) -> p a d", d=HD),
                                               asum[:, u, 2 * r:2 * r + 2].unsqueeze(2).to_broadcast([P, 2, HD]), ALU.mult)
                    if grp >= 2:
                        v.drain()
                        flat = attn[:, b, 256 * grp:256 * (grp + 1)]
                        cg = CG + 256 * (grp - 2)
                        last = v.tensor_tensor(flat, flat, proj[:, b, cg:cg + 256], ALU.mult)
                    last.then_inc(mx["at"], 1)

                for u in range(8):
                    b, grp = UNITS[u]
                    n = P * (b + 1)
                    dve.wait_ge(mx["s"], (lay.times(8) + (u + 1)).v)
                    if u >= 2:
                        dve.wait_ge(mx["t"], (lay.times(8) + (u - 1)).v)
                    bias = (dsa_bias if grp == 0 else causal)[:, b:b + 1, 0:n].to_broadcast([P, 2, n])
                    k = 2 * (u % 2)
                    for r in range(2):
                        v.tensor_tensor(Sb[:, u % 2, 2 * r:2 * r + 2, 0:n], W[:, k + r, 0:2 * n].rearrange("p (h k) -> p h k", k=n),
                                        bias, ALU.add)
                    v.drain()
                    v.tensor_reduce(amax[:, u, :], Sb[:, u % 2, :, 0:n], AX, ALU.max, negate=True)
                    v.drain().then_inc(mx["sb"], 1)
                    if u:
                        finish(u - 1)
                    if u < 6:
                        best_keys(u // 3, *((0, 3), (3, 6), (6, 8))[u % 3])
                        if u % 3 == 2:
                            chosen_bias(u // 3)
                finish(7)
                transposed(N(6, (l, 4)))
                for k in range(KC - 1):
                    rest(c0 + (C_MIX_OUT + k + AHEAD), D if k + AHEAD < KC else SLOT)
                add_to_x(c0 + (C_MIX_OUT + KC), 1.0)

            with dve.Fori(0, DEPTH) as l:
                c0 = N(C_LAYERS).plus(l, LAYER_CHUNKS)
                rms(N(0, (l, 3)))
                transposed(N(4, (l, 4)), gain_of("ffn1_norm_2", l))
                ffn(c0 + C_FFN1, N(0, (l, 2 * FF_GROUPS)), False)
                rms(N(1, (l, 3)))
                rest(c0 + (C_FFN1 + FF_CHUNKS - 1 + AHEAD))
                transposed(N(5, (l, 4)), gain_of("mix_norm_2", l))
                mixer(l, c0)
                rms(N(2, (l, 3)))
                rest(c0 + (C_MIX_OUT + KC - 1 + AHEAD))
                transposed(N(7, (l, 4)), gain_of("ffn2_norm_2", l))
                ffn(c0 + C_FFN2, N(FF_GROUPS, (l, 2 * FF_GROUPS)), True)
                with dve.If(l < DEPTH - 1):
                    for k in range(AHEAD):
                        rest(c0 + (LAYER_CHUNKS + k))

        @block.tensor
        def _(pe):
            t = nc.tensor

            def transposes(call, src, waits, first=None):
                def turn(q, b):
                    for kk in range(2):
                        k = 2 * q + kk
                        last = t.transpose(W[:, q, kk * SEQ + b * P:kk * SEQ + (b + 1) * P], src[:, b, k * P:(k + 1) * P], ident[:])
                    return last

                if first is not None:
                    pe.wait_ge(*first)
                    for q in range(4):
                        turn(q, 0)
                for sm, n in waits:
                    pe.wait_ge(sm, n)
                for q in range(4):
                    if first is None:
                        turn(q, 0)
                    turn(q, 1).then_inc(xt_ps, 1)

            def wait_xT(call, kc=KC - 1):
                if kc % 2 == 0 or kc == KC - 1:
                    pe.wait_ge(xt_lo_s, (call.times(4) + max(kc // 2 + 1, 2)).v)

            def exact(out, a_hi, a_lo, b_hi, b_lo, first, last):
                t.matmul(out, a_hi, b_hi, start=first, stop=False)
                t.matmul(out, a_hi, b_lo, start=False, stop=False)
                return t.matmul(out, a_lo, b_hi, start=False, stop=last)

            def projection(c0, groups, n, before, call):
                for j in range(groups):
                    for half in range(2):
                        c = c0 + (2 * j + half)
                        pe.wait_ge(lo_ready, (c + 1).v)
                        if half == 0 and j >= 2:
                            pe.wait_ge(tm_act, (before + (j - 1)).v)
                            pe.wait_ge(tm_dve, (before + (j - 1)).v)
                        hi, lo = w_hi[split_slot(c)], w_lo[split_slot(c)]
                        for k in range(4):
                            kc = 4 * half + k
                            if j == 0:
                                wait_xT(call, kc)
                            for b in range(TB):
                                tok = slice(b * P, (b + 1) * P)
                                last = exact(W[:, (2 * j + b) % 4, 0:n], xT_hi[:, kc, tok], xT_lo[:, kc, tok],
                                             hi[:, k * n:(k + 1) * n], lo[:, k * n:(k + 1) * n], kc == 0, kc == KC - 1)
                        last.then_inc(used, 1)

            def into_acc(c, kn, a_hi, a_lo, first, final):
                pe.wait_ge(lo_ready, (c + 1).v)
                hi, lo = w_hi[split_slot(c)], w_lo[split_slot(c)]
                for k in range(kn):
                    for b in range(TB):
                        tok = slice(b * P, (b + 1) * P)
                        st, sp_ = first and k == 0, final and k == kn - 1
                        for n in range(2):
                            cols = slice(k * D + 512 * n, k * D + 512 * (n + 1))
                            t.matmul(acc[:, 2 * b + n, :], a_hi(k)[:, tok], hi[:, cols], start=st, stop=False)
                            t.matmul(acc[:, 2 * b + n, :], a_hi(k)[:, tok], lo[:, cols], start=False, stop=False)
                        for n in range(2):
                            cols = slice(k * D + 512 * n, k * D + 512 * (n + 1))
                            last = t.matmul(acc[:, 2 * b + n, :], a_lo(k)[:, tok], hi[:, cols], start=False, stop=sp_)
                last.then_inc(used, 1)

            def out_projection(c0, halves=()):
                for kc in range(KC):
                    if kc % 4 == 0:
                        for sm in halves:
                            pe.wait_ge(sm, kc // 4 + 1)
                    into_acc(c0 + kc, 1, lambda k: xT_hi[:, kc, :], lambda k: xT_lo[:, kc, :], kc == 0, kc == KC - 1)

            pe.wait_ge(consts, 1)
            transposes(N(0), x, ((x_ready, 1),))
            projection(N(C_EVEN_IN), EVEN_IN // 512, 512, N(0), N(0))

            pe.wait_ge(small_in, SMALL_LOADS * 16)
            for i, names in enumerate(VEC_SETS):
                n = sum(r for _, r in names)
                last = t.transpose(acc[:, 1 + i, 0:n], vrows[i][0:n, :], ident[0:n, 0:n])
            last.then_inc(vec_ps, 1)

            pe.wait_ge(tm_act, EVEN_IN // 512)
            pe.wait_ge(tm_dve, EVEN_IN // 512)
            for i in range(6):
                if i == 0:
                    pe.wait_ge(ev["a"], 1)
                if i == 2:
                    pe.wait_ge(ev["bx"], 1)
                if i >= 4:
                    pe.wait_ge(ev["tr"], i - 3)
                for kk in range(2):
                    c = 2 * i + kk
                    col = (0, 1536, 1024)[c // 4] + (c % 4) * P
                    for b in range(TB):
                        last = t.transpose(W[:, i % 4, kk * SEQ + b * P:kk * SEQ + (b + 1) * P], u_even[:, b, col:col + P], ident[:])
                last.then_inc(ev["tp"], 1)
            for k in range(CONV_A):
                pe.wait_ge(ev["product"], k + 1)
                t.matmul(acc[:, 0, :], ident[:], taps[:, k % 4, :, :].rearrange("p c t -> p (c t)"), start=(k == 0),
                         stop=(k == CONV_A - 1)).then_inc(ev["summed"], 1)
            pe.wait_ge(ev["conv"], 2)
            pe.wait_ge(ev["tr"], 6)
            for b in range(TB):
                for c in range(4):
                    last = t.transpose(W[:, b, c * P:(c + 1) * P], ca[:, c, b * P:(b + 1) * P], ident[:])
            last.then_inc(ev["back"], 1)
            def output(kc):
                i = EVEN_ORDER.index(kc)
                into_acc(N(C_EVEN_OUT + i), 1, lambda k: xT_hi[:, kc, :], lambda k: xT_lo[:, kc, :], i == 0, i == KC - 1)

            pe.wait_ge(ev["done"], 1)
            output(4)
            output(5)
            pe.wait_ge(ev["an"], 1)
            for i in range(2):
                for kk in range(2):
                    c = 2 * i + kk
                    for b in range(TB):
                        last = t.transpose(W[:, 2 + i, kk * SEQ + b * P:kk * SEQ + (b + 1) * P], an[:, b, c * P:(c + 1) * P], ident[:])
                last.then_inc(ev["an_ps"], 1)
            output(6)
            output(7)
            pe.wait_ge(ev["done"], 2)
            for kc in range(4):
                output(kc)

            def gather(done):
                for kc in range(KC):
                    for b in range(TB):
                        last = t.matmul(W[:, 3, kc * CAP:(kc + 1) * CAP], x[:, b, kc * P:(kc + 1) * P],
                                        pick[:, b, 0:CAP], start=(b == 0), stop=(b == TB - 1))
                last.then_inc(done, 1)

            def scatter(done, ready):
                for n in range(2):
                    pe.wait_ge(*ready[n])
                    for b in range(TB):
                        for Y in (Y_hi, Y_lo):
                            last = t.matmul(acc[:, 2 * b + n, :], pickT[:, b * P:(b + 1) * P], Y[:, 512 * n:512 * (n + 1)],
                                            start=False, stop=False, skip_group_check=True)
                last.then_inc(done, 1)

            def experts(layer, c0):
                i = layer
                transposes(N(1 + 2 * layer), x, ((x_ready, 2 + 2 * layer),), (ln_x0, 2 * layer + 1))
                pe.wait_ge(wr_ok, 1)
                for k in range(KC):
                    wait_xT(N(1 + 2 * layer), k)
                    last = exact(W[0:NE, 1, 0:SEQ], wr_hi[:, k, :], wr_lo[:, k, :], xT_hi[:, k, :], xT_lo[:, k, :],
                                 k == 0, k == KC - 1)
                last.then_inc(rt["logitsT"], 1)
                pe.wait_ge(rt["logits_sb"], i + 1)
                for b in range(TB):
                    last = t.matmul(W[:, 0, b * NE:(b + 1) * NE], logitsT[:, b * P:(b + 1) * P], ident[0:NE, 0:NE],
                                    start=True, stop=True)
                last.then_inc(rt["logits"], 1)
                for n in range(4):
                    t.matmul(acc[:, n, :], zeros[:], xT_hi[:, 0:2, :].rearrange("p a t -> p (a t)"), start=True, stop=False, skip_group_check=True)
                pe.wait_ge(rt["chosen"], i + 1)
                ones = tri[:, P:2 * P]
                t.matmul(W[:, 1, 0:NE], tri_strict[:], top2[:, 0, :], start=True, stop=True)
                t.matmul(W[:, 1, NE:2 * NE], ones, top2[:, 0, :], start=True, stop=False)
                t.matmul(W[:, 1, NE:2 * NE], tri_strict[:], top2[:, 1, :], start=False, stop=True)
                t.matmul(W[:, 1, 2 * NE:3 * NE], ones, top2[:, 0, :], start=True, stop=False)
                t.matmul(W[:, 1, 2 * NE:3 * NE], ones, top2[:, 1, :], start=False, stop=True).then_inc(rt["ranks"], 1)

                pe.wait_ge(me["pick"], NE * layer + 1)
                gather(me["ga"])
                def chunk(c, bank, first):
                    pe.wait_ge(lo_ready, (c + 1).v)
                    for k in range(4):
                        kc = k + (0 if first else 4)
                        cols = slice(512 * k, 512 * (k + 1))
                        t.matmul(W[:, bank, :], xe[:, kc, :], w_hi[split_slot(c)][:, cols], start=(kc == 0), stop=False)
                        last = t.matmul(W[:, bank, :], xe[:, kc, :], w_lo[split_slot(c)][:, cols], start=False, stop=(kc == KC - 1))
                    last.then_inc(used, 1)

                def expert(e, c, last):
                    one = N(NE * layer).plus(e, 1)
                    two = one.times(2)

                    def turn_hidden(n):
                        pe.wait_ge(me["h"], (two + (n + 1)).v)
                        for k in range(4):
                            turn = t.matmul if k == 0 else t.transpose
                            last = turn(W[:, TURN_BANK[n], k * CAP:(k + 1) * CAP], ub[:, n, k * P:(k + 1) * P],
                                        ident[0:CAP, 0:CAP], **({"start": True, "stop": True} if k == 0 else {}))
                        last.then_inc(me["tr"], 1)

                    def down(c, i):
                        pe.wait_ge(lo_ready, (c + 1).v)
                        for k in range(2):
                            kc = 2 * i + k
                            for w in (w_hi, w_lo):
                                for n in range(2):
                                    cols = slice(k * D + 512 * n, k * D + 512 * (n + 1))
                                    last = t.matmul(W[:, 1 + n, :], heT[:, kc, :], w[split_slot(c)][:, cols],
                                                    start=(kc == 0 and w is w_hi),
                                                    stop=(kc == KC - 1 and w is w_lo))
                        last.then_inc(used, 1)

                    for b in range(TB):
                        t.transpose(W[:, 1, b * P:(b + 1) * P], pick[:, b, :], ident[:])
                    gates = gate[:, :, bass.ds(e, 1)]
                    for b in range(TB):
                        turned = t.matmul(W[:, 1, SEQ:SEQ + 1], pick[:, b, :], gates[:, b], start=(b == 0), stop=(b == TB - 1))
                    turned.then_inc(me["pt"], 1)
                    chunk(c, 2, True)
                    chunk(c + 1, 2, False)
                    pe.wait_ge(me["g"], (two + 1).v)
                    chunk(c + 2, 0, True)
                    pe.wait_ge(me["pte"], (one + 1).v)
                    turn_hidden(0)
                    chunk(c + 3, 0, False)
                    if not last:
                        pe.wait_ge(me["pick"], (one + 2).v)
                        gather(me["ga"])
                    pe.wait_ge(me["hT"], (two + 1).v)
                    pe.wait_ge(me["g"], (two + 2).v)
                    down(c + 4, 0)
                    down(c + 5, 1)
                    if not last:
                        pe.wait_ge(me["xe"], (one + 2).v)
                    turn_hidden(1)
                    if not last:
                        chunk(c + 6, 0, True)
                        chunk(c + 7, 0, False)
                    pe.wait_ge(me["hT"], (two + 2).v)
                    d = c + (6 if last else 8)
                    down(d, 2)
                    down(d + 1, 3)
                    if not last:
                        chunk(c + 10, 3, True)
                        chunk(c + 11, 3, False)
                    scatter(me["sc"], [(me["y"], (two + (n + 1)).v) for n in range(2)])

                pe.wait_ge(me["xe"], NE * layer + 1)
                chunk(N(c0), 0, True)
                chunk(N(c0 + 1), 0, False)
                chunk(N(c0 + 2), 3, True)
                chunk(N(c0 + 3), 3, False)
                with pe.Fori(0, NE - 1) as e:
                    expert(e, N(c0 + 4).plus(e, MOE_CHUNKS), False)
                expert(NE - 1, N(c0 + 4 + MOE_CHUNKS * (NE - 1)), True)
                with crowded(pe, layer):
                    more_rounds(layer)

            def more_rounds(layer):
                o = ov[layer]
                pe.sem_inc(o["free"], 1)
                with pe.Fori(0, ROUNDS - 1) as r:
                    with pe.Fori(0, NE) as e:
                        k = N(0, (r, NE), (e, 1))
                        pe.wait_ge(*ov_done(o, "pick", k))
                        gather(o["tensor"])
                        for b in range(TB):
                            t.transpose(W[:, 0, b * P:(b + 1) * P], pick[:, b, :], ident[:])
                        for b in range(TB):
                            last = t.matmul(W[:, 0, SEQ:SEQ + 1], pick[:, b, :], gate[:, b, bass.ds(e, 1)],
                                            start=(b == 0), stop=(b == TB - 1))
                        last.then_inc(o["tensor"], 1)
                        pe.wait_ge(*ov_done(o, "tokens_lo", k))
                        pe.wait_ge(*ov_done(o, "choice", k))
                        for i in range(2 * KC):
                            pe.wait_ge(o["lo"], (k.times(24) + (i + 1)).v)
                            kc = i % KC
                            for n in range(2):
                                cols = slice(512 * n, 512 * (n + 1))
                                out = W[:, 2 * (i // KC) + n, :]
                                t.matmul(out, xe[:, kc, :], ov_hi[:, cols], start=(kc == 0), stop=False)
                                last = t.matmul(out, xe[:, kc, :], ov_lo[:, cols], start=False, stop=(kc == KC - 1))
                            last.then_inc(o["free"], 1)
                        pe.wait_ge(*ov_done(o, "hidden", k))
                        for kc in range(KC):
                            turn = t.matmul if kc == 0 else t.transpose
                            last = turn(W[:, 0, kc * CAP:(kc + 1) * CAP], ub[:, kc // 4, (kc % 4) * P:(kc % 4 + 1) * P],
                                        ident[0:CAP, 0:CAP], **({"start": True, "stop": True} if kc == 0 else {}))
                        last.then_inc(o["tensor"], 1)
                        pe.wait_ge(*ov_done(o, "hidden_lo", k))
                        for kc in range(KC):
                            pe.wait_ge(o["lo"], (k.times(24) + (2 * KC + kc + 1)).v)
                            for n in range(2):
                                cols = slice(512 * n, 512 * (n + 1))
                                t.matmul(W[:, 1 + n, :], heT[:, kc, :], ov_hi[:, cols], start=(kc == 0), stop=False)
                                last = t.matmul(W[:, 1 + n, :], heT[:, kc, :], ov_lo[:, cols], start=False, stop=(kc == KC - 1))
                            last.then_inc(o["free"], 1)
                        scatter(o["tensor"], [ov_done(o, "out_lo", k)] * 2)

            experts(0, C_MOE0)

            transposes(N(2), x, ((x_ready, 3),), (ln_x0, 2))
            projection(N(C_ODD_IN), 2 * D // 512, 512, N(5), N(2))
            pe.wait_ge(tm_act, 9)
            pe.wait_ge(tm_dve, 9)
            for i in range(8):
                if i >= 4:
                    pe.wait_ge(od["tr"], i - 3)
                for kk in range(2):
                    c = (2 * i + kk) % KC
                    col = (D if i < 4 else 0) + c * P
                    for b in range(TB):
                        last = t.transpose(W[:, i % 4, kk * SEQ + b * P:kk * SEQ + (b + 1) * P], u_odd[:, b, col:col + P], ident[:])
                last.then_inc(od["tp"], 1)
            ga, gx = N(C_GATES), N(C_GATES + 1)
            pe.wait_ge(lo_ready, C_GATES + 2)
            pe.wait_ge(od["tr"], 8)
            for h in range(RNN_HEADS):
                if h % 2 == 0:
                    pe.wait_ge(od["lo"], h // 2 + 1)
                for jc in range(2):
                    i = 2 * h + jc
                    if i >= 4:
                        pe.wait_ge(od["ri"], i - 3)
                    for part, c in enumerate((ga, gx)):
                        for ic in range(2):
                            cols = slice((2 * h + ic) * 256 + jc * P, (2 * h + ic) * 256 + (jc + 1) * P)
                            last = exact(W[:, i % 4, part * SEQ:(part + 1) * SEQ], w_hi[split_slot(c)][:, cols], w_lo[split_slot(c)][:, cols],
                                         xT_hi[:, 2 * h + ic, :], xT_lo[:, 2 * h + ic, :], ic == 0, ic == 1)
                    last.then_inc(od["gates"], 1)
            pe.drain().then_inc(used, 2)
            out_projection(N(C_ODD_OUT), [od["done"]])

            experts(1, C_MOE1)

            def ffn(c0, h0, call):
                def up(c, bank, first=False):
                    pe.wait_ge(lo_ready, (c + 1).v)
                    hi, lo = w_hi[split_slot(c)], w_lo[split_slot(c)]
                    for f in range(2):
                        for kc in range(KC):
                            if first and f == 0:
                                wait_xT(call, kc)
                            cols = slice(kc * FF_COLS + f * P, kc * FF_COLS + (f + 1) * P)
                            last = exact_w(W[:, bank, f * SEQ:(f + 1) * SEQ], hi[:, cols], lo[:, cols], kc)
                    last.then_inc(used, 1)

                def exact_w(out, hi, lo, kc):
                    t.matmul(out, hi, xT_hi[:, kc, :], start=(kc == 0), stop=False)
                    t.matmul(out, hi, xT_lo[:, kc, :], start=False, stop=False)
                    return t.matmul(out, lo, xT_hi[:, kc, :], start=False, stop=(kc == KC - 1))

                def down(c, parity, n, first, final):
                    pe.wait_ge(ff["hT"], n.v)
                    into_acc(c, 2, lambda k: hT_hi[:, parity, k, :], lambda k: hT_lo[:, parity, k, :], first, final)

                up(c0, 0, True)
                up(c0 + 1, 1)
                def group(c, j_par, n, first):
                    pe.wait_ge(ff["h"], n.v)
                    up(c, 2 * (1 - j_par))
                    up(c + 1, 2 * (1 - j_par) + 1)
                    down(c + 2, j_par, n, first, False)
                group(c0 + 2, 0, h0 + 1, True)
                group(c0 + 5, 1, h0 + 2, False)
                with pe.Fori(0, (FF_GROUPS - 3) // 2) as i:
                    for p in range(2):
                        group((c0 + (8 + 3 * p)).plus(i, 6), p, (h0 + (3 + p)).plus(i, 2), False)
                down(c0 + (FF_CHUNKS - 1), 0, h0 + FF_GROUPS, False, True)

            def mixer(l, c0):
                lay = N(0, (l, 1))
                projection(c0 + C_MIX_IN, IN_GROUPS, IN_COLS, N(9, (l, IN_GROUPS)), N(5, (l, 4)))
                pe.wait_ge(mx["dup"], (lay + 1).v)
                for i in range(10):
                    if i == 6:
                        pe.wait_ge(mx["qkd"], (lay + 1).times(2).v)
                    if i >= 4:
                        pe.wait_ge(mx["qkta" if i % 2 == 0 else "qktd"], (lay.times(5) + ((i - 4) // 2 + 1)).v)
                    for kk in range(2):
                        ch = 2 * i + kk
                        for b in range(TB):
                            last = t.transpose(W[:, i % 4, kk * SEQ + b * P:kk * SEQ + (b + 1) * P], QK[:, b, ch * P:(ch + 1) * P], ident[:])
                    last.then_inc(mx["qkt"], 1)
                pe.wait_ge(mx["qkta"], (lay + 1).times(5).v)
                pe.wait_ge(mx["qktd"], (lay + 1).times(5).v)

                def rows(ch, r, tok):
                    return QKT[r * HD:(r + 1) * HD, ch, tok]

                for b in range(TB):
                    n = P * (b + 1)
                    for h in range(8):
                        i = 4 * (h % 2) + h // 2
                        k, o = (i * n) // 512, (i * n) % 512
                        last = t.matmul((acc, W)[b][:, k, o:o + n], rows(3 + h // 2, h % 2, slice(b * P, (b + 1) * P)),
                                        rows(7, h % 2, slice(0, n)), start=True, stop=True)
                    last.then_inc(mx["is"], 1)
                pe.wait_ge(mx["relu"], (lay + 1).times(2).v)
                pe.wait_ge(mx["nlf"], (lay + 1).v)

                def keep_warm(n, u):
                    for _ in range(n):
                        t.matmul(acc[:, 2 + u % 2, 0:SEQ], zeros[:], xT_hi[:, 0, :], start=True, stop=True, skip_group_check=True)

                def scores(u):
                    b, grp = UNITS[u]
                    if u >= 2:
                        pe.wait_ge(mx["sb"], (lay.times(8) + (u - 1)).v)
                    for h in range(4):
                        n = P * (b + 1)
                        k, o = 2 * (u % 2) + h % 2, (h // 2) * n
                        hh = 4 * (grp - 2) + h
                        q, kk = ((h // 2, 2), (8 + h // 2, 10 + h // 2), (12 + hh // 2, 16 + hh // 2), (12 + hh // 2, 16 + hh // 2))[grp]
                        last = t.matmul(W[:, k, o:o + n], rows(q, h % 2, slice(b * P, (b + 1) * P)), rows(kk, h % 2, slice(0, n)),
                                        start=True, stop=(grp < 2))
                        if grp >= 2:
                            for sb in range(b + 1):
                                w = n - P * sb
                                last = t.matmul(W[:, k, o + P * sb:o + n], nlf[:, sb, hh:hh + 1].to_broadcast([P, P]), tri[:, 0:w],
                                                start=False, stop=(sb == b))
                    last.then_inc(mx["s"], 1)

                scores(0)
                for u in range(8):
                    b, grp = UNITS[u]
                    if u < 7:
                        scores(u + 1)
                    if u >= 2:
                        pe.wait_ge(mx["at"], (lay.times(8) + (u - 1)).v)
                    keep_warm(8, u)
                    pe.wait_ge(mx["p"], (lay.times(8) + (u + 1)).v)
                    n = P * (b + 1)
                    for h in range(4):
                        for kb in range(b + 1):
                            o = h * n + kb * P
                            last = t.transpose(acc[:, o // 512, o % 512:o % 512 + P], Sb[:, u % 2, h, kb * P:(kb + 1) * P], ident[:])
                    last.then_inc(mx["t"], 1)
                    keep_warm(4, u)
                    pe.wait_ge(mx["te"], (lay.times(8) + (u + 1)).v)
                    for i in range(4):
                        h = 2 * (i % 2) + i // 2
                        hh = 4 * (grp - 2) + h
                        col = (AV, BV + HD * h, CV + HD * hh, CV + HD * hh)[grp]
                        for kb in range(b + 1):
                            last = t.matmul(acc[:, 2 + u % 2, i * HD:(i + 1) * HD], PT[:, i, kb * P:(kb + 1) * P], proj[:, kb, col:col + HD],
                                            start=(kb == 0), stop=(kb == b))
                    last.then_inc(mx["o"], 1)
                transposes(N(6, (l, 4)), attn, ((mx["at"], (lay + 1).times(8).v), (mx["cg"], (lay + 1).v)))
                wait_xT(N(6, (l, 4)))
                out_projection(c0 + C_MIX_OUT)

            with pe.Fori(0, DEPTH) as l:
                c0 = N(C_LAYERS).plus(l, LAYER_CHUNKS)

                def norm(call):
                    transposes(N(4 + call, (l, 4)), xn, ((rm["xd"], N(min(call, 2) + 1, (l, 3)).v),), (rm["xa"], N(min(call, 2) + 1, (l, 3)).v))

                norm(0)
                ffn(c0 + C_FFN1, N(0, (l, 2 * FF_GROUPS)), N(4, (l, 4)))
                norm(1)
                mixer(l, c0)
                norm(3)
                ffn(c0 + C_FFN2, N(FF_GROUPS, (l, 2 * FF_GROUPS)), N(7, (l, 4)))


SMALL_LOADS = 4 + sum(len(names) for names in VEC_SETS)

_OUT = (1, SEQ, D)


def kernel(**inputs):
    import numpy as np
    import concourse.bacc as bacc
    from concourse.bass_utils import run_bass_kernel_spmd

    nc = bacc.Bacc("TRN2", target_bir_lowering=False, num_devices=1)
    cos, sin = rope_tables()
    arrays, A = {}, {}
    for name, a in {**inputs, "rope_cos": cos, "rope_sin": sin}.items():
        a = np.ascontiguousarray(a)
        arrays[f"in_{name}"] = a
        A[name] = nc.dram_tensor(f"in_{name}", a.shape, mybir.dt.from_np(a.dtype), kind="ExternalInput").ap()
    out = nc.dram_tensor("out", _OUT, F32, kind="ExternalOutput").ap()
    build_program(nc, A, out)
    r = run_bass_kernel_spmd(nc, [arrays], core_ids=[0])
    return r.results[0]["out"]
```
